# Optimizing a Trainium2 kernel written in Bass

```python
import math
import jax, jax.numpy as jnp
from jax import lax
import numpy as np

D_MODEL = 1024
BATCH = 1
SEQ = 256
DEPTH = 2
DEC_BATCH = 8
DEC_SEQ = 4
PAST_LEN = 2048
PAGE_SIZE = 128

N_MIXERS = 2
N_A_LAYERS = (DEPTH + 1) // 2
N_B_LAYERS = DEPTH // 2
S5_GROUP = 16
S5_GROUPS = D_MODEL // S5_GROUP
S5_STATE = 64
S5_DT_MIN = 1e-3
S5_DT_MAX = 1e-1
HG_EXPAND = 128
HG_HEADS = D_MODEL // HG_EXPAND
HG_DK = HG_EXPAND
HG_FDIM = HG_HEADS * HG_DK
HG_DV = D_MODEL // HG_HEADS
HG_CHUNK = 64
PEER_HEADS = 8
PEER_NKEYS = 128
PEER_EXPERTS = PEER_NKEYS * PEER_NKEYS
PEER_TOPK = 16
PEER_DKEY = 256
PEER_HALF = PEER_DKEY // 2
PEER_BLOCK = 256
RMS_EPS = 1e-6

kernel_name = "hybrid_s5_hgrn2_peer_step"

F32 = jnp.float32

def _rmsnorm(x, w):
    xf = x.astype(F32)
    y = xf * lax.rsqrt(jnp.mean(xf * xf, axis=-1, keepdims=True) + RMS_EPS)
    return (y * w.astype(F32)).astype(x.dtype)

def _complex_affine_combine(e1, e2):
    a1r, a1i, b1r, b1i = e1
    a2r, a2i, b2r, b2i = e2
    return (a1r * a2r - a1i * a2i,
            a1r * a2i + a1i * a2r,
            a2r * b1r - a2i * b1i + b2r,
            a2r * b1i + a2i * b1r + b2i)

def _s5_mixer(h, s0_re, s0_im, lam_re, lam_im, log_dt, b_re, b_im, c_re, c_im, d, w_glu):
    nb, L, _ = h.shape
    u = h.astype(F32).reshape(nb, L, S5_GROUPS, S5_GROUP)
    lr = jnp.minimum(lam_re.astype(F32), -1e-4)
    li = lam_im.astype(F32)
    dt = jnp.exp(log_dt.astype(F32))[:, None]
    mag = jnp.exp(lr * dt)
    ang = li * dt
    ab_re = mag * jnp.cos(ang)
    ab_im = mag * jnp.sin(ang)
    den = lr * lr + li * li
    nr = ab_re - 1.0
    zr = (nr * lr + ab_im * li) / den
    zi = (ab_im * lr - nr * li) / den
    br = b_re.astype(F32)
    bi = b_im.astype(F32)
    bb_re = zr[..., None] * br - zi[..., None] * bi
    bb_im = zr[..., None] * bi + zi[..., None] * br
    bu_re = jnp.einsum('blgh,gph->lbgp', u, bb_re)
    bu_im = jnp.einsum('blgh,gph->lbgp', u, bb_im)
    a_re = jnp.broadcast_to(ab_re[None, None], (L, 1, S5_GROUPS, S5_STATE))
    a_im = jnp.broadcast_to(ab_im[None, None], (L, 1, S5_GROUPS, S5_STATE))
    acr, aci, sr, si = lax.associative_scan(_complex_affine_combine, (a_re, a_im, bu_re, bu_im), axis=0)
    s0r = s0_re.astype(F32)[None]
    s0i = s0_im.astype(F32)[None]
    st_re = sr + acr * s0r - aci * s0i
    st_im = si + acr * s0i + aci * s0r
    y = (jnp.einsum('lbgp,ghp->blgh', st_re, c_re.astype(F32))
         - jnp.einsum('lbgp,ghp->blgh', st_im, c_im.astype(F32))
         + d.astype(F32).reshape(S5_GROUPS, S5_GROUP) * u)
    y = jax.nn.gelu(y.reshape(nb, L, D_MODEL), approximate=False).astype(h.dtype)
    z = y @ w_glu
    out = z[..., :D_MODEL] * jax.nn.sigmoid(z[..., D_MODEL:])
    return out, st_re[-1].astype(s0_re.dtype), st_im[-1].astype(s0_im.dtype)

def _gla_chunked(q, k, v, logf, S0):
    nb, L, H, DK = q.shape
    C = math.gcd(L, HG_CHUNK)
    NC = L // C

    def to_chunks(t):
        return t.reshape(nb, NC, C, H, t.shape[-1]).transpose(1, 0, 3, 2, 4)

    qc, kc, vc, lc = to_chunks(q), to_chunks(k), to_chunks(v), to_chunks(logf)
    b = jnp.cumsum(lc, axis=3)
    b_last = b[:, :, :, C - 1:C, :]
    b_mid = b[:, :, :, C // 2:C // 2 + 1, :]
    scores = jnp.einsum('nbhtk,nbhsk->nbhts', qc * jnp.exp(b - b_mid), kc * jnp.exp(b_mid - b))
    causal = jnp.tril(jnp.ones((C, C), dtype=bool))
    scores = jnp.where(causal, scores, 0.0)
    o_intra = jnp.einsum('nbhts,nbhsv->nbhtv', scores, vc)
    q_inter = qc * jnp.exp(b)
    kv = jnp.einsum('nbhsk,nbhsv->nbhkv', kc * jnp.exp(b_last - b), vc)
    decay = jnp.exp(b_last[:, :, :, 0, :])

    def step(S, xs):
        qi, dec, kvi = xs
        o = jnp.einsum('bhtk,bhkv->bhtv', qi, S)
        return dec[..., None] * S + kvi, o

    S_last, o_inter = lax.scan(step, S0, (q_inter, decay, kv))
    o = (o_intra + o_inter).transpose(1, 0, 3, 2, 4).reshape(nb, L, H, v.shape[-1])
    return o, S_last

def _hgrn2_mixer(h, S0, w_in, lb, norm_w, w_out):
    nb, L, _ = h.shape
    proj = h @ w_in
    q, fz, iv, g = jnp.split(proj, [HG_FDIM, 2 * HG_FDIM, 2 * HG_FDIM + D_MODEL], axis=-1)
    q = jax.nn.silu(q.astype(F32)).reshape(nb, L, HG_HEADS, HG_DK)
    fz = fz.astype(F32).reshape(nb, L, HG_HEADS, HG_DK)
    lbh = lb.astype(F32).reshape(HG_HEADS, HG_DK)
    logf = jnp.logaddexp(jnp.log(lbh), jnp.log1p(-lbh) + jax.nn.log_sigmoid(fz))
    k = (1.0 - lbh) * jax.nn.sigmoid(-fz)
    v = iv.astype(F32).reshape(nb, L, HG_HEADS, HG_DV)
    o, S_last = _gla_chunked(q, k, v, logf, S0.astype(F32))
    o = o * lax.rsqrt(jnp.mean(o * o, axis=-1, keepdims=True) + RMS_EPS)
    o = o * norm_w.astype(F32) * jax.nn.silu(g.astype(F32).reshape(nb, L, HG_HEADS, HG_DV))
    out = o.reshape(nb, L, D_MODEL).astype(h.dtype) @ w_out
    return out, S_last.astype(S0.dtype)

def _peer_ffn(h, w_q, keys1, keys2, u_tab, v_tab):
    nb, L, D = h.shape
    T = nb * L
    x = h.reshape(T, D)
    q = (x @ w_q).astype(F32).reshape(T, PEER_HEADS, PEER_DKEY)
    s1 = jnp.einsum('thd,nd->thn', q[..., :PEER_HALF], keys1.astype(F32))
    s2 = jnp.einsum('thd,nd->thn', q[..., PEER_HALF:], keys2.astype(F32))
    v1, i1 = lax.top_k(s1, PEER_TOPK)
    v2, i2 = lax.top_k(s2, PEER_TOPK)
    cand = (v1[..., :, None] + v2[..., None, :]).reshape(T, PEER_HEADS, PEER_TOPK * PEER_TOPK)
    cidx = (i1[..., :, None] * PEER_NKEYS + i2[..., None, :]).reshape(T, PEER_HEADS, PEER_TOPK * PEER_TOPK)
    sc, pos = lax.top_k(cand, PEER_TOPK)
    idx = jnp.take_along_axis(cidx, pos, axis=-1).reshape(T, PEER_HEADS * PEER_TOPK)
    gate = jax.nn.softmax(sc, axis=-1).reshape(T, PEER_HEADS * PEER_TOPK).astype(x.dtype)
    blk = min(PEER_BLOCK, T)
    nblk = -(-T // blk)
    pad = nblk * blk - T
    xb = jnp.pad(x, ((0, pad), (0, 0))).reshape(nblk, blk, D)
    ib = jnp.pad(idx, ((0, pad), (0, 0))).reshape(nblk, blk, PEER_HEADS * PEER_TOPK)
    gb = jnp.pad(gate, ((0, pad), (0, 0))).reshape(nblk, blk, PEER_HEADS * PEER_TOPK)

    def block(args):
        xi, ii, gi = args
        act = jax.nn.gelu(jnp.einsum('tkd,td->tk', u_tab[ii], xi), approximate=False) * gi
        return jnp.einsum('tk,tkd->td', act, v_tab[ii])

    out = lax.map(block, (xb, ib, gb)).reshape(nblk * blk, D)[:T]
    return out.reshape(nb, L, D)

def _trunk(x, s5_re, s5_im, s_hg, norm_mix, norm_ffn, norm_final, s5_lambda_re, s5_lambda_im,
           s5_log_dt, s5_b_re, s5_b_im, s5_c_re, s5_c_im, s5_d, s5_w_glu, hg_w_in, hg_lower_bounds,
           hg_norm_w, hg_w_out, peer_w_q, peer_keys1, peer_keys2, peer_u, peer_v):
    lb_all = jnp.cumsum(jax.nn.softmax(hg_lower_bounds.astype(F32), axis=0), axis=0)
    lb_all = lb_all - lb_all[0:1]
    new_re, new_im, new_hg = [], [], []
    for i in range(DEPTH):
        h = _rmsnorm(x, norm_mix[i])
        j = i // N_MIXERS
        if i % N_MIXERS == 0:
            y, sr, si = _s5_mixer(h, s5_re[j], s5_im[j], s5_lambda_re[j], s5_lambda_im[j], s5_log_dt[j],
                                  s5_b_re[j], s5_b_im[j], s5_c_re[j], s5_c_im[j], s5_d[j], s5_w_glu[j])
            new_re.append(sr)
            new_im.append(si)
        else:
            y, S = _hgrn2_mixer(h, s_hg[j], hg_w_in[j], lb_all[i], hg_norm_w[j], hg_w_out[j])
            new_hg.append(S)
        x = x + y
        x = x + _peer_ffn(_rmsnorm(x, norm_ffn[i]), peer_w_q[i], peer_keys1[i], peer_keys2[i],
                          peer_u[i], peer_v[i])
    return _rmsnorm(x, norm_final), jnp.stack(new_re), jnp.stack(new_im), jnp.stack(new_hg)

def setup_inputs(seed: int = 0) -> dict:
    key = jax.random.key(seed)
    ks = jax.random.split(key, 26)

    def nrm(k, shape, s):
        return jax.random.normal(k, shape, F32) * s

    n_idx = jnp.arange(S5_STATE, dtype=F32)
    g_shape = (N_A_LAYERS, S5_GROUPS, S5_STATE)
    return {
        "x_prompt": nrm(ks[0], (BATCH, SEQ, D_MODEL), 1.0),
        "x_sample": nrm(ks[1], (DEC_BATCH, DEC_SEQ, D_MODEL), 1.0),
        "state_s5_re": nrm(ks[2], (N_A_LAYERS, DEC_BATCH, S5_GROUPS, S5_STATE), 0.1),
        "state_s5_im": nrm(ks[3], (N_A_LAYERS, DEC_BATCH, S5_GROUPS, S5_STATE), 0.1),
        "state_hgrn": nrm(ks[4], (N_B_LAYERS, DEC_BATCH, HG_HEADS, HG_DK, HG_DV), 0.5),
        "norm_mix": 1.0 + nrm(ks[5], (DEPTH, D_MODEL), 0.01),
        "norm_ffn": 1.0 + nrm(ks[6], (DEPTH, D_MODEL), 0.01),
        "norm_final": 1.0 + nrm(ks[7], (D_MODEL,), 0.01),
        "s5_lambda_re": -0.5 + nrm(ks[8], g_shape, 0.01),
        "s5_lambda_im": math.pi * n_idx + nrm(ks[9], g_shape, 0.01),
        "s5_log_dt": jax.random.uniform(ks[10], (N_A_LAYERS, S5_GROUPS), F32,
                                        math.log(S5_DT_MIN), math.log(S5_DT_MAX)),
        "s5_b_re": nrm(ks[11], (N_A_LAYERS, S5_GROUPS, S5_STATE, S5_GROUP), (2 * S5_GROUP) ** -0.5),
        "s5_b_im": nrm(ks[12], (N_A_LAYERS, S5_GROUPS, S5_STATE, S5_GROUP), (2 * S5_GROUP) ** -0.5),
        "s5_c_re": nrm(ks[13], (N_A_LAYERS, S5_GROUPS, S5_GROUP, S5_STATE), S5_STATE ** -0.5),
        "s5_c_im": nrm(ks[14], (N_A_LAYERS, S5_GROUPS, S5_GROUP, S5_STATE), S5_STATE ** -0.5),
        "s5_d": nrm(ks[15], (N_A_LAYERS, D_MODEL), 1.0),
        "s5_w_glu": nrm(ks[16], (N_A_LAYERS, D_MODEL, 2 * D_MODEL), D_MODEL ** -0.5),
        "hg_w_in": nrm(ks[17], (N_B_LAYERS, D_MODEL, 2 * HG_FDIM + 2 * D_MODEL), D_MODEL ** -0.5),
        "hg_lower_bounds": nrm(ks[18], (DEPTH, HG_FDIM), 0.1),
        "hg_norm_w": 1.0 + nrm(ks[19], (N_B_LAYERS, HG_DV), 0.01),
        "hg_w_out": nrm(ks[20], (N_B_LAYERS, D_MODEL, D_MODEL), D_MODEL ** -0.5),
        "peer_w_q": nrm(ks[21], (DEPTH, D_MODEL, PEER_HEADS * PEER_DKEY), D_MODEL ** -0.5),
        "peer_keys1": nrm(ks[22], (DEPTH, PEER_NKEYS, PEER_HALF), PEER_HALF ** -0.5),
        "peer_keys2": nrm(ks[23], (DEPTH, PEER_NKEYS, PEER_HALF), PEER_HALF ** -0.5),
        "peer_u": nrm(ks[24], (DEPTH, PEER_EXPERTS, D_MODEL), D_MODEL ** -0.5),
        "peer_v": nrm(ks[25], (DEPTH, PEER_EXPERTS, D_MODEL), PEER_HEADS ** -0.5),
    }

def reference(x_prompt, x_sample, state_s5_re, state_s5_im, state_hgrn, norm_mix, norm_ffn, norm_final,
              s5_lambda_re, s5_lambda_im, s5_log_dt, s5_b_re, s5_b_im, s5_c_re, s5_c_im, s5_d, s5_w_glu,
              hg_w_in, hg_lower_bounds, hg_norm_w, hg_w_out, peer_w_q, peer_keys1, peer_keys2, peer_u, peer_v):
    nbp = x_prompt.shape[0]
    z_s5 = jnp.zeros((N_A_LAYERS, nbp, S5_GROUPS, S5_STATE), state_s5_re.dtype)
    z_hg = jnp.zeros((N_B_LAYERS, nbp, HG_HEADS, HG_DK, HG_DV), state_hgrn.dtype)
    y_prompt, s5_re_p, s5_im_p, hg_p = _trunk(
        x_prompt, z_s5, z_s5, z_hg, norm_mix, norm_ffn, norm_final, s5_lambda_re, s5_lambda_im,
        s5_log_dt, s5_b_re, s5_b_im, s5_c_re, s5_c_im, s5_d, s5_w_glu, hg_w_in, hg_lower_bounds,
        hg_norm_w, hg_w_out, peer_w_q, peer_keys1, peer_keys2, peer_u, peer_v)
    y_sample, s5_re_s, s5_im_s, hg_s = _trunk(
        x_sample, state_s5_re, state_s5_im, state_hgrn, norm_mix, norm_ffn, norm_final, s5_lambda_re,
        s5_lambda_im, s5_log_dt, s5_b_re, s5_b_im, s5_c_re, s5_c_im, s5_d, s5_w_glu, hg_w_in,
        hg_lower_bounds, hg_norm_w, hg_w_out, peer_w_q, peer_keys1, peer_keys2, peer_u, peer_v)
    return (y_prompt, y_sample, s5_re_p, s5_im_p, hg_p, s5_re_s, s5_im_s, hg_s)


_drawn_inputs = setup_inputs


def setup_inputs(seed=0):
    import zlib

    import numpy as np

    out = dict(_drawn_inputs(seed))
    spreads = {}
    factors = {}
    for name, (base, spread) in spreads.items():
        noise = np.random.default_rng([zlib.crc32(name.encode()), seed]).standard_normal(out[name].shape)
        drawn = base * np.exp(spread * noise) if base else spread * noise
        out[name] = __import__('jax').numpy.asarray(drawn.astype(out[name].dtype))
    for name, factor in factors.items():
        out[name] = (out[name] * factor).astype(out[name].dtype)
    return out
```

```python
from contextlib import ExitStack

import numpy as np
import concourse.bass as bass
from concourse import mybir

F32 = mybir.dt.float32
I32 = mybir.dt.int32
U32 = mybir.dt.uint32
ACT = mybir.ActivationFunctionType
ALU = mybir.AluOpType
AX = mybir.AxisListType
ds = bass.ds

P = 128
D = 1024
KC = D // P
TP, NB, LS = 256, 8, 4
TS = NB * LS
T = TP + TS
TILES = [(0, P), (P, P), (2 * P, TS)]

PAIRS = 32
GH = 16
QC = 4
HH = 8
CH = 64
NCH = TP // CH
PH, NK, TK = 8, 128, 16
RECTS = [(0, 1, 16), (1, 1, 8), (2, 2, 5), (4, 4, 3), (8, 8, 1)]
NC_ = sum(r * c for _, r, c in RECTS)

RING = 4
BLK = KC * P
EPS = 1e-6
F_LEAST = 2.0 ** -64
LOWEST = -3.0e38

SEGMENTS = [("glu", 16), ("wq0", 16), ("u0", NK), ("v0", NK), ("win", 32), ("wout", 8),
            ("wq1", 16), ("u1", NK), ("v1", NK)]
FIRST, _n = {}, 0
for _name, _c in SEGMENTS:
    FIRST[_name] = _n
    _n += _c

ACC = [[(c, 0, 0, T)] for c in range(6)] + \
      [[(0, T, 0, 512 - T), (1, T, 512 - T, 2 * T - 512)], [(2, T, 0, 512 - T), (3, T, 512 - T, 2 * T - 512)]]


class Count:

    def __init__(self, eng, sem):
        self.eng, self.sem, self.n, self.loop = eng, sem, 0, None

    def add(self, ins):
        ins.then_inc(self.sem, 1)
        self.n += 1
        return self.n

    def wait(self, n=None):
        v = self.n if n is None else n
        self.eng.wait_ge(self.sem, v if self.loop is None else v + self.loop)

    def link(self, ins):
        self.add(ins)
        self.wait()

    def enter(self, i, first, per):
        self.start, self.per, self.loop = self.n, per, (i - first) * per

    def leave(self, trips):
        assert self.n - self.start == self.per, (self.n - self.start, self.per)
        self.n, self.loop = self.start + trips * self.per, None


def build(nc, t_in, t_out):
    with ExitStack() as ctx:
        def sb(name, shape, dt=F32):
            return ctx.enter_context(nc.sbuf_tensor(name, shape, dt))

        def sem(name):
            return ctx.enter_context(nc.semaphore(name))

        big = sb("big", [P, NK * T])
        xT = sb("xT", [P, KC, T])
        hT = sb("hT", [P, KC, T])
        ring = sb("ring", [P, RING, BLK])
        ident = sb("ident", [P, P])
        ones = sb("ones", [P, P])
        iota = sb("iota", [P, P])
        iota_c = sb("iota_c", [P, NC_])
        epsc = sb("epsc", [P, 1])
        normw = sb("normw", [P, 5, KC])
        std = sb("std", [P, T])
        rinv = sb("rinv", [P, T])
        keysT = sb("keysT", [P, 2, 2, NK])
        i1T = sb("i1T", [P, T])
        i2T = sb("i2T", [P, T])
        gateT = sb("gateT", [P, T])
        stage = sb("stage", [P, 2, 4, 2, P])
        small = sb("small", [P, 256])
        ps = ctx.enter_context(nc.psum_tensor("ps", [P, 8, 512], F32))

        def bg(off, n):
            return big[:, off:off + n]

        loaded = [sem(f"loaded{k}") for k in range(RING)]
        used = sem("used")
        s_const = sem("s_const")
        s_x = sem("s_x")
        s_par = sem("s_par")
        s_keys = sem("s_keys")
        out_y = sem("out_y")
        out_s5 = sem("out_s5")
        out_hgp = sem("out_hgp")
        out_hgs = sem("out_hgs")
        dv = sem("dv")
        x_ready = sem("x_ready")
        norm_sq = sem("norm_sq")
        norm_ss = sem("norm_ss")
        norm_std = sem("norm_std")
        norm_h = sem("norm_h")

        block = ctx.enter_context(nc.Block())

        def zbank(k):
            return ps[:, 4 + k, 0:T]

        def stream_segment(sp, name):
            n0, src = FIRST[name], t_in[name]
            trips = dict(SEGMENTS)[name] // RING

            def body(i, first):
                for k in range(RING):
                    if not (first and n0 == 0):
                        sp.wait_ge(used, i * RING + (n0 + k - RING + 1))
                    sp.dma_start(ring[:, k, :], src[i * RING + k]).then_inc(loaded[k], 16)
            if n0 == 0:
                body(0, True)
                with sp.Fori(1, trips) as i:
                    body(i, False)
            else:
                with sp.Fori(0, trips) as i:
                    body(i, False)

        def project(pe, name, wait_bank, wait_bank_first, after=None):
            n0 = FIRST[name]
            trips = dict(SEGMENTS)[name] // RING

            def body(i, first):
                for k in range(RING):
                    pe.wait_ge(loaded[k], i * 16 + 16 * (n0 // RING + 1))
                    (wait_bank_first if first else wait_bank)(i, k)
                    for c in range(KC):
                        mm = nc.tensor.matmul(zbank(k), ring[:, k, c * P:(c + 1) * P], hT[:, c, :],
                                              start=(c == 0), stop=(c == KC - 1))
                    mm.then_inc(used, 1)
                    if after:
                        after(i, k, first)
            body(0, True)
            if trips > 1:
                with pe.Fori(1, trips) as i:
                    body(i, False)

        def norm_act(act, k, sq_at):
            act.wait_ge(x_ready, k + 1)
            if k == 0:
                act.wait_ge(s_const, 6)
            nc.scalar.activation(bg(sq_at, KC * T), xT[:, :, :].rearrange("p c t -> p (c t)"),
                                 ACT.Square).then_inc(norm_sq, 1)
            act.wait_ge(norm_ss, k + 1)
            nc.scalar.activation(std[:, :], ps[:, 0, 0:T], ACT.Sqrt, bias=epsc[:, 0:1],
                                 scale=1.0 / D).then_inc(norm_std, 1)

        def norm_pe(pe, k, sq_at):
            pe.wait_ge(norm_sq, k + 1)
            if k == 0:
                pe.wait_ge(s_const, 6)
            for c in range(KC):
                mm = nc.tensor.matmul(ps[:, 0, 0:T], ones[:, :], bg(sq_at + c * T, T),
                                      start=(c == 0), stop=(c == KC - 1))
            mm.then_inc(norm_ss, 1)

        def norm_dve(v, cnt, k):
            v.wait_ge(norm_std, k + 1)
            cnt.link(nc.vector.reciprocal(rinv[:, :], std[:, :]))
            for c in range(KC):
                nc.vector.scalar_tensor_tensor(out=hT[:, c, :], in0=xT[:, c, :], scalar=normw[:, k, c:c + 1],
                                               in1=rinv[:, :], op0=ALU.mult, op1=ALU.mult).then_inc(norm_h, 1)

        ST = bg(0, 2 * PAIRS * T).rearrange("p (r q t) -> p r q t", r=2, q=PAIRS)
        TMPW = 2 * PAIRS * T
        TAB = [bg(TMPW + 4096 * k, 4096).rearrange("p (q t) -> p q t", q=PAIRS) for k in range(4)]
        bbar = bg(34816, 1024).rearrange("p (r n) -> p r n", r=2)
        craw = bg(35840, 1024).rearrange("p (r n) -> p r n", r=2)
        s5w = sb("s5w", [P, 2, PAIRS * GH])
        wdiag = [bg(TMPW + 1280 * k, 1280).rearrange("p (r m) -> p r m", r=2) for k in range(2)]
        btr = [bg(TMPW + 2560 + 1024 * k, 1024).rearrange("p (r m) -> p r m", r=2) for k in range(2)]
        w0 = TMPW + 4608
        prod = [[bg(w0 + 1024 * k + 512 * m, 512).rearrange("p (r t) -> p r t", r=2) for m in range(2)]
                for k in range(2)]
        w0 += 2048
        zin = [bg(w0 + 512 * k, 512).rearrange("p (r t) -> p r t", r=2) for k in range(2)]
        w0 += 1024
        zsc = [bg(w0 + 512 * k, 512).rearrange("p (r t) -> p r t", r=2) for k in range(2)]
        w0 += 1024
        pout = [[bg(w0 + 1024 * k + 512 * m, 512).rearrange("p (r t) -> p r t", r=2) for m in range(2)]
                for k in range(2)]
        w0 += 2048
        s0 = bg(w0, 512).rearrange("p (r q b) -> p r q b", r=2, q=PAIRS)
        w0 += 512
        sa = [bg(w0 + 512 * k, 512).rearrange("p (r q b) -> p r q b", r=2, q=PAIRS) for k in range(2)]
        w0 += 1024
        fin5 = bg(w0, 2 * PAIRS * 9).rearrange("p (r q b) -> p r q b", r=2, q=PAIRS)
        w0 += 576
        assert w0 <= 34816
        par = sb("par", [P, 16, PAIRS])
        dcol = sb("dcol", [P, KC])
        PR = {n: par[:, i, :] for i, n in enumerate(
            ["lr", "li", "dt", "mag", "ang", "c", "s", "ar", "ai", "zr", "zi", "t0", "t1", "t2", "t3", "t4"])}

        s5_in = sem("s5_in")
        s5_s0 = sem("s5_s0")
        s5_exp = sem("s5_exp")
        s5_arg = sem("s5_arg")
        s5_table = sem("s5_table")
        s5_tab_add = sem("s5_tab_add")
        s5_tab_mul = sem("s5_tab_mul")
        s5_diag = sem("s5_diag")
        s5_zero = sem("s5_zero")
        s5_tr = sem("s5_tr")
        s5_trc = sem("s5_trc")
        s5_bu = sem("s5_bu")
        s5_smp = sem("s5_smp")
        s5_min = sem("s5_min")
        s5_ain = sem("s5_ain")
        s5_scan = sem("s5_scan")
        s5_mout = sem("s5_mout")
        s5_aout = sem("s5_aout")
        s5_rec = sem("s5_rec")
        s5_cd = sem("s5_cd")
        s5_y = sem("s5_y")
        s5_yd = sem("s5_yd")
        s5_g = sem("s5_g")
        s5_fin = sem("s5_fin")

        def s5_params_act(act):
            act.wait_ge(s5_in, 16 * 6)
            nc.scalar.activation(PR["dt"], PR["dt"], ACT.Exp).then_inc(s5_exp, 1)
            act.wait_ge(s5_arg, 1)
            nc.scalar.activation(PR["mag"], PR["t0"], ACT.Exp).then_inc(s5_exp, 1)

        def s5_params_dve(v, cnt):
            tt, ts = nc.vector.tensor_tensor, nc.vector.tensor_scalar
            L = cnt.link
            v.wait_ge(s5_in, 16 * 6)
            L(ts(PR["lr"], PR["lr"], -1e-4, None, ALU.min))
            v.wait_ge(s5_exp, 1)
            tt(PR["t0"], PR["lr"], PR["dt"], ALU.mult).then_inc(s5_arg, 1)
            L(tt(PR["ang"], PR["li"], PR["dt"], ALU.mult))
            rnd = 1.5 * 2.0 ** 23
            L(ts(PR["t1"], PR["ang"], 1.0 / (2 * np.pi), rnd, ALU.mult, ALU.add))
            L(ts(PR["t1"], PR["t1"], rnd, None, ALU.subtract))
            whole = 2 * np.pi
            for part in (6.28125, float(np.float32(whole - 6.28125)),
                         float(whole - 6.28125 - np.float64(np.float32(whole - 6.28125)))):
                L(ts(PR["t2"], PR["t1"], part, None, ALU.mult))
                L(tt(PR["ang"], PR["ang"], PR["t2"], ALU.subtract))
            L(ts(PR["t1"], PR["ang"], 0.125, None, ALU.mult))
            L(tt(PR["t2"], PR["t1"], PR["t1"], ALU.mult))
            L(ts(PR["s"], PR["t2"], 1.0 / 362880, -1.0 / 5040, ALU.mult, ALU.add))
            L(ts(PR["c"], PR["t2"], -1.0 / 3628800, 1.0 / 40320, ALU.mult, ALU.add))
            for a, b in ((1.0 / 120, -1.0 / 720), (-1.0 / 6, 1.0 / 24), (1.0, -0.5)):
                L(tt(PR["s"], PR["s"], PR["t2"], ALU.mult))
                L(ts(PR["s"], PR["s"], a, None, ALU.add))
                L(tt(PR["c"], PR["c"], PR["t2"], ALU.mult))
                L(ts(PR["c"], PR["c"], b, None, ALU.add))
            L(tt(PR["s"], PR["s"], PR["t1"], ALU.mult))
            L(tt(PR["c"], PR["c"], PR["t2"], ALU.mult))
            for _ in range(3):
                L(tt(PR["t3"], PR["s"], PR["c"], ALU.mult))
                L(tt(PR["t2"], PR["s"], PR["s"], ALU.mult))
                L(ts(PR["c"], PR["t2"], -2.0, None, ALU.mult))
                L(tt(PR["t3"], PR["t3"], PR["s"], ALU.add))
                L(ts(PR["s"], PR["t3"], 2.0, None, ALU.mult))
            L(ts(PR["c"], PR["c"], 1.0, None, ALU.add))
            v.wait_ge(s5_exp, 2)
            L(tt(PR["ar"], PR["mag"], PR["c"], ALU.mult))
            L(tt(PR["ai"], PR["mag"], PR["s"], ALU.mult))
            L(tt(PR["t0"], PR["lr"], PR["lr"], ALU.mult))
            L(tt(PR["t1"], PR["li"], PR["li"], ALU.mult))
            L(tt(PR["t0"], PR["t0"], PR["t1"], ALU.add))
            L(nc.vector.reciprocal(PR["t1"], PR["t0"]))
            L(ts(PR["t0"], PR["ar"], -1.0, None, ALU.add))
            L(tt(PR["t2"], PR["t0"], PR["lr"], ALU.mult))
            L(tt(PR["t3"], PR["ai"], PR["li"], ALU.mult))
            L(tt(PR["t2"], PR["t2"], PR["t3"], ALU.add))
            L(tt(PR["zr"], PR["t2"], PR["t1"], ALU.mult))
            L(tt(PR["t2"], PR["ai"], PR["lr"], ALU.mult))
            L(tt(PR["t3"], PR["t0"], PR["li"], ALU.mult))
            L(tt(PR["t2"], PR["t2"], PR["t3"], ALU.subtract))
            L(tt(PR["zi"], PR["t2"], PR["t1"], ALU.mult))
            sh = [P, PAIRS, GH]
            zr, zi = (PR[n][:, :, None].to_broadcast(sh) for n in ("zr", "zi"))
            w3 = [s5w[:, r, :].rearrange("p (q h) -> p q h", q=PAIRS) for r in range(2)]
            b3 = [bbar[:, r, :].rearrange("p (q h) -> p q h", q=PAIRS) for r in range(2)]
            u3 = [TAB[k].rearrange("p q t -> p (q t)")[:, 0:512].rearrange("p (q h) -> p q h", q=PAIRS)
                  for k in range(4)]
            cnt.add(tt(u3[0], zr, w3[0], ALU.mult))
            cnt.add(tt(u3[1], zi, w3[1], ALU.mult))
            cnt.add(tt(u3[2], zr, w3[1], ALU.mult))
            L(tt(u3[3], zi, w3[0], ALU.mult))
            cnt.add(tt(b3[0], u3[0], u3[1], ALU.subtract))
            L(tt(b3[1], u3[2], u3[3], ALU.add))
            L(ts(craw[:, 1, :], craw[:, 1, :], -1.0, None, ALU.mult))

        def s5_table_dve(v, cnt):
            tt = nc.vector.tensor_tensor
            L = cnt.link
            L(nc.vector.memset(ST[:, 0, :, 0:1], 1.0))
            L(nc.vector.memset(ST[:, 1, :, 0:1], 0.0))
            cr, ci = PR["c"], PR["s"]
            for lev in range(8):
                w = 1 << lev
                sh = [P, PAIRS, w]
                crb, cib = cr[:, :, None].to_broadcast(sh), ci[:, :, None].to_broadcast(sh)
                if lev:
                    v.wait_ge(s5_tab_add, 2 * lev)
                tt(TAB[0][:, :, 0:w], ST[:, 0, :, 0:w], crb, ALU.mult).then_inc(s5_tab_mul, 1)
                tt(TAB[1][:, :, 0:w], ST[:, 1, :, 0:w], cib, ALU.mult).then_inc(s5_tab_mul, 1)
                tt(TAB[2][:, :, 0:w], ST[:, 0, :, 0:w], cib, ALU.mult).then_inc(s5_tab_mul, 1)
                tt(TAB[3][:, :, 0:w], ST[:, 1, :, 0:w], crb, ALU.mult).then_inc(s5_tab_mul, 1)
                if lev < 7:
                    v.wait_ge(s5_tab_mul, 4 * lev + 4)
                    cnt.add(tt(PR["t0"], cr, cr, ALU.mult))
                    cnt.add(tt(PR["t1"], ci, ci, ALU.mult))
                    L(tt(PR["t2"], cr, ci, ALU.mult))
                    cnt.add(tt(cr, PR["t0"], PR["t1"], ALU.subtract))
                    L(nc.vector.tensor_scalar(ci, PR["t2"], 2.0, None, ALU.mult))

        def s5_table_pool(g):
            tt = nc.gpsimd.tensor_tensor
            for lev in range(8):
                w = 1 << lev
                g.wait_ge(s5_tab_mul, 4 * lev + 4)
                tt(ST[:, 0, :, w:2 * w], TAB[0][:, :, 0:w], TAB[1][:, :, 0:w], ALU.subtract).then_inc(s5_tab_add, 1)
                tt(ST[:, 1, :, w:2 * w], TAB[2][:, :, 0:w], TAB[3][:, :, 0:w], ALU.add).then_inc(s5_tab_add, 1)
            g.wait_ge(s5_tab_add, 16)
            for k in range(2):
                nc.gpsimd.memset(wdiag[k], 0.0).then_inc(s5_zero, 1)
            g.wait_ge(s5_zero, 2)

        def fill_diag(x, src, c):
            for g2 in range(2):
                rows = slice(64 * g2, 64 * g2 + 64)
                dst = wdiag[x][rows, :, :].rearrange("p r (q m) -> p r q m", q=QC)[:, :, :, GH * g2:GH * g2 + GH]
                s = src[rows, :, ds(c * (QC * GH), QC * GH)].rearrange("p r (q h) -> p r q h", q=QC)
                nc.scalar.activation(dst, s, ACT.Copy).then_inc(s5_diag, 1)

        def s5_in_pool(g):
            def add_in(i, k, first):
                g.wait_ge(s5_min, i * 16 + 2 * k + 2)
                if not (first and k < 2):
                    g.wait_ge(s5_scan, i * 16 + 2 * (k - 2) + 2)
                nc.gpsimd.tensor_tensor(zin[k % 2][:, 0, :], prod[k % 2][0][:, 0, :], prod[k % 2][1][:, 1, :],
                                        ALU.add).then_inc(s5_ain, 1)
                nc.gpsimd.tensor_tensor(zin[k % 2][:, 1, :], prod[k % 2][1][:, 0, :], prod[k % 2][0][:, 1, :],
                                        ALU.subtract).then_inc(s5_ain, 1)

            def add_out(i, k):
                pair = i * 8 + k
                g.wait_ge(s5_mout, i * 16 + 2 * k + 2)
                nc.gpsimd.tensor_tensor(ST[:, 0, ds(pair, 1), 0:TP].rearrange("p o t -> p (o t)"),
                                        pout[k % 2][0][:, 0, :], pout[k % 2][1][:, 1, :],
                                        ALU.subtract).then_inc(s5_aout, 1)
                nc.gpsimd.tensor_tensor(ST[:, 1, ds(pair, 1), 0:TP].rearrange("p o t -> p (o t)"),
                                        pout[k % 2][0][:, 1, :], pout[k % 2][1][:, 0, :],
                                        ALU.add).then_inc(s5_aout, 1)

            def body(i, first):
                for k in range(8):
                    add_in(i, k, first)
                    if k:
                        add_out(i, k - 1)
                    elif not first:
                        add_out(i - 1, 7)
            body(0, True)
            with g.Fori(1, 4) as i:
                body(i, False)
            add_out(3, 7)

        def s5_in_pe(pe):
            pe.wait_ge(norm_h, KC)

            def body(i, first):
                for x in range(2):
                    pe.wait_ge(s5_diag, i * 4 + 2 * x + 2)
                    if not (first and x == 0):
                        pe.wait_ge(s5_trc, i * 4 + 2 * x)
                    for r in range(2):
                        for q in range(QC):
                            mm = nc.tensor.transpose(ps[:, r, q * P:(q + 1) * P], wdiag[x][:, r, q * P:(q + 1) * P],
                                                     ident[:, :])
                    mm.then_inc(s5_tr, 1)
                    pe.wait_ge(s5_trc, i * 4 + 2 * x + 2)
                    for q in range(QC):
                        k = x * QC + q
                        if not (first and k < 2):
                            pe.wait_ge(s5_min, i * 16 + 2 * (k - 2) + 2)
                            pe.wait_ge(s5_smp, i * 8 + k - 1)
                        for r in range(2):
                            mm = nc.tensor.matmul(ps[:, 2 + 2 * (k % 2) + r, 0:T], btr[x][:, r, q * P:(q + 1) * P],
                                                  hT[:, ds(i * 2 + x, 1), :].rearrange("p o t -> p (o t)"),
                                                  start=True, stop=True)
                        mm.then_inc(s5_bu, 1)
            body(0, True)
            with pe.Fori(1, 4) as i:
                body(i, False)

        def s5_in_act(act):
            act.wait_ge(s5_tab_add, 16)
            act.wait_ge(s5_zero, 2)

            def body(i, first):
                for x in range(2):
                    if not first:
                        act.wait_ge(s5_tr, i * 2 + x - 1)
                    fill_diag(x, bbar, i * 2 + x)
                    act.wait_ge(s5_tr, i * 2 + x + 1)
                    if not first:
                        act.wait_ge(s5_bu, i * 8 + x * 4 - 4)
                    for r in range(2):
                        nc.scalar.activation(btr[x][:, r, :], ps[:, r, :], ACT.Copy).then_inc(s5_trc, 1)
                    for q in range(QC):
                        k = x * QC + q
                        act.wait_ge(s5_bu, i * 8 + k + 1)
                        nc.scalar.activation(
                            ST[:, :, ds(i * 8 + k, 1), TP:T].rearrange("p r o t -> p r (o t)"),
                            ps[:, 2 + 2 * (k % 2):4 + 2 * (k % 2), TP:T], ACT.Copy).then_inc(s5_smp, 1)
            body(0, True)
            with act.Fori(1, 4) as i:
                body(i, False)

        def s5_in_dve(v):
            v.wait_ge(s5_tab_add, 16)
            sh = [P, 2, TP]

            def e_of(pair):
                return ST[:, :, ds(pair, 1), 0:TP].rearrange("p r o t -> p r (o t)")

            def mul_in(i, k, first):
                v.wait_ge(s5_smp, i * 8 + k + 1)
                if not (first and k < 2):
                    v.wait_ge(s5_ain, i * 16 + 2 * (k - 2) + 2)
                for m in range(2):
                    nc.vector.tensor_tensor(prod[k % 2][m], ps[:, 2 + 2 * (k % 2) + m, None, 0:TP].to_broadcast(sh),
                                            e_of(i * 8 + k), ALU.mult).then_inc(s5_min, 1)

            def scan_out(i, k, first):
                pair = i * 8 + k
                v.wait_ge(s5_ain, i * 16 + 2 * k + 2)
                if not (first and k < 2):
                    v.wait_ge(s5_mout, i * 16 + 2 * (k - 2) + 2)
                for r in range(2):
                    nc.vector.tensor_tensor_scan(zsc[k % 2][:, r, :], PR["mag"][:, ds(pair, 1)].to_broadcast([P, TP]),
                                                 zin[k % 2][:, r, :], 0.0, ALU.mult, ALU.add).then_inc(s5_scan, 1)
                v.wait_ge(s5_scan, i * 16 + 2 * k + 2)
                if not (first and k < 2):
                    v.wait_ge(s5_aout, i * 16 + 2 * (k - 2) + 2)
                for m in range(2):
                    nc.vector.tensor_tensor(pout[k % 2][m], zsc[k % 2][:, m:m + 1, :].to_broadcast(sh),
                                            e_of(pair), ALU.mult).then_inc(s5_mout, 1)

            def body(i, first):
                for k in range(8):
                    mul_in(i, k, first)
                    if k:
                        scan_out(i, k - 1, first)
                    elif not first:
                        scan_out(i - 1, 7, False)
            body(0, True)
            with v.Fori(1, 4) as i:
                body(i, False)
            scan_out(3, 7, False)

        def s5_samples_dve(v, cnt):
            tt = nc.vector.tensor_tensor
            L = cnt.link
            v.wait_ge(s5_smp, 32)
            v.wait_ge(s5_s0, 16)
            smp = ST[:, :, :, TP:T].rearrange("p r q (b s) -> p r q b s", b=NB)
            sh3 = [P, PAIRS, NB]
            arb, aib = (PR[n][:, :, None].to_broadcast(sh3) for n in ("ar", "ai"))
            for s in range(LS):
                prev = [s0[:, r] if s == 0 else smp[:, r, :, :, s - 1] for r in range(2)]
                cnt.add(tt(sa[0][:, 0], arb, prev[0], ALU.mult))
                cnt.add(tt(sa[0][:, 1], arb, prev[1], ALU.mult))
                cnt.add(tt(sa[1][:, 0], aib, prev[1], ALU.mult))
                L(tt(sa[1][:, 1], aib, prev[0], ALU.mult))
                cnt.add(tt(sa[0][:, 0], sa[0][:, 0], sa[1][:, 0], ALU.subtract))
                L(tt(sa[0][:, 1], sa[0][:, 1], sa[1][:, 1], ALU.add))
                for r in range(2):
                    ins = tt(smp[:, r, :, :, s], smp[:, r, :, :, s], sa[0][:, r], ALU.add)
                    if s == LS - 1:
                        ins.then_inc(s5_rec, 1)
                    else:
                        cnt.add(ins)
                if s < LS - 1:
                    cnt.wait()
            v.wait_ge(s5_rec, 2)
            v.wait_ge(s5_aout, 64)
            for r in range(2):
                nc.vector.tensor_copy(fin5[:, r, :, 0:1], ST[:, r, :, TP - 1:TP]).then_inc(s5_fin, 1)
                nc.vector.tensor_copy(fin5[:, r, :, 1:9], smp[:, r, :, :, LS - 1]).then_inc(s5_fin, 1)

        def s5_out_pe(pe):
            pe.wait_ge(s5_rec, 2)
            pe.wait_ge(s5_aout, 64)
            pe.wait_ge(s5_smp, 32)

            def body(i, first):
                for x in range(2):
                    pe.wait_ge(s5_diag, 16 + i * 4 + 2 * x + 2)
                    if first:
                        pe.wait_ge(s5_min, 64)
                    else:
                        pe.wait_ge(s5_yd, i * 2 + x - 1)
                    for q in range(QC):
                        for r in range(2):
                            mm = nc.tensor.matmul(ps[:, 2 + x, 0:T], wdiag[x][:, r, q * P:(q + 1) * P],
                                                  ST[:, r, ds(i * 8 + x * QC + q, 1), :].rearrange("p o t -> p (o t)"),
                                                  start=(q == 0 and r == 0), stop=(q == QC - 1 and r == 1))
                    mm.then_inc(s5_y, 1)
            body(0, True)
            with pe.Fori(1, 4) as i:
                body(i, False)

        def s5_out_dve(v):
            v.wait_ge(s5_bu, 32)
            with v.Fori(0, 4) as i:
                for x in range(2):
                    v.wait_ge(s5_y, i * 2 + x + 1)
                    u = hT[:, ds(i * 2 + x, 1), :].rearrange("p o t -> p (o t)")
                    nc.vector.scalar_tensor_tensor(out=u, in0=u, scalar=dcol[:, ds(i * 2 + x, 1)],
                                                   in1=ps[:, 2 + x, 0:T], op0=ALU.mult, op1=ALU.add).then_inc(s5_yd, 1)

        def s5_out_act(act):
            act.wait_ge(s5_tr, 8)

            def gelu(c):
                act.wait_ge(s5_yd, c + 1)
                u = hT[:, ds(c, 1), :].rearrange("p o t -> p (o t)")
                nc.scalar.activation(u, u, ACT.Gelu).then_inc(s5_g, 1)

            def body(i, first):
                for x in range(2):
                    if not first:
                        act.wait_ge(s5_y, i * 2 + x - 1)
                    fill_diag(x, craw, i * 2 + x)
                    if x or not first:
                        gelu(i * 2 + x - 1)
            body(0, True)
            with act.Fori(1, 4) as i:
                body(i, False)
            gelu(KC - 1)

        sig = [bg(TMPW + T * k, T) for k in range(2)]
        gated = [bg(TMPW + 2 * T + T * k, T) for k in range(2)]
        glu_sig = sem("glu_sig")
        glu_mul = sem("glu_mul")
        glu_x = sem("glu_x")

        def glu_pe(pe):
            pe.wait_ge(s5_g, KC)

            def first(i, k):
                if k == 0:
                    pe.wait_ge(s5_min, 64)

            project(pe, "glu", lambda i, k: pe.wait_ge(glu_mul, i * 2 + k // 2 - 1) if k % 2 == 0 else None, first)

        def glu_act(act):
            act.wait_ge(s5_y, KC)

            def body(i, first):
                for m in range(2):
                    act.wait_ge(used, i * 4 + 2 * m + 2)
                    if not first:
                        act.wait_ge(glu_mul, i * 2 + m - 1)
                    nc.scalar.activation(sig[m], zbank(2 * m + 1), ACT.Sigmoid).then_inc(glu_sig, 1)
            body(0, True)
            with act.Fori(1, 4) as i:
                body(i, False)

        def glu_dve(v):
            def body(i, first):
                for m in range(2):
                    v.wait_ge(glu_sig, i * 2 + m + 1)
                    if not first:
                        v.wait_ge(glu_x, i * 2 + m - 1)
                    nc.vector.tensor_tensor(gated[m], zbank(2 * m), sig[m], ALU.mult).then_inc(glu_mul, 1)
                    v.wait_ge(glu_mul, i * 2 + m + 1)
                    x = xT[:, ds(i * 2 + m, 1), :].rearrange("p o t -> p (o t)")
                    nc.vector.tensor_tensor(x, x, gated[m], ALU.add).then_inc(glu_x, 1)
            body(0, True)
            with v.Fori(1, 4) as i:
                body(i, False)
            v.wait_ge(glu_x, KC)
            v.sem_inc(x_ready, 1)

        act3 = big[:, :].rearrange("p (j t) -> p j t", j=NK)
        SPLITS = [(0, 64), (64, 96), (96, NK)]
        o = 96 * T

        def take(n, dt=None):
            nonlocal o
            a = bg(o, n)
            o += n
            return a.bitcast(dt) if dt else a

        val = take(768).rearrange("p (j f h k) -> p j f h k", j=3, f=2, h=PH)
        idu = take(768, U32).rearrange("p (j f h k) -> p j f h k", j=3, f=2, h=PH)
        idf = take(768).rearrange("p (j f h k) -> p j f h k", j=3, f=2, h=PH)
        rest = [take(NK) for _ in range(3)]
        cand = take(PH * NC_).rearrange("p (h n) -> p h n", h=PH)
        cidx = take(PH * NC_).rearrange("p (h n) -> p h n", h=PH)
        rest2 = [take(NC_) for _ in range(2)]
        sc = take(3 * P).rearrange("p (j h k) -> p j h k", j=3, h=PH)
        gate = take(3 * P).rearrange("p (j h k) -> p j h k", j=3, h=PH)
        posu = take(P, U32).rearrange("p (h k) -> p h k", h=PH)
        posf = take(P).rearrange("p (h k) -> p h k", h=PH)
        eq = [take(TK * NC_).rearrange("p (k n) -> p k n", k=TK) for _ in range(2)]
        eid = take(3 * P).rearrange("p (j n) -> p j n", j=3)
        eii = take(3 * P, I32).rearrange("p (j n) -> p j n", j=3)
        e12i = take(6 * P, I32).rearrange("p (j f n) -> p j f n", j=3, f=2)
        e12 = take(6 * P).rearrange("p (j f n) -> p j f n", j=3, f=2)
        sm = take(3 * PH).rearrange("p (j h) -> p j h", j=3)
        rs = take(3 * PH).rearrange("p (j h) -> p j h", j=3)
        assert o <= NK * T
        qbuf = [stage[:, k, :, :, :].rearrange("p a b c -> p (a b c)")[:, 0:T] for k in range(2)]

        pq = [sem(f"peer_q{L}") for L in range(2)]
        psc = [sem(f"peer_scores{L}") for L in range(2)]
        ptk = [sem(f"peer_topk{L}") for L in range(2)]
        pge = [sem(f"peer_gelu{L}") for L in range(2)]
        psh = [sem(f"peer_shift{L}") for L in range(2)]
        pex = [sem(f"peer_exp{L}") for L in range(2)]
        pgt = [sem(f"peer_gate{L}") for L in range(2)]
        ptr = [sem(f"peer_tr{L}") for L in range(2)]
        ptc = [sem(f"peer_trc{L}") for L in range(2)]
        poh = [sem(f"peer_onehot{L}") for L in range(2)]
        pG = [sem(f"peer_G{L}") for L in range(2)]
        pmul = [sem(f"peer_mul{L}") for L in range(2)]
        pacc = [sem(f"peer_acc{L}") for L in range(2)]

        def peer_query_pe(pe, L):
            n0 = FIRST[f"wq{L}"]
            pe.wait_ge(norm_h, KC * (2 * L + 2))
            if L == 0:
                pe.wait_ge(s_keys, 16)

            def scores(i, k, first):
                pe.wait_ge(pq[L], i * 4 + k + 1)
                if not (first and k < 2):
                    pe.wait_ge(ptk[L], i * 4 + k - 1)
                for j, (t0, w) in enumerate(TILES):
                    mm = nc.tensor.matmul(ps[0:w, k % 2, j * NK:(j + 1) * NK], qbuf[k % 2][:, t0:t0 + w],
                                          keysT[:, L, k % 2, :], start=True, stop=True)
                mm.then_inc(psc[L], 1)

            def after(i, k, first):
                if k:
                    scores(i, k - 1, first)
                elif not first:
                    scores(i - 1, 3, False)
            project(pe, f"wq{L}", lambda i, k: pe.wait_ge(pq[L], i * 4 + k - 3), lambda i, k: None, after)
            scores(3, 3, False)

        def peer_query_act(act, L):
            n0 = FIRST[f"wq{L}"]

            def body(i, first):
                for k in range(4):
                    act.wait_ge(used, i * 4 + (n0 + k + 1))
                    if not (first and k < 2):
                        act.wait_ge(psc[L], i * 4 + k - 1)
                    nc.scalar.activation(qbuf[k % 2], zbank(k), ACT.Copy).then_inc(pq[L], 1)
            body(0, True)
            with act.Fori(1, 4) as i:
                body(i, False)

        def states_out(eng, L):
            for o_ in ((out_s5,), (out_hgp, out_hgs))[L]:
                eng.wait_ge(o_, 16)

        def peer_topk_dve(v, cnt, L):
            vv = nc.vector
            states_out(v, L)
            for b in range(2 * PH):
                h, f = b // 2, b % 2
                v.wait_ge(psc[L], b + 1)
                for j, (_, w) in enumerate(TILES):
                    s = ps[0:w, b % 2, j * NK:(j + 1) * NK]
                    cnt.add(vv.max(val[0:w, j, f, h, 0:8], s))
                cnt.wait()
                for j, (_, w) in enumerate(TILES):
                    s = ps[0:w, b % 2, j * NK:(j + 1) * NK]
                    cnt.add(vv.max_index(idu[0:w, j, f, h, 0:8], val[0:w, j, f, h, 0:8], s))
                for j, (_, w) in enumerate(TILES):
                    s = ps[0:w, b % 2, j * NK:(j + 1) * NK]
                    ins = vv.match_replace(rest[j][0:w, :], val[0:w, j, f, h, 0:8], s, LOWEST)
                    if j == 2:
                        ins.then_inc(ptk[L], 1)
                    else:
                        cnt.add(ins)
                v.wait_ge(ptk[L], b + 1)
                for j, (_, w) in enumerate(TILES):
                    cnt.add(vv.max(val[0:w, j, f, h, 8:16], rest[j][0:w, :]))
                cnt.wait()
                for j, (_, w) in enumerate(TILES):
                    cnt.add(vv.max_index(idu[0:w, j, f, h, 8:16], val[0:w, j, f, h, 8:16], rest[j][0:w, :]))
                cnt.wait()

        def peer_pairs_dve(v, cnt, L):
            vv = nc.vector
            L_ = cnt.link
            for j, (_, w) in enumerate(TILES):
                for f in range(2):
                    L_(vv.tensor_copy(idf[0:w, j, f], idu[0:w, j, f]))
                L_(vv.tensor_scalar(idf[0:w, j, 0], idf[0:w, j, 0], float(NK), None, ALU.mult))
                for src, dst in ((val, cand), (idf, cidx)):
                    at = 0
                    for a0, na, nb in RECTS:
                        sh = [w, PH, na, nb]
                        cnt.add(vv.tensor_tensor(
                            dst[0:w, :, at:at + na * nb].rearrange("p h (a b) -> p h a b", a=na),
                            src[0:w, j, 0, :, a0:a0 + na, None].to_broadcast(sh),
                            src[0:w, j, 1, :, None, 0:nb].to_broadcast(sh), ALU.add))
                        at += na * nb
                cnt.wait()
                for h in range(PH):
                    c = cand[0:w, h, :]
                    r = rest2[h % 2][0:w, :]
                    L_(vv.max(sc[0:w, j, h, 0:8], c))
                    cnt.add(vv.max_index(posu[0:w, h, 0:8], sc[0:w, j, h, 0:8], c))
                    L_(vv.match_replace(r, sc[0:w, j, h, 0:8], c, LOWEST))
                    L_(vv.max(sc[0:w, j, h, 8:16], r))
                    L_(vv.max_index(posu[0:w, h, 8:16], sc[0:w, j, h, 8:16], r))
                L_(vv.tensor_copy(posf[0:w], posu[0:w]))
                sh = [w, TK, NC_]
                for h in range(PH):
                    e = eq[h % 2][0:w]
                    L_(vv.tensor_tensor(e, iota_c[0:w, None, :].to_broadcast(sh),
                                        posf[0:w, h, :, None].to_broadcast(sh), ALU.is_equal))
                    L_(vv.tensor_tensor(e, e, cidx[0:w, h, None, :].to_broadcast(sh), ALU.mult))
                    L_(vv.tensor_reduce(eid[0:w, j, h * TK:(h + 1) * TK], e, AX.X, ALU.add))
                vv.tensor_tensor(gate[0:w, j], sc[0:w, j], sc[0:w, j, :, 0:1].to_broadcast([w, PH, TK]),
                                 ALU.subtract).then_inc(psh[L], 1)
                L_(vv.tensor_copy(eii[0:w, j], eid[0:w, j]))
                cnt.add(vv.tensor_scalar(e12i[0:w, j, 0], eii[0:w, j], 7, None, ALU.arith_shift_right))
                L_(vv.tensor_scalar(e12i[0:w, j, 1], eii[0:w, j], NK - 1, None, ALU.bitwise_and))
                L_(vv.tensor_copy(e12[0:w, j], e12i[0:w, j]))
            for j, (_, w) in enumerate(TILES):
                v.wait_ge(pex[L], j + 1)
                L_(vv.tensor_reduce(sm[0:w, j], gate[0:w, j], AX.X, ALU.add))
                L_(vv.reciprocal(rs[0:w, j], sm[0:w, j]))
                vv.tensor_tensor(gate[0:w, j], gate[0:w, j], rs[0:w, j, :, None].to_broadcast([w, PH, TK]),
                                 ALU.mult).then_inc(pgt[L], 1)
            for j, (t0, w) in enumerate(TILES):
                for m, dst in enumerate((i1T, i2T, gateT)):
                    v.wait_ge(ptr[L], 3 * j + m + 1)
                    vv.tensor_copy(dst[:, t0:t0 + w], ps[:, m, 0:w]).then_inc(ptc[L], 1)

        def peer_exp_act(act, L):
            act.wait_ge(psh[L], 3)
            for j, (_, w) in enumerate(TILES):
                nc.scalar.activation(gate[0:w, j], gate[0:w, j], ACT.Exp).then_inc(pex[L], 1)

        def peer_tr_pe(pe, L):
            pe.wait_ge(pgt[L], 3)
            pe.wait_ge(ptk[L], 2 * PH)
            for j, (t0, w) in enumerate(TILES):
                for m in range(3):
                    src = (e12[0:w, j, m] if m < 2 else gate[0:w, j].rearrange("p h k -> p (h k)"))
                    if j:
                        pe.wait_ge(ptc[L], 3 * (j - 1) + m + 1)
                    nc.tensor.transpose(ps[:, m, 0:w], src, ident[0:w, 0:w]).then_inc(ptr[L], 1)

        def peer_u_pe(pe, L, a, b):
            n0 = FIRST[f"u{L}"]
            if a == 0:
                pe.wait_ge(pq[L], 16)
            with pe.Fori(a // RING, b // RING) as i:
                for k in range(RING):
                    pe.wait_ge(loaded[k], i * 16 + 16 * (n0 // RING + 1))
                    pe.wait_ge(pge[L], i * 4 + k - 3 + 4)
                    for c in range(KC):
                        mm = nc.tensor.matmul(zbank(k), ring[:, k, c * P:(c + 1) * P], hT[:, c, :],
                                              start=(c == 0), stop=(c == KC - 1))
                    mm.then_inc(used, 1)

        def peer_u_act(act, L, a, b):
            n0 = FIRST[f"u{L}"]
            if a == 0:
                states_out(act, L)
                act.sem_inc(pge[L], 4)
            if a == 96:
                act.wait_ge(ptr[L], 9)
            with act.Fori(a // RING, b // RING) as i:
                for k in range(RING):
                    act.wait_ge(used, i * 4 + (n0 + k + 1))
                    nc.scalar.activation(act3[:, ds(i * RING + k, 1), :].rearrange("p o t -> p (o t)"), zbank(k),
                                         ACT.Gelu).then_inc(pge[L], 1)

        def peer_g_dve(v, L):
            vv = nc.vector
            v.wait_ge(ptc[L], 9)
            v.wait_ge(pge[L], NK + 4)

            def build(i, x, first):
                if not first:
                    v.wait_ge(pG[L], i * 2 + x - 1)
                for s in range(4):
                    tok = i * 8 + 4 * x + s
                    vv.tensor_scalar(stage[:, x, s, 0, :], iota[:, :], i1T[:, ds(tok, 1)], None,
                                     ALU.is_equal).then_inc(poh[L], 1)
                    vv.tensor_scalar(stage[:, x, s, 1, :], iota[:, :], i2T[:, ds(tok, 1)], gateT[:, ds(tok, 1)],
                                     ALU.is_equal, ALU.mult).then_inc(poh[L], 1)

            def mul(i, x):
                v.wait_ge(pG[L], i * 2 + x + 1)
                a = act3[:, :, ds(i * 8 + 4 * x, 4)]
                vv.tensor_tensor(a, a, ps[:, x, :].rearrange("p (s j) -> p j s", s=4), ALU.mult).then_inc(pmul[L], 1)

            def body(i, first):
                build(i, 0, first)
                if not first:
                    mul(i - 1, 1)
                build(i, 1, first)
                mul(i, 0)
            body(0, True)
            with v.Fori(1, T // 8) as i:
                body(i, False)
            mul(T // 8 - 1, 1)

        def peer_g_pe(pe, L):
            def body(i, first):
                for x in range(2):
                    if not first:
                        pe.wait_ge(pmul[L], i * 2 + x - 1)
                    pe.wait_ge(poh[L], i * 16 + 8 * x + 8)
                    for s in range(4):
                        mm = nc.tensor.matmul(ps[:, x, s * NK:(s + 1) * NK], stage[:, x, s, 0, :],
                                              stage[:, x, s, 1, :], start=True, stop=True)
                    mm.then_inc(pG[L], 1)
            body(0, True)
            with pe.Fori(1, T // 8) as i:
                body(i, False)

        def peer_v_pe(pe, L):
            n0 = FIRST[f"v{L}"]
            pe.wait_ge(pmul[L], T // 4)

            def body(i, first):
                for k in range(RING):
                    pe.wait_ge(loaded[k], i * 16 + 16 * (n0 // RING + 1))
                    for c in range(KC):
                        for bank, col, t0, w in ACC[c]:
                            mm = nc.tensor.matmul(
                                ps[:, bank, col:col + w], ring[:, k, c * P:(c + 1) * P],
                                act3[:, ds(i * RING + k, 1), t0:t0 + w].rearrange("p o t -> p (o t)"),
                                start=(first and k == 0 and c < 6), stop=False, skip_group_check=True)
                    mm.then_inc(used, 1)
            body(0, True)
            with pe.Fori(1, NK // RING) as i:
                body(i, False)

        def peer_x_dve(v, L):
            v.wait_ge(used, FIRST[f"v{L}"] + NK)
            for c in range(KC):
                for bank, col, t0, w in ACC[c]:
                    nc.vector.tensor_tensor(xT[:, c, t0:t0 + w], xT[:, c, t0:t0 + w], ps[:, bank, col:col + w],
                                            ALU.add).then_inc(pacc[L], 1)
            v.wait_ge(pacc[L], 10)
            v.sem_inc(x_ready, 1)

        U = KC * T

        def unit(k):
            return bg(U * k, U)

        def h3(a):
            return a.rearrange("p (h t) -> p h t", h=HH)

        Bc, K_, Q_, VT, GS, QM, QI, KM, KD, D1 = (unit(k) for k in range(10))
        CU = bg(U * 10, U)
        vtok = [bg(1024 * j, 1024) for j in range(3)]
        ktok = [bg(3072 + 1024 * j, 1024) for j in range(3)]
        sall = [bg(U * 10 + 1024 * c, 1024).rearrange("p (h v) -> p h v", h=HH) for c in range(NCH)]
        ss = bg(U * 10 + 4096, 8192).rearrange("p (h b v) -> p h b v", h=HH, b=NB)
        smask = bg(U * 10 + 4096 + 8192, TS)
        bmask = bg(U * 10 + 4096 + 8192 + TS, NB)
        pmask = bg(U * 10 + 4096 + 8192 + TS + NB, P)
        pp = [bg(U * 9 + 1024 * j, 1024 if j < 2 else 256).rearrange("p (h t) -> p h t", h=HH) for j in range(3)]
        vb = [bg(U * 8 + 1024 * k, 1024).rearrange("p (b v) -> p b v", b=NB) for k in range(2)]
        O_ = unit(3)
        SQ = unit(7)
        RS = unit(5)
        carry = sb("carry", [P, T])
        lbr = sb("lbr", [P, 2, KC])
        lb, oml = (small[:, 8 * k:8 * k + 8] for k in range(2))
        lt = [small[:, 16 + 8 * k:24 + 8 * k] for k in range(4)]
        dec = small[:, 64:64 + 12 * HH].rearrange("p (h c) -> p h c", h=HH)
        nwv = sb("nwv", [P, 1])

        hg_in = sem("hg_in")
        hg_s0 = sem("hg_s0")
        hg_lbm = sem("hg_lbm")
        hg_lbe = sem("hg_lbe")
        hg_mask = sem("hg_mask")
        hg_ev = sem("hg_evac")
        hg_f = sem("hg_f")
        hg_log = sem("hg_log")
        hg_cum = sem("hg_cum")
        hg_d = sem("hg_d")
        hg_e = sem("hg_e")
        hg_m = sem("hg_m")
        hg_tv = sem("hg_tv")
        hg_tk = sem("hg_tk")
        hg_tvc = sem("hg_tvc")
        hg_tkc = sem("hg_tkc")
        hg_z = sem("hg_z")
        hg_s = sem("hg_s")
        hg_p = sem("hg_p")
        hg_kv = sem("hg_kv")
        hg_S = sem("hg_S")
        hg_o = sem("hg_o")
        hg_oc = sem("hg_oc")
        hg_vb = sem("hg_vb")
        hg_kvs = sem("hg_kvs")
        hg_Ss = sem("hg_Ss")
        hg_sq = sem("hg_sq")
        hg_ssq = sem("hg_ssq")
        hg_rs = sem("hg_rs")
        hg_h = sem("hg_h")
        hg_x = sem("hg_x")

        def hg_masks_pool(g):
            g.wait_ge(x_ready, 3)
            step = [0]

            def L_(ins):
                ins.then_inc(hg_mask, 1)
                step[0] += 1
                g.wait_ge(hg_mask, step[0])
            for m in (pmask, smask, bmask):
                L_(nc.gpsimd.memset(m, 1.0))
            L_(nc.gpsimd.affine_select(out=pmask, in_=pmask, pattern=[[1, P]], base=0, channel_multiplier=-1,
                                       compare_op=ALU.is_ge, fill=0.0))
            L_(nc.gpsimd.memset(pmask[0:CH, CH:P], 0.0))
            s2 = smask[0:TS, :].rearrange("p (b i) -> p b i", b=NB)
            L_(nc.gpsimd.affine_select(out=s2, in_=s2, pattern=[[LS, NB], [1, LS]], base=0, channel_multiplier=-1,
                                       compare_op=ALU.is_ge, fill=0.0))
            for m, pat in ((s2, [[-LS, NB], [0, LS]]), (bmask[0:TS, :], [[-LS, NB]])):
                L_(nc.gpsimd.affine_select(out=m, in_=m, pattern=pat, base=0, channel_multiplier=1,
                                           compare_op=ALU.is_ge, fill=0.0))
                L_(nc.gpsimd.affine_select(out=m, in_=m, pattern=[[-a, n] for a, n in pat], base=LS - 1,
                                           channel_multiplier=-1, compare_op=ALU.is_ge, fill=0.0))
        N_MASK = 10

        def hg_lb_dve(v, cnt):
            vv = nc.vector
            v.wait_ge(hg_in, 32)
            cnt.link(vv.tensor_tensor(lt[0], lbr[:, 0, :], lbr[:, 1, :], ALU.max))
            vv.tensor_tensor(lt[1], lbr[:, 0, :], lt[0], ALU.subtract).then_inc(hg_lbm, 1)
            vv.tensor_tensor(lt[2], lbr[:, 1, :], lt[0], ALU.subtract).then_inc(hg_lbm, 1)
            v.wait_ge(hg_lbe, 2)
            cnt.link(vv.tensor_tensor(lt[3], lt[1], lt[2], ALU.add))
            cnt.link(vv.reciprocal(lt[0], lt[3]))
            cnt.add(vv.tensor_tensor(lt[1], lt[1], lt[0], ALU.mult))
            cnt.link(vv.tensor_tensor(lt[2], lt[2], lt[0], ALU.mult))
            cnt.link(vv.tensor_tensor(lt[3], lt[1], lt[2], ALU.add))
            cnt.link(vv.tensor_tensor(lb, lt[3], lt[1], ALU.subtract))
            cnt.link(vv.tensor_scalar(oml, lb, -1.0, 1.0, ALU.mult, ALU.add))
            cnt.add(vv.memset(carry[:, :], 1.0))
            cnt.wait()
            cnt.add(vv.memset(carry[:, 0:TP:CH], 0.0))
            cnt.link(vv.memset(carry[:, TP:T:LS], 0.0))

        def hg_lb_act(act):
            act.wait_ge(hg_lbm, 2)
            for k in (1, 2):
                nc.scalar.activation(lt[k], lt[k], ACT.Exp).then_inc(hg_lbe, 1)

        def hg_in_pe(pe):
            pe.wait_ge(norm_h, 3 * KC)
            project(pe, "win", lambda i, k: pe.wait_ge(hg_ev, i * 4 + k - 3), lambda i, k: None)

        def hg_evac_act(act, part, fns):
            n0 = FIRST["win"] + 8 * part
            with act.Fori(0, 2) as i:
                for k in range(4):
                    act.wait_ge(used, i * 4 + (n0 + k + 1))
                    for dst, fn, scale in fns:
                        ins = nc.scalar.activation(h3(dst)[:, ds(i * 4 + k, 1), :].rearrange("p o t -> p (o t)"),
                                                   zbank(k), fn, scale=scale)
                    ins.then_inc(hg_ev, 1)

        def hg_act(act):
            act.wait_ge(x_ready, 3)
            hg_evac_act(act, 0, [(Bc, ACT.Sigmoid, 1.0), (K_, ACT.Sigmoid, -1.0)])
            act.wait_ge(hg_f, 1)
            nc.scalar.activation(Bc, Bc, ACT.Ln).then_inc(hg_log, 1)
            hg_evac_act(act, 1, [(Q_, ACT.Silu, 1.0)])
            act.wait_ge(hg_cum, 8)
            nc.scalar.activation(QI, CU, ACT.Exp).then_inc(hg_e, 1)
            act.wait_ge(hg_d, 2)
            nc.scalar.activation(QM, D1, ACT.Exp).then_inc(hg_e, 1)
            nc.scalar.activation(KM, D1, ACT.Exp, scale=-1.0).then_inc(hg_e, 1)
            act.wait_ge(hg_d, 4)
            nc.scalar.activation(KD, Bc, ACT.Exp).then_inc(hg_e, 1)
            hg_evac_act(act, 2, [(VT, ACT.Copy, 1.0)])
            hg_evac_act(act, 3, [(GS, ACT.Silu, 1.0)])
            for j, (_, w) in enumerate(TILES):
                act.wait_ge(hg_tv, j + 1)
                if j == 0:
                    act.wait_ge(hg_m, 4)
                nc.scalar.activation(vtok[j][0:w, :], ps[0:w, 0:2, :].rearrange("p b n -> p (b n)"),
                                     ACT.Copy).then_inc(hg_tvc, 1)
            act.wait_ge(hg_tv, 3)
            for h in range(HH):
                act.wait_ge(hg_o, h + 1)
                nc.scalar.activation(h3(O_)[:, h, :], ps[:, 6 + h % 2, 0:T], ACT.Copy).then_inc(hg_oc, 1)
            act.wait_ge(hg_oc, 8)
            nc.scalar.activation(SQ, O_, ACT.Square).then_inc(hg_sq, 1)
            for h in range(HH):
                act.wait_ge(hg_ssq, h + 1)
                nc.scalar.activation(h3(RS)[:, h, :], ps[:, 2 + h % 2, 0:T], ACT.Sqrt, bias=epsc[:, 0:1],
                                     scale=1.0 / P).then_inc(hg_rs, 1)

        def hg_dve(v, cnt):
            vv = nc.vector
            tt = vv.tensor_tensor
            v.wait_ge(hg_ev, 8)
            for h in range(HH):
                cnt.add(vv.tensor_scalar(h3(Bc)[:, h, :], h3(Bc)[:, h, :], oml[:, h:h + 1], lb[:, h:h + 1],
                                         ALU.mult, ALU.add))
            cnt.wait()
            vv.tensor_scalar(Bc, Bc, F_LEAST, None, ALU.max).then_inc(hg_f, 1)
            cnt.link(tt(h3(K_), h3(K_), oml[:, :, None].to_broadcast([P, HH, T]), ALU.mult))
            v.wait_ge(hg_log, 1)
            for h in range(HH):
                vv.tensor_tensor_scan(h3(CU)[:, h, :], carry[:, :], h3(Bc)[:, h, :], 0.0, ALU.mult,
                                      ALU.add).then_inc(hg_cum, 1)
            v.wait_ge(hg_cum, 8)

            def parts(a):
                p = h3(a)[:, :, 0:TP].rearrange("p h (c t) -> p h c t", c=NCH)
                s = h3(a)[:, :, TP:T].rearrange("p h (c t) -> p h c t", c=NB)
                return (p, NCH, CH), (s, NB, LS)
            for (b_, n, c), (d_, _, _) in zip(parts(CU), parts(D1)):
                tt(d_, b_, b_[:, :, :, c // 2:c // 2 + 1].to_broadcast([P, HH, n, c]), ALU.subtract).then_inc(hg_d, 1)
            for (b_, n, c), (d_, _, _) in zip(parts(CU), parts(Bc)):
                tt(d_, b_[:, :, :, c - 1:c].to_broadcast([P, HH, n, c]), b_, ALU.subtract).then_inc(hg_d, 1)
            v.wait_ge(hg_e, 1)
            cnt.add(vv.tensor_copy(dec[:, :, 0:NCH], h3(QI)[:, :, CH - 1:TP:CH]))
            cnt.link(vv.tensor_copy(dec[:, :, NCH:12], h3(QI)[:, :, TP + LS - 1:T:LS]))
            v.wait_ge(hg_e, 4)
            v.wait_ge(hg_ev, 16)
            for dst, src in ((QI, Q_), (QM, Q_), (KM, K_), (KD, K_)):
                tt(dst, dst, src, ALU.mult).then_inc(hg_m, 1)
            v.wait_ge(hg_e, 4)
            for j in range(3):
                vv.memset(pp[j], 0.0).then_inc(hg_z, 1)
            for j, (_, w) in enumerate(TILES):
                v.wait_ge(hg_tk, j + 1)
                if j == 0:
                    v.wait_ge(hg_m, 4)
                vv.tensor_copy(ktok[j][0:w, :], ps[0:w, 2:4, :].rearrange("p b n -> p (b n)")).then_inc(hg_tkc, 1)
            v.wait_ge(hg_mask, N_MASK)
            v.wait_ge(hg_z, 3)
            for j, (_, w) in enumerate(TILES):
                v.wait_ge(hg_s, j + 1)
                m = (pmask if w == P else smask)[0:w, None, 0:w].to_broadcast([w, 4, w]).bitcast(I32)
                for half in range(2):
                    bank = 4 + 2 * (j % 2) + half
                    vv.copy_predicated(pp[j][0:w, 4 * half:4 * half + 4, :], m,
                                       ps[0:w, bank, 0:4 * w].rearrange("p (h t) -> p h t", h=4)).then_inc(hg_p, 1)
            for c in range(NCH):
                kv = ps[:, 2 * (c % 2):2 * (c % 2) + 2, :].rearrange("p b (h v) -> p (b h) v", h=4)
                v.wait_ge(hg_kv, c + 1)
                if c == 0:
                    vv.tensor_copy(sall[0], kv).then_inc(hg_S, 1)
                else:
                    v.wait_ge(hg_S, c)
                    cnt.link(tt(sall[c], sall[c - 1], dec[:, :, c:c + 1].to_broadcast([P, HH, P]), ALU.mult))
                    tt(sall[c], sall[c], kv, ALU.add).then_inc(hg_S, 1)
            v.wait_ge(hg_tvc, 3)
            v.wait_ge(hg_s0, 16)
            v.wait_ge(hg_tk, 3)
            for h in range(HH):
                if h >= 2:
                    v.wait_ge(hg_kvs, h - 1)
                sh = [TS, NB, P]
                tt(vb[h % 2][0:TS], vtok[2][0:TS, None, h * P:(h + 1) * P].to_broadcast(sh),
                   bmask[0:TS, :, None].to_broadcast(sh), ALU.mult).then_inc(hg_vb, 1)
                v.wait_ge(hg_o, h + 1)
                cnt.link(tt(ss[:, h], ss[:, h], dec[:, h, NCH:12, None].to_broadcast([P, NB, P]), ALU.mult))
                v.wait_ge(hg_kvs, h + 1)
                b0 = 4 * (h % 2)
                tt(ss[:, h], ss[:, h], ps[:, b0:b0 + 2, :].rearrange("p b (c v) -> p (b c) v", c=4),
                   ALU.add).then_inc(hg_Ss, 1)
            v.wait_ge(hg_rs, 8)
            cnt.link(vv.reciprocal(RS, RS))
            cnt.link(tt(O_, O_, RS, ALU.mult))
            vv.scalar_tensor_tensor(out=hT[:, :, :].rearrange("p c t -> p (c t)"), in0=O_, scalar=nwv[:, 0:1],
                                    in1=GS, op0=ALU.mult, op1=ALU.mult).then_inc(hg_h, 1)

            def body(i):
                for k in range(4):
                    v.wait_ge(used, i * 4 + (FIRST["wout"] + k + 1))
                    x = xT[:, ds(i * 4 + k, 1), :].rearrange("p o t -> p (o t)")
                    tt(x, x, zbank(k), ALU.add).then_inc(hg_x, 1)
            with v.Fori(0, 2) as i:
                body(i)
            v.wait_ge(hg_x, 8)
            v.sem_inc(x_ready, 1)

        def hg_pe(pe):
            mm_, tr = nc.tensor.matmul, nc.tensor.transpose
            pe.wait_ge(hg_ev, 32)
            pe.wait_ge(hg_m, 4)
            for j, (t0, w) in enumerate(TILES):
                if j:
                    pe.wait_ge(hg_tvc, j)
                for h in range(HH):
                    mm = tr(ps[0:w, h // 4, (h % 4) * P:(h % 4 + 1) * P], h3(VT)[:, h, t0:t0 + w], ident[:, :])
                mm.then_inc(hg_tv, 1)
                if j:
                    pe.wait_ge(hg_tkc, j)
                for h in range(HH):
                    mm = tr(ps[0:w, 2 + h // 4, (h % 4) * P:(h % 4 + 1) * P], h3(KD)[:, h, t0:t0 + w], ident[:, :])
                mm.then_inc(hg_tk, 1)
            for j, (t0, w) in enumerate(TILES):
                if j == 2:
                    pe.wait_ge(hg_p, 2)
                for h in range(HH):
                    mm = mm_(ps[0:w, 4 + 2 * (j % 2) + h // 4, (h % 4) * w:(h % 4 + 1) * w],
                             h3(KM)[:, h, t0:t0 + w], h3(QM)[:, h, t0:t0 + w], start=True, stop=True)
                mm.then_inc(hg_s, 1)
            pe.wait_ge(hg_tvc, 3)
            pe.wait_ge(hg_tkc, 3)
            for c in range(NCH):
                if c >= 2:
                    pe.wait_ge(hg_S, c - 1)
                j, r0 = c // 2, CH * (c % 2)
                for h in range(HH):
                    mm = mm_(ps[:, 2 * (c % 2) + h // 4, (h % 4) * P:(h % 4 + 1) * P],
                             ktok[j][r0:r0 + CH, h * P:(h + 1) * P], vtok[j][r0:r0 + CH, h * P:(h + 1) * P],
                             start=True, stop=True)
                mm.then_inc(hg_kv, 1)
            pe.wait_ge(hg_p, 6)
            pe.wait_ge(hg_S, 3)
            pe.wait_ge(hg_s0, 16)
            for h in range(HH):
                if h >= 2:
                    pe.wait_ge(hg_oc, h - 1)
                bank = 6 + h % 2
                for j, (t0, w) in enumerate(TILES):
                    mm = mm_(ps[:, bank, t0:t0 + w], vtok[j][0:w, h * P:(h + 1) * P], pp[j][0:w, h, :],
                             start=True, stop=False, skip_group_check=True)
                    if w == P:
                        for c in range(2 * j, 2 * j + 2):
                            if c:
                                a = c * CH
                                mm = mm_(ps[:, bank, a:a + CH], sall[c - 1][:, h, :], h3(QI)[:, h, a:a + CH],
                                         start=False, stop=False, skip_group_check=True)
                    else:
                        for b in range(NB):
                            a = TP + b * LS
                            mm = mm_(ps[:, bank, a:a + LS], ss[:, h, b, :], h3(QI)[:, h, a:a + LS],
                                     start=False, stop=False, skip_group_check=True)
                mm.then_inc(hg_o, 1)
            pe.wait_ge(hg_S, 4)
            for h in range(HH):
                if h >= 2:
                    pe.wait_ge(hg_Ss, h - 1)
                pe.wait_ge(hg_vb, h + 1)
                b0 = 4 * (h % 2)
                for half in range(2):
                    mm = mm_(ps[:, b0 + half, :], ktok[2][0:TS, h * P:(h + 1) * P],
                             vb[h % 2][0:TS, 4 * half:4 * half + 4, :].rearrange("p b v -> p (b v)"),
                             start=True, stop=True)
                mm.then_inc(hg_kvs, 1)
            pe.wait_ge(hg_sq, 1)
            for h in range(HH):
                if h >= 2:
                    pe.wait_ge(hg_rs, h - 1)
                mm_(ps[:, 2 + h % 2, 0:T], ones[:, :], h3(SQ)[:, h, :], start=True, stop=True).then_inc(hg_ssq, 1)
            pe.wait_ge(hg_h, 1)
            pe.wait_ge(hg_Ss, 8)
            pe.wait_ge(hg_oc, 8)
            project(pe, "wout", lambda i, k: pe.wait_ge(hg_x, i * 4 + k - 3), lambda i, k: None)

        SQ5, SQP = TMPW, 0

        @block.sync
        def _(sp):
            sp.dma_start(xT[:, :, :], t_in["xT"]).then_inc(s_x, 16)
            sp.dma_start(normw[:, :, :], t_in["normw"]).then_inc(s_par, 16)
            for k, n in enumerate(("lam_re", "lam_im", "log_dt")):
                sp.dma_start(par[:, k, :], t_in[n]).then_inc(s5_in, 16)
            sp.dma_start(s5w[:, :, :], t_in["s5b"]).then_inc(s5_in, 16)
            sp.dma_start(craw, t_in["s5c"]).then_inc(s5_in, 16)
            sp.dma_start(dcol[:, :], t_in["s5d"]).then_inc(s5_in, 16)
            sp.dma_start(keysT[:, :, :, :], t_in["keysT"]).then_inc(s_keys, 16)
            sp.dma_start(lbr[:, :, :], t_in["lbr"]).then_inc(hg_in, 16)
            sp.dma_start(nwv[:, :], t_in["hgnw"]).then_inc(hg_in, 16)
            stream_segment(sp, "glu")
            for n in ("wq0", "u0", "v0", "win", "wout", "wq1", "u1", "v1"):
                stream_segment(sp, n)
            sp.wait_ge(norm_h, 5 * KC)
            sp.dma_start(t_out["y"], hT[:, :, :]).then_inc(out_y, 16)
            sp.wait_ge(out_y, 16)

        @block.gpsimd
        def _(g):
            n = [0]

            def L_(ins):
                ins.then_inc(s_const, 1)
                n[0] += 1
                g.wait_ge(s_const, n[0])
            L_(nc.gpsimd.memset(ident[:, :], 0.0))
            L_(nc.gpsimd.affine_select(out=ident[:, :], in_=ident[:, :], compare_op=ALU.not_equal, fill=1.0,
                                       base=0, pattern=[[-1, P]], channel_multiplier=1))
            L_(nc.gpsimd.memset(ones[:, :], 1.0))
            L_(nc.gpsimd.memset(epsc[:, :], EPS))
            L_(nc.gpsimd.iota(iota[:, :], pattern=[[1, P]], base=0, channel_multiplier=0,
                              allow_small_or_imprecise_dtypes=True))
            L_(nc.gpsimd.iota(iota_c[:, :], pattern=[[1, NC_]], base=0, channel_multiplier=0,
                              allow_small_or_imprecise_dtypes=True))
            s5_table_pool(g)
            g.dma_start(s0.rearrange("p r q b -> p (r q b)"), t_in["s5s0"]).then_inc(s5_s0, 16)
            s5_in_pool(g)
            g.wait_ge(s5_fin, 4)
            g.dma_start(t_out["s5f"], fin5.rearrange("p r q b -> p (r q b)")).then_inc(out_s5, 16)
            g.wait_ge(x_ready, 3)
            g.dma_start(ss.rearrange("p h b v -> p (h b v)"), t_in["hgs0"]).then_inc(hg_s0, 16)
            hg_masks_pool(g)
            g.wait_ge(hg_S, 4)
            g.dma_start(t_out["hgp"], sall[3].rearrange("p h v -> p (h v)")).then_inc(out_hgp, 16)
            g.wait_ge(hg_Ss, 8)
            g.dma_start(t_out["hgs"], ss.rearrange("p h b v -> p (h b v)")).then_inc(out_hgs, 16)
            g.wait_ge(out_s5, 16)
            g.wait_ge(out_hgp, 16)
            g.wait_ge(out_hgs, 16)

        @block.tensor
        def _(pe):
            pe.wait_ge(s_const, 6)
            norm_pe(pe, 0, SQ5)
            s5_in_pe(pe)
            s5_out_pe(pe)
            glu_pe(pe)
            for L in range(2):
                norm_pe(pe, 2 * L + 1, SQP)
                peer_query_pe(pe, L)
                peer_u_pe(pe, L, *SPLITS[0])
                peer_u_pe(pe, L, *SPLITS[1])
                peer_tr_pe(pe, L)
                peer_u_pe(pe, L, *SPLITS[2])
                peer_g_pe(pe, L)
                peer_v_pe(pe, L)
                norm_pe(pe, 2 * L + 2, SQP)
                if L == 0:
                    hg_in_pe(pe)
                    hg_pe(pe)

        @block.scalar
        def _(act):
            act.wait_ge(s_const, 6)
            act.wait_ge(s_x, 16)
            norm_act(act, 0, SQ5)
            s5_params_act(act)
            s5_in_act(act)
            s5_out_act(act)
            glu_act(act)
            for L in range(2):
                norm_act(act, 2 * L + 1, SQP)
                peer_query_act(act, L)
                peer_u_act(act, L, *SPLITS[0])
                peer_exp_act(act, L)
                peer_u_act(act, L, *SPLITS[1])
                peer_u_act(act, L, *SPLITS[2])
                norm_act(act, 2 * L + 2, SQP)
                if L == 0:
                    hg_lb_act(act)
                    hg_act(act)

        @block.vector
        def _(v):
            cnt = Count(v, dv)
            v.wait_ge(s_x, 16)
            v.wait_ge(s_par, 16)
            v.wait_ge(s_const, 6)
            v.sem_inc(x_ready, 1)
            norm_dve(v, cnt, 0)
            s5_params_dve(v, cnt)
            s5_table_dve(v, cnt)
            s5_in_dve(v)
            s5_samples_dve(v, cnt)
            s5_out_dve(v)
            glu_dve(v)
            for L in range(2):
                norm_dve(v, cnt, 2 * L + 1)
                peer_topk_dve(v, cnt, L)
                peer_pairs_dve(v, cnt, L)
                peer_g_dve(v, L)
                peer_x_dve(v, L)
                norm_dve(v, cnt, 2 * L + 2)
                if L == 0:
                    hg_lb_dve(v, cnt)
                    hg_dve(v, cnt)


def host_layout(i):
    f = {k: np.ascontiguousarray(np.asarray(v)) for k, v in i.items()}
    c = np.ascontiguousarray

    def cols(w):
        n = w.shape[1] // P
        return w.reshape(KC, P, n, P).transpose(2, 1, 0, 3).reshape(n, P, BLK)

    def vec(a):
        return np.moveaxis(a.reshape(a.shape[:-1] + (KC, P)), -1, 0)

    def states(a):
        b = a.reshape((PAIRS, 2, 64) + a.shape[2:])
        return np.moveaxis(b, 0, 2).reshape((P, PAIRS) + a.shape[2:])

    x = np.concatenate([f["x_prompt"].reshape(TP, D), f["x_sample"].reshape(TS, D)])
    glu = cols(f["s5_w_glu"][0])
    win = cols(f["hg_w_in"][0])
    r = {
        "xT": c(x.reshape(T, KC, P).transpose(2, 1, 0)),
        "normw": c(vec(np.stack([f["norm_mix"][0], f["norm_ffn"][0], f["norm_mix"][1], f["norm_ffn"][1],
                                 f["norm_final"]]))),
        "lam_re": c(states(f["s5_lambda_re"][0])),
        "lam_im": c(states(f["s5_lambda_im"][0])),
        "log_dt": c(states(np.repeat(f["s5_log_dt"][0][:, None], 64, axis=1))),
        "s5b": c(np.stack([states(f[n][0]) for n in ("s5_b_re", "s5_b_im")], 1).reshape(P, 2, PAIRS * GH)),
        "s5c": c(np.stack([states(f[n][0].transpose(0, 2, 1)) for n in ("s5_c_re", "s5_c_im")], 1)
                 .reshape(P, 2, PAIRS * GH)),
        "s5d": c(vec(f["s5_d"][0])),
        "s5s0": c(np.stack([states(f[n][0].transpose(1, 2, 0)) for n in ("state_s5_re", "state_s5_im")], 1)
                  .reshape(P, 2 * PAIRS * NB)),
        "keysT": c(np.stack([np.stack([f["peer_keys1"][l].T, f["peer_keys2"][l].T], 1) for l in range(2)], 1)),
        "lbr": c(vec(f["hg_lower_bounds"])),
        "hgnw": c(f["hg_norm_w"][0][:, None]),
        "hgs0": c(f["state_hgrn"][0].transpose(2, 1, 0, 3).reshape(P, HH * NB * P)),
        "glu": c(glu.reshape(2, KC, P, BLK).transpose(1, 0, 2, 3).reshape(16, P, BLK)),
        "win": c(np.concatenate([win[8:16], win[0:8], win[16:24], win[24:32]])),
        "wout": c(cols(f["hg_w_out"][0])),
    }
    for l in range(2):
        r[f"wq{l}"] = c(cols(f["peer_w_q"][l]))
        r[f"u{l}"] = c(f["peer_u"][l].reshape(NK, NK, KC, P).transpose(1, 3, 2, 0).reshape(NK, P, BLK))
        r[f"v{l}"] = c(f["peer_v"][l].reshape(NK, NK, D).transpose(1, 0, 2))
    return r


OUTS = {"y": (P, KC, T), "s5f": (P, 2 * PAIRS * 9), "hgp": (P, HH * P), "hgs": (P, HH * NB * P)}


def kernel(**inputs):
    import concourse.bacc as bacc
    from concourse.bass_utils import run_bass_kernel_spmd

    nc = bacc.Bacc("TRN2", target_bir_lowering=False, num_devices=1)
    arrays = host_layout(inputs)
    t_in = {k: nc.dram_tensor("in_" + k, a.shape, mybir.dt.from_np(a.dtype), kind="ExternalInput").ap()
            for k, a in arrays.items()}
    t_out = {k: nc.dram_tensor("out_" + k, s, F32, kind="ExternalOutput").ap() for k, s in OUTS.items()}
    build(nc, t_in, t_out)
    r = run_bass_kernel_spmd(nc, [{"in_" + k: a for k, a in arrays.items()}], core_ids=[0]).results[0]
    y = r["out_y"].transpose(2, 1, 0).reshape(T, D)
    s5 = r["out_s5f"].reshape(2, 64, 2, PAIRS, 9).transpose(2, 4, 3, 0, 1).reshape(2, 1, 9, 2 * PAIRS, 64)
    hgp = r["out_hgp"].reshape(P, HH, P).transpose(1, 0, 2).reshape(1, 1, HH, P, P)
    hgs = r["out_hgs"].reshape(P, HH, NB, P).transpose(2, 1, 0, 3).reshape(1, NB, HH, P, P)
    return (y[:TP].reshape(1, TP, D), y[TP:].reshape(NB, LS, D),
            s5[0, :, 0:1], s5[1, :, 0:1], hgp, s5[0, :, 1:], s5[1, :, 1:], hgs)
```

```python
from contextlib import ExitStack

import numpy as np
import concourse.bass as bass
from concourse import mybir

F32 = mybir.dt.float32
F16 = mybir.dt.float16
I32 = mybir.dt.int32
U32 = mybir.dt.uint32
ACT = mybir.ActivationFunctionType
ALU = mybir.AluOpType
AX = mybir.AxisListType
ds = bass.ds

P = 128
D = 1024
KC = D // P
TP, NB, LS = 256, 8, 4
TS = NB * LS
T = TP + TS
TILES = [(0, P), (P, P), (2 * P, TS)]

PAIRS = 32
GH = 16
QC = 4
HH = 8
CH = 64
NCH = TP // CH
PH, NK, TK = 8, 128, 16
RECTS = [(0, 1, 16), (1, 1, 8), (2, 2, 5), (4, 4, 3), (8, 8, 1)]
NC_ = sum(r * c for _, r, c in RECTS)

GT = 8
RING = 4
BLK = KC * P
EPS = 1e-6
F_LEAST = 2.0 ** -64
LOWEST = -3.0e38

SC = 16.0
UNSC = 1.0 / (SC * SC)

UA, UB = 72, 96
SEGMENTS = [("glu", 16), ("wq0", 16), ("ua0", UA), ("ub0", NK - UA), ("v0", NK), ("win", 32), ("wout", 8),
            ("wq1", 16), ("ua1", UA), ("ub1", NK - UA), ("v1", NK)]
FIRST, _n = {}, 0
for _name, _c in SEGMENTS:
    FIRST[_name] = _n
    _n += _c

BY_POOL = {"wq0", "ua0", "wq1", "ua1", "win"}
LO_FIRST, _c2 = {}, {True: 0, False: 0}
for _name, _c in SEGMENTS:
    LO_FIRST[_name] = _c2[_name in BY_POOL]
    _c2[_name in BY_POOL] += _c
N_BLOCKS = dict(SEGMENTS)

ACC = [[(c, 0, 0, T)] for c in range(6)] + \
      [[(0, T, 0, 512 - T), (1, T, 512 - T, 2 * T - 512)], [(2, T, 0, 512 - T), (3, T, 512 - T, 2 * T - 512)]]


class Count:

    def __init__(self, eng, sem):
        self.eng, self.sem, self.n, self.loop = eng, sem, 0, None

    def add(self, ins):
        ins.then_inc(self.sem, 1)
        self.n += 1
        return self.n

    def wait(self, n=None):
        v = self.n if n is None else n
        self.eng.wait_ge(self.sem, v if self.loop is None else v + self.loop)

    def link(self, ins):
        self.add(ins)
        self.wait()

    def enter(self, i, first, per):
        self.start, self.per, self.loop = self.n, per, (i - first) * per

    def leave(self, trips):
        assert self.n - self.start == self.per, (self.n - self.start, self.per)
        self.n, self.loop = self.start + trips * self.per, None


def build(nc, t_in, t_out):
    with ExitStack() as ctx:
        def sb(name, shape, dt=F32):
            return ctx.enter_context(nc.sbuf_tensor(name, shape, dt))

        def sem(name):
            return ctx.enter_context(nc.semaphore(name))

        big = sb("big", [P, NK * T])
        xT = sb("xT", [P, KC, T])
        hT = sb("hT", [P, KC, T])
        hs = sb("hs", [P, 2, KC, T], F16)
        ring = sb("ring", [P, RING, BLK])
        wsp = sb("wsp", [P, 2, 2, BLK], F16)
        ident = sb("ident", [P, P])
        ident_h = sb("ident_h", [P, P], F16)
        ones = sb("ones", [P, P])
        iota_r = sb("iota_r", [P, NK, GT], F16)
        iota_c = sb("iota_c", [P, NC_])
        epsc = sb("epsc", [P, 1])
        normw = sb("normw", [P, 5, KC])
        std = sb("std", [P, T])
        keysT = sb("keysT", [P, 2, 2, NK])
        hT_half = hT[:, :, :].rearrange("p c t -> p (c t)").bitcast(F16)
        neg_i1T, i2T, gate_hi, gate_lo = (hT_half[:, T * k:T * k + T] for k in range(4))
        asp = hT[:, 3:5, :].rearrange("p a t -> p (a t)").bitcast(F16).rearrange("p (s f t) -> p s f t", s=2, f=2)
        qbuf = [hT[:, 6 + k, :] for k in range(2)]
        hs_half = hs[:, :, :, :].rearrange("p f c t -> p (f c t)")

        def spread_buffer(k):
            n = NK * GT
            flat = (hs_half[:, n * k:n * k + n] if k < 4 else
                    hT_half[:, 4 * T + n * (k - 4):4 * T + n * (k - 4) + n])
            return flat.rearrange("p (j t) -> p j t", t=GT)
        hot1 = [spread_buffer(k) for k in range(2)]
        hot2g = [[spread_buffer(2 + 2 * k + f) for f in range(2)] for k in range(2)]
        hot2 = spread_buffer(6)
        small = sb("small", [P, 256])
        ps = ctx.enter_context(nc.psum_tensor("ps", [P, 8, 512], F32))

        def bg(off, n):
            return big[:, off:off + n]

        loaded = [sem(f"loaded{k}") for k in range(RING)]
        scaled = sem("scaled")
        hi_ready = sem("hi_ready")
        lo_dve = sem("lo_dve")
        lo_pool = sem("lo_pool")
        used = sem("used")
        hs_hi = sem("hs_hi")
        hs_lo = sem("hs_lo")
        s_const = sem("s_const")
        s_x = sem("s_x")
        s_par = sem("s_par")
        s_keys = sem("s_keys")
        out_y = sem("out_y")
        out_s5 = sem("out_s5")
        out_hgp = sem("out_hgp")
        out_hgs = sem("out_hgs")
        dv = sem("dv")
        x_ready = sem("x_ready")
        norm_sq = sem("norm_sq")
        norm_ss = sem("norm_ss")
        norm_std = sem("norm_std")
        norm_h = sem("norm_h")

        block = ctx.enter_context(nc.Block())

        def zbank(k):
            return ps[:, 4 + k, 0:T]

        def lo_done(eng, name, i, k):
            lo_half_done(eng, name, i, k, 1)

        def lo_half_done(eng, name, i, k, h):
            eng.wait_ge(lo_pool if name in BY_POOL else lo_dve, i * 2 * RING + (2 * (LO_FIRST[name] + k) + h + 1))

        def block_used(eng, name, i, k):
            eng.wait_ge(used, i * 2 * RING + 2 * (FIRST[name] + k + 1))

        def stream_segment(sp, name, before):
            src, trips = t_in[name], N_BLOCKS[name] // RING

            def load(i, k):
                sp.dma_start(ring[:, k, :], src[i * RING + k]).then_inc(loaded[k], 16)
            for k in range(RING):
                if before:
                    lo_done(sp, before, N_BLOCKS[before] // RING - 1, k)
                load(0, k)
            with sp.Fori(1, trips) as i:
                for k in range(RING):
                    lo_done(sp, name, i - 1, k)
                    load(i, k)

        HALF = BLK // 2

        def split_hi(act, name, i, k):
            i, k = (i, k) if k < RING else (i + 1, k - RING)
            n0 = FIRST[name]
            act.wait_ge(loaded[k], i * 16 + 16 * (n0 // RING + 1))
            scale = SC
            if name in BY_POOL:
                nc.scalar.activation(ring[:, k, :], ring[:, k, :], ACT.Copy, scale=SC).then_inc(scaled, 1)
                act.wait_ge(scaled, i * RING + (LO_FIRST[name] + k + 1))
                scale = 1.0
            for h in range(2):
                if not (n0 == 0 and isinstance(i, int) and i == 0 and k < 2):
                    act.wait_ge(used, i * 2 * RING + (2 * (n0 + k) - 3 + h))
                cols = slice(h * HALF, (h + 1) * HALF)
                nc.scalar.activation(wsp[:, k % 2, 0, cols], ring[:, k, cols], ACT.Copy,
                                     scale=scale).then_inc(hi_ready, 1)

        def split_lo(eng, name, i, k):
            i, k = (i, k) if k < RING else (i + 1, k - RING)
            for h in range(2):
                eng.wait_ge(hi_ready, i * 2 * RING + (2 * (FIRST[name] + k) + h + 1))
                cols = slice(h * HALF, (h + 1) * HALF)
                hi, lo, w = wsp[:, k % 2, 0, cols], wsp[:, k % 2, 1, cols], ring[:, k, cols]
                if name in BY_POOL:
                    nc.gpsimd.tensor_tensor(lo, w, hi, ALU.subtract).then_inc(lo_pool, 1)
                else:
                    nc.vector.scalar_tensor_tensor(out=lo, in0=w, scalar=SC, in1=hi, op0=ALU.mult,
                                                   op1=ALU.subtract).then_inc(lo_dve, 1)

        def split_pool(g, name):
            with g.Fori(0, N_BLOCKS[name] // RING) as i:
                for k in range(RING):
                    split_lo(g, name, i, k)

        def per_block(eng, name, split, post, a=0, b=None):
            trips = N_BLOCKS[name] // RING
            b = trips if b is None else b

            def body(i, first, last):
                for k in range(RING):
                    if split and not (last and k >= 2):
                        split(eng, name, i, k + 2)
                    post(i, k, first)
            if split and a == 0:
                split(eng, name, 0, 0)
                split(eng, name, 0, 1)
            if a == 0:
                body(0, True, trips == 1)
                a = 1
            end = b - 1 if b == trips else b
            if a < end:
                with eng.Fori(a, end) as i:
                    body(i, False, False)
            if b == trips and a < b:
                body(trips - 1, False, True)

        def three_passes(out, slot, c, hi, lo, start, stop, **kw):
            w_hi, w_lo = (wsp[:, slot, f, c * P:(c + 1) * P] for f in range(2))
            nc.tensor.matmul(out, w_hi, hi, start=start, stop=False, **kw)
            nc.tensor.matmul(out, w_hi, lo, start=False, stop=False, **kw)
            return nc.tensor.matmul(out, w_lo, hi, start=False, stop=stop, **kw)

        def project(pe, name, wait_bank, after=None, a=0, b=None):
            def post(i, k, first):
                wait_bank(i, k, first)
                for c in range(KC):
                    if c % 4 == 0:
                        lo_half_done(pe, name, i, k, c // 4)
                    mm = three_passes(zbank(k), k % 2, c, hs[:, 0, c, :], hs[:, 1, c, :], c == 0, c == KC - 1)
                    if c % 4 == 3:
                        mm.then_inc(used, 1)
                if after:
                    after(i, k, first)
            per_block(pe, name, None, post, a, b)

        def high_part(c):
            return nc.scalar.activation(hs[:, 0, c, :], hT[:, c, :], ACT.Copy, scale=SC)

        def low_part(c):
            return nc.vector.scalar_tensor_tensor(out=hs[:, 1, c, :], in0=hT[:, c, :], scalar=SC,
                                                  in1=hs[:, 0, c, :], op0=ALU.mult, op1=ALU.subtract)

        def norm_act(act, k, sq_at):
            act.wait_ge(x_ready, k + 1)
            if k == 0:
                act.wait_ge(s_const, 7)
            nc.scalar.activation(bg(sq_at, KC * T), xT[:, :, :].rearrange("p c t -> p (c t)"),
                                 ACT.Square).then_inc(norm_sq, 1)
            act.wait_ge(norm_ss, k + 1)
            nc.scalar.activation(std[:, :], ps[:, 0, 0:T], ACT.Sqrt, bias=epsc[:, 0:1],
                                 scale=1.0 / D).then_inc(norm_std, 1)
            if 0 < k < 4:
                for c in range(KC):
                    act.wait_ge(norm_h, KC * k + c + 1)
                    high_part(c).then_inc(hs_hi, 1)

        def norm_pe(pe, k, sq_at):
            pe.wait_ge(norm_sq, k + 1)
            if k == 0:
                pe.wait_ge(s_const, 7)
            for c in range(KC):
                mm = nc.tensor.matmul(ps[:, 0, 0:T], ones[:, :], bg(sq_at + c * T, T),
                                      start=(c == 0), stop=(c == KC - 1))
            mm.then_inc(norm_ss, 1)

        def norm_dve(v, cnt, k):
            v.wait_ge(norm_std, k + 1)
            cnt.link(nc.vector.reciprocal(std[:, :], std[:, :]))
            for c in range(KC):
                nc.vector.scalar_tensor_tensor(out=hT[:, c, :], in0=xT[:, c, :], scalar=normw[:, k, c:c + 1],
                                               in1=std[:, :], op0=ALU.mult, op1=ALU.mult).then_inc(norm_h, 1)
            if 0 < k < 4:
                before = {1: 1, 2: 2, 3: 4}[k] * KC
                for c in range(KC):
                    v.wait_ge(hs_hi, before + c + 1)
                    low_part(c).then_inc(hs_lo, 1)

        ST = bg(0, 2 * PAIRS * T).rearrange("p (r q t) -> p r q t", r=2, q=PAIRS)
        TMPW = 2 * PAIRS * T
        TAB = [bg(TMPW + 4096 * k, 4096).rearrange("p (q t) -> p q t", q=PAIRS) for k in range(4)]
        bbar = bg(34816, 1024).rearrange("p (r n) -> p r n", r=2)
        craw = bg(35840, 1024).rearrange("p (r n) -> p r n", r=2)
        s5w = hs_half.bitcast(F32)[:, 0:2 * PAIRS * GH].rearrange("p (r n) -> p r n", r=2)
        wdiag = [bg(TMPW + 1280 * k, 1280).rearrange("p (r m) -> p r m", r=2) for k in range(2)]
        btr = [bg(TMPW + 2560 + 1024 * k, 1024).rearrange("p (r m) -> p r m", r=2) for k in range(2)]
        w0 = TMPW + 4608
        prod = [[bg(w0 + 1024 * k + 512 * m, 512).rearrange("p (r t) -> p r t", r=2) for m in range(2)]
                for k in range(2)]
        w0 += 2048
        zin = [bg(w0 + 512 * k, 512).rearrange("p (r t) -> p r t", r=2) for k in range(2)]
        w0 += 1024
        zsc = [bg(w0 + 512 * k, 512).rearrange("p (r t) -> p r t", r=2) for k in range(2)]
        w0 += 1024
        pout = [[bg(w0 + 1024 * k + 512 * m, 512).rearrange("p (r t) -> p r t", r=2) for m in range(2)]
                for k in range(2)]
        w0 += 2048
        s0 = bg(w0, 512).rearrange("p (r q b) -> p r q b", r=2, q=PAIRS)
        w0 += 512
        sa = [bg(w0 + 512 * k, 512).rearrange("p (r q b) -> p r q b", r=2, q=PAIRS) for k in range(2)]
        w0 += 1024
        fin5 = bg(w0, 2 * PAIRS * 9).rearrange("p (r q b) -> p r q b", r=2, q=PAIRS)
        w0 += 576
        assert w0 <= 34816
        par = sb("par", [P, 16, PAIRS])
        dcol = sb("dcol", [P, KC])
        PR = {n: par[:, i, :] for i, n in enumerate(
            ["lr", "li", "dt", "mag", "ang", "c", "s", "ar", "ai", "zr", "zi", "t0", "t1", "t2", "t3", "t4"])}

        s5_in = sem("s5_in")
        s5_s0 = sem("s5_s0")
        s5_exp = sem("s5_exp")
        s5_arg = sem("s5_arg")
        s5_table = sem("s5_table")
        s5_tab_add = sem("s5_tab_add")
        s5_tab_mul = sem("s5_tab_mul")
        s5_diag = sem("s5_diag")
        s5_zero = sem("s5_zero")
        s5_tr = sem("s5_tr")
        s5_trc = sem("s5_trc")
        s5_bu = sem("s5_bu")
        s5_smp = sem("s5_smp")
        s5_min = sem("s5_min")
        s5_ain = sem("s5_ain")
        s5_scan = sem("s5_scan")
        s5_mout = sem("s5_mout")
        s5_aout = sem("s5_aout")
        s5_rec = sem("s5_rec")
        s5_cd = sem("s5_cd")
        s5_y = sem("s5_y")
        s5_yd = sem("s5_yd")
        s5_g = sem("s5_g")
        s5_fin = sem("s5_fin")

        def s5_params_act(act):
            act.wait_ge(s5_in, 16 * 6)
            nc.scalar.activation(PR["dt"], PR["dt"], ACT.Exp).then_inc(s5_exp, 1)
            act.wait_ge(s5_arg, 1)
            nc.scalar.activation(PR["mag"], PR["t0"], ACT.Exp).then_inc(s5_exp, 1)

        def s5_params_dve(v, cnt):
            tt, ts = nc.vector.tensor_tensor, nc.vector.tensor_scalar
            L = cnt.link
            v.wait_ge(s5_in, 16 * 6)
            L(ts(PR["lr"], PR["lr"], -1e-4, None, ALU.min))
            v.wait_ge(s5_exp, 1)
            tt(PR["t0"], PR["lr"], PR["dt"], ALU.mult).then_inc(s5_arg, 1)
            L(tt(PR["ang"], PR["li"], PR["dt"], ALU.mult))
            rnd = 1.5 * 2.0 ** 23
            L(ts(PR["t1"], PR["ang"], 1.0 / (2 * np.pi), rnd, ALU.mult, ALU.add))
            L(ts(PR["t1"], PR["t1"], rnd, None, ALU.subtract))
            whole = 2 * np.pi
            for part in (6.28125, float(np.float32(whole - 6.28125)),
                         float(whole - 6.28125 - np.float64(np.float32(whole - 6.28125)))):
                L(ts(PR["t2"], PR["t1"], part, None, ALU.mult))
                L(tt(PR["ang"], PR["ang"], PR["t2"], ALU.subtract))
            L(ts(PR["t1"], PR["ang"], 0.125, None, ALU.mult))
            L(tt(PR["t2"], PR["t1"], PR["t1"], ALU.mult))
            L(ts(PR["s"], PR["t2"], 1.0 / 362880, -1.0 / 5040, ALU.mult, ALU.add))
            L(ts(PR["c"], PR["t2"], -1.0 / 3628800, 1.0 / 40320, ALU.mult, ALU.add))
            for a, b in ((1.0 / 120, -1.0 / 720), (-1.0 / 6, 1.0 / 24), (1.0, -0.5)):
                L(tt(PR["s"], PR["s"], PR["t2"], ALU.mult))
                L(ts(PR["s"], PR["s"], a, None, ALU.add))
                L(tt(PR["c"], PR["c"], PR["t2"], ALU.mult))
                L(ts(PR["c"], PR["c"], b, None, ALU.add))
            L(tt(PR["s"], PR["s"], PR["t1"], ALU.mult))
            L(tt(PR["c"], PR["c"], PR["t2"], ALU.mult))
            for _ in range(3):
                L(tt(PR["t3"], PR["s"], PR["c"], ALU.mult))
                L(tt(PR["t2"], PR["s"], PR["s"], ALU.mult))
                L(ts(PR["c"], PR["t2"], -2.0, None, ALU.mult))
                L(tt(PR["t3"], PR["t3"], PR["s"], ALU.add))
                L(ts(PR["s"], PR["t3"], 2.0, None, ALU.mult))
            L(ts(PR["c"], PR["c"], 1.0, None, ALU.add))
            v.wait_ge(s5_exp, 2)
            L(tt(PR["ar"], PR["mag"], PR["c"], ALU.mult))
            L(tt(PR["ai"], PR["mag"], PR["s"], ALU.mult))
            L(tt(PR["t0"], PR["lr"], PR["lr"], ALU.mult))
            L(tt(PR["t1"], PR["li"], PR["li"], ALU.mult))
            L(tt(PR["t0"], PR["t0"], PR["t1"], ALU.add))
            L(nc.vector.reciprocal(PR["t1"], PR["t0"]))
            L(ts(PR["t0"], PR["ar"], -1.0, None, ALU.add))
            L(tt(PR["t2"], PR["t0"], PR["lr"], ALU.mult))
            L(tt(PR["t3"], PR["ai"], PR["li"], ALU.mult))
            L(tt(PR["t2"], PR["t2"], PR["t3"], ALU.add))
            L(tt(PR["zr"], PR["t2"], PR["t1"], ALU.mult))
            L(tt(PR["t2"], PR["ai"], PR["lr"], ALU.mult))
            L(tt(PR["t3"], PR["t0"], PR["li"], ALU.mult))
            L(tt(PR["t2"], PR["t2"], PR["t3"], ALU.subtract))
            L(tt(PR["zi"], PR["t2"], PR["t1"], ALU.mult))
            sh = [P, PAIRS, GH]
            zr, zi = (PR[n][:, :, None].to_broadcast(sh) for n in ("zr", "zi"))
            w3 = [s5w[:, r, :].rearrange("p (q h) -> p q h", q=PAIRS) for r in range(2)]
            b3 = [bbar[:, r, :].rearrange("p (q h) -> p q h", q=PAIRS) for r in range(2)]
            u3 = [TAB[k].rearrange("p q t -> p (q t)")[:, 0:512].rearrange("p (q h) -> p q h", q=PAIRS)
                  for k in range(4)]
            cnt.add(tt(u3[0], zr, w3[0], ALU.mult))
            cnt.add(tt(u3[1], zi, w3[1], ALU.mult))
            cnt.add(tt(u3[2], zr, w3[1], ALU.mult))
            L(tt(u3[3], zi, w3[0], ALU.mult))
            cnt.add(tt(b3[0], u3[0], u3[1], ALU.subtract))
            L(tt(b3[1], u3[2], u3[3], ALU.add))
            L(ts(craw[:, 1, :], craw[:, 1, :], -1.0, None, ALU.mult))

        def s5_table_dve(v, cnt):
            tt = nc.vector.tensor_tensor
            L = cnt.link
            L(nc.vector.memset(ST[:, 0, :, 0:1], 1.0))
            L(nc.vector.memset(ST[:, 1, :, 0:1], 0.0))
            cr, ci = PR["c"], PR["s"]
            for lev in range(8):
                w = 1 << lev
                sh = [P, PAIRS, w]
                crb, cib = cr[:, :, None].to_broadcast(sh), ci[:, :, None].to_broadcast(sh)
                if lev:
                    v.wait_ge(s5_tab_add, 2 * lev)
                tt(TAB[0][:, :, 0:w], ST[:, 0, :, 0:w], crb, ALU.mult).then_inc(s5_tab_mul, 1)
                tt(TAB[1][:, :, 0:w], ST[:, 1, :, 0:w], cib, ALU.mult).then_inc(s5_tab_mul, 1)
                tt(TAB[2][:, :, 0:w], ST[:, 0, :, 0:w], cib, ALU.mult).then_inc(s5_tab_mul, 1)
                tt(TAB[3][:, :, 0:w], ST[:, 1, :, 0:w], crb, ALU.mult).then_inc(s5_tab_mul, 1)
                if lev < 7:
                    v.wait_ge(s5_tab_mul, 4 * lev + 4)
                    cnt.add(tt(PR["t0"], cr, cr, ALU.mult))
                    cnt.add(tt(PR["t1"], ci, ci, ALU.mult))
                    L(tt(PR["t2"], cr, ci, ALU.mult))
                    cnt.add(tt(cr, PR["t0"], PR["t1"], ALU.subtract))
                    L(nc.vector.tensor_scalar(ci, PR["t2"], 2.0, None, ALU.mult))

        def s5_table_pool(g):
            tt = nc.gpsimd.tensor_tensor
            for lev in range(8):
                w = 1 << lev
                g.wait_ge(s5_tab_mul, 4 * lev + 4)
                tt(ST[:, 0, :, w:2 * w], TAB[0][:, :, 0:w], TAB[1][:, :, 0:w], ALU.subtract).then_inc(s5_tab_add, 1)
                tt(ST[:, 1, :, w:2 * w], TAB[2][:, :, 0:w], TAB[3][:, :, 0:w], ALU.add).then_inc(s5_tab_add, 1)
            g.wait_ge(s5_tab_add, 16)
            for k in range(2):
                nc.gpsimd.memset(wdiag[k], 0.0).then_inc(s5_zero, 1)
            g.wait_ge(s5_zero, 2)

        def fill_diag(x, src, c):
            for g2 in range(2):
                rows = slice(64 * g2, 64 * g2 + 64)
                dst = wdiag[x][rows, :, :].rearrange("p r (q m) -> p r q m", q=QC)[:, :, :, GH * g2:GH * g2 + GH]
                s = src[rows, :, ds(c * (QC * GH), QC * GH)].rearrange("p r (q h) -> p r q h", q=QC)
                nc.scalar.activation(dst, s, ACT.Copy).then_inc(s5_diag, 1)

        def s5_in_pool(g):
            def add_in(i, k, first):
                g.wait_ge(s5_min, i * 16 + 2 * k + 2)
                if not (first and k < 2):
                    g.wait_ge(s5_scan, i * 16 + 2 * (k - 2) + 2)
                nc.gpsimd.tensor_tensor(zin[k % 2][:, 0, :], prod[k % 2][0][:, 0, :], prod[k % 2][1][:, 1, :],
                                        ALU.add).then_inc(s5_ain, 1)
                nc.gpsimd.tensor_tensor(zin[k % 2][:, 1, :], prod[k % 2][1][:, 0, :], prod[k % 2][0][:, 1, :],
                                        ALU.subtract).then_inc(s5_ain, 1)

            def add_out(i, k):
                pair = i * 8 + k
                g.wait_ge(s5_mout, i * 16 + 2 * k + 2)
                nc.gpsimd.tensor_tensor(ST[:, 0, ds(pair, 1), 0:TP].rearrange("p o t -> p (o t)"),
                                        pout[k % 2][0][:, 0, :], pout[k % 2][1][:, 1, :],
                                        ALU.subtract).then_inc(s5_aout, 1)
                nc.gpsimd.tensor_tensor(ST[:, 1, ds(pair, 1), 0:TP].rearrange("p o t -> p (o t)"),
                                        pout[k % 2][0][:, 1, :], pout[k % 2][1][:, 0, :],
                                        ALU.add).then_inc(s5_aout, 1)

            def body(i, first):
                for k in range(8):
                    add_in(i, k, first)
                    if k:
                        add_out(i, k - 1)
                    elif not first:
                        add_out(i - 1, 7)
            body(0, True)
            with g.Fori(1, 4) as i:
                body(i, False)
            add_out(3, 7)

        def s5_in_pe(pe):
            pe.wait_ge(norm_h, KC)

            def body(i, first):
                for x in range(2):
                    pe.wait_ge(s5_diag, i * 4 + 2 * x + 2)
                    if not (first and x == 0):
                        pe.wait_ge(s5_trc, i * 4 + 2 * x)
                    for r in range(2):
                        for q in range(QC):
                            mm = nc.tensor.transpose(ps[:, r, q * P:(q + 1) * P], wdiag[x][:, r, q * P:(q + 1) * P],
                                                     ident[:, :])
                    mm.then_inc(s5_tr, 1)
                    pe.wait_ge(s5_trc, i * 4 + 2 * x + 2)
                    for q in range(QC):
                        k = x * QC + q
                        if not (first and k < 2):
                            pe.wait_ge(s5_min, i * 16 + 2 * (k - 2) + 2)
                            pe.wait_ge(s5_smp, i * 8 + k - 1)
                        for r in range(2):
                            mm = nc.tensor.matmul(ps[:, 2 + 2 * (k % 2) + r, 0:T], btr[x][:, r, q * P:(q + 1) * P],
                                                  hT[:, ds(i * 2 + x, 1), :].rearrange("p o t -> p (o t)"),
                                                  start=True, stop=True)
                        mm.then_inc(s5_bu, 1)
            body(0, True)
            with pe.Fori(1, 4) as i:
                body(i, False)

        def s5_in_act(act):
            act.wait_ge(s5_tab_add, 16)
            act.wait_ge(s5_zero, 2)

            def body(i, first):
                for x in range(2):
                    if not first:
                        act.wait_ge(s5_tr, i * 2 + x - 1)
                    fill_diag(x, bbar, i * 2 + x)
                    act.wait_ge(s5_tr, i * 2 + x + 1)
                    if not first:
                        act.wait_ge(s5_bu, i * 8 + x * 4 - 4)
                    for r in range(2):
                        nc.scalar.activation(btr[x][:, r, :], ps[:, r, :], ACT.Copy).then_inc(s5_trc, 1)
                    for q in range(QC):
                        k = x * QC + q
                        act.wait_ge(s5_bu, i * 8 + k + 1)
                        nc.scalar.activation(
                            ST[:, :, ds(i * 8 + k, 1), TP:T].rearrange("p r o t -> p r (o t)"),
                            ps[:, 2 + 2 * (k % 2):4 + 2 * (k % 2), TP:T], ACT.Copy).then_inc(s5_smp, 1)
            body(0, True)
            with act.Fori(1, 4) as i:
                body(i, False)

        def s5_in_dve(v):
            v.wait_ge(s5_tab_add, 16)
            sh = [P, 2, TP]

            def e_of(pair):
                return ST[:, :, ds(pair, 1), 0:TP].rearrange("p r o t -> p r (o t)")

            def mul_in(i, k, first):
                v.wait_ge(s5_smp, i * 8 + k + 1)
                if not (first and k < 2):
                    v.wait_ge(s5_ain, i * 16 + 2 * (k - 2) + 2)
                for m in range(2):
                    nc.vector.tensor_tensor(prod[k % 2][m], ps[:, 2 + 2 * (k % 2) + m, None, 0:TP].to_broadcast(sh),
                                            e_of(i * 8 + k), ALU.mult).then_inc(s5_min, 1)

            def scan_out(i, k, first):
                pair = i * 8 + k
                v.wait_ge(s5_ain, i * 16 + 2 * k + 2)
                if not (first and k < 2):
                    v.wait_ge(s5_mout, i * 16 + 2 * (k - 2) + 2)
                for r in range(2):
                    nc.vector.tensor_tensor_scan(zsc[k % 2][:, r, :], PR["mag"][:, ds(pair, 1)].to_broadcast([P, TP]),
                                                 zin[k % 2][:, r, :], 0.0, ALU.mult, ALU.add).then_inc(s5_scan, 1)
                v.wait_ge(s5_scan, i * 16 + 2 * k + 2)
                if not (first and k < 2):
                    v.wait_ge(s5_aout, i * 16 + 2 * (k - 2) + 2)
                for m in range(2):
                    nc.vector.tensor_tensor(pout[k % 2][m], zsc[k % 2][:, m:m + 1, :].to_broadcast(sh),
                                            e_of(pair), ALU.mult).then_inc(s5_mout, 1)

            def body(i, first):
                for k in range(8):
                    mul_in(i, k, first)
                    if k:
                        scan_out(i, k - 1, first)
                    elif not first:
                        scan_out(i - 1, 7, False)
            body(0, True)
            with v.Fori(1, 4) as i:
                body(i, False)
            scan_out(3, 7, False)

        def s5_samples_dve(v, cnt):
            tt = nc.vector.tensor_tensor
            L = cnt.link
            v.wait_ge(s5_smp, 32)
            v.wait_ge(s5_s0, 16)
            smp = ST[:, :, :, TP:T].rearrange("p r q (b s) -> p r q b s", b=NB)
            sh3 = [P, PAIRS, NB]
            arb, aib = (PR[n][:, :, None].to_broadcast(sh3) for n in ("ar", "ai"))
            for s in range(LS):
                prev = [s0[:, r] if s == 0 else smp[:, r, :, :, s - 1] for r in range(2)]
                cnt.add(tt(sa[0][:, 0], arb, prev[0], ALU.mult))
                cnt.add(tt(sa[0][:, 1], arb, prev[1], ALU.mult))
                cnt.add(tt(sa[1][:, 0], aib, prev[1], ALU.mult))
                L(tt(sa[1][:, 1], aib, prev[0], ALU.mult))
                cnt.add(tt(sa[0][:, 0], sa[0][:, 0], sa[1][:, 0], ALU.subtract))
                L(tt(sa[0][:, 1], sa[0][:, 1], sa[1][:, 1], ALU.add))
                for r in range(2):
                    ins = tt(smp[:, r, :, :, s], smp[:, r, :, :, s], sa[0][:, r], ALU.add)
                    if s == LS - 1:
                        ins.then_inc(s5_rec, 1)
                    else:
                        cnt.add(ins)
                if s < LS - 1:
                    cnt.wait()
            v.wait_ge(s5_rec, 2)
            v.wait_ge(s5_aout, 64)
            for r in range(2):
                nc.vector.tensor_copy(fin5[:, r, :, 0:1], ST[:, r, :, TP - 1:TP]).then_inc(s5_fin, 1)
                nc.vector.tensor_copy(fin5[:, r, :, 1:9], smp[:, r, :, :, LS - 1]).then_inc(s5_fin, 1)

        def s5_out_pe(pe):
            pe.wait_ge(s5_rec, 2)
            pe.wait_ge(s5_aout, 64)
            pe.wait_ge(s5_smp, 32)

            def body(i, first):
                for x in range(2):
                    pe.wait_ge(s5_diag, 16 + i * 4 + 2 * x + 2)
                    if first:
                        pe.wait_ge(s5_min, 64)
                    else:
                        pe.wait_ge(s5_yd, i * 2 + x - 1)
                    for q in range(QC):
                        for r in range(2):
                            mm = nc.tensor.matmul(ps[:, 2 + x, 0:T], wdiag[x][:, r, q * P:(q + 1) * P],
                                                  ST[:, r, ds(i * 8 + x * QC + q, 1), :].rearrange("p o t -> p (o t)"),
                                                  start=(q == 0 and r == 0), stop=(q == QC - 1 and r == 1))
                    mm.then_inc(s5_y, 1)
            body(0, True)
            with pe.Fori(1, 4) as i:
                body(i, False)

        def s5_out_dve(v):
            v.wait_ge(s5_bu, 32)
            with v.Fori(0, 4) as i:
                for x in range(2):
                    v.wait_ge(s5_y, i * 2 + x + 1)
                    u = hT[:, ds(i * 2 + x, 1), :].rearrange("p o t -> p (o t)")
                    nc.vector.scalar_tensor_tensor(out=u, in0=u, scalar=dcol[:, ds(i * 2 + x, 1)],
                                                   in1=ps[:, 2 + x, 0:T], op0=ALU.mult, op1=ALU.add).then_inc(s5_yd, 1)

        def s5_out_act(act):
            act.wait_ge(s5_tr, 8)

            def gelu(c):
                act.wait_ge(s5_yd, c + 1)
                u = hT[:, ds(c, 1), :].rearrange("p o t -> p (o t)")
                nc.scalar.activation(u, u, ACT.Gelu).then_inc(s5_g, 1)

            def body(i, first):
                for x in range(2):
                    if not first:
                        act.wait_ge(s5_y, i * 2 + x - 1)
                    fill_diag(x, craw, i * 2 + x)
                    if x or not first:
                        gelu(i * 2 + x - 1)
            body(0, True)
            with act.Fori(1, 4) as i:
                body(i, False)
            gelu(KC - 1)
            for c in range(KC):
                act.wait_ge(s5_g, c + 1)
                high_part(c).then_inc(hs_hi, 1)

        sig = [bg(TMPW + T * k, T) for k in range(2)]
        gated = [bg(TMPW + 2 * T + T * k, T) for k in range(2)]
        glu_sig = sem("glu_sig")
        glu_mul = sem("glu_mul")
        glu_x = sem("glu_x")

        def glu_pe(pe):
            pe.wait_ge(hs_lo, KC)
            pe.wait_ge(s5_min, 64)

            def free(i, k, first):
                if k % 2 == 0 and not first:
                    pe.wait_ge(glu_mul, i * 2 + k // 2 - 1)

            project(pe, "glu", free)

        def glu_act(act):
            act.wait_ge(s5_y, KC)

            def post(i, k, first):
                if k % 2:
                    m = k // 2
                    block_used(act, "glu", i, k)
                    if not first:
                        act.wait_ge(glu_mul, i * 2 + m - 1)
                    nc.scalar.activation(sig[m], zbank(k), ACT.Sigmoid, scale=UNSC).then_inc(glu_sig, 1)
            per_block(act, "glu", split_hi, post)

        def glu_dve(v):
            for c in range(KC):
                v.wait_ge(hs_hi, c + 1)
                low_part(c).then_inc(hs_lo, 1)

            def post(i, k, first):
                if k % 2:
                    m = k // 2
                    v.wait_ge(glu_sig, i * 2 + m + 1)
                    if not first:
                        v.wait_ge(glu_x, i * 2 + m - 1)
                    nc.vector.scalar_tensor_tensor(out=gated[m], in0=zbank(k - 1), scalar=UNSC, in1=sig[m],
                                                   op0=ALU.mult, op1=ALU.mult).then_inc(glu_mul, 1)
                    v.wait_ge(glu_mul, i * 2 + m + 1)
                    x = xT[:, ds(i * 2 + m, 1), :].rearrange("p o t -> p (o t)")
                    nc.vector.tensor_tensor(x, x, gated[m], ALU.add).then_inc(glu_x, 1)
            per_block(v, "glu", split_lo, post)
            v.wait_ge(glu_x, KC)
            v.sem_inc(x_ready, 1)

        act3 = big[:, :].rearrange("p (j t) -> p j t", j=NK)
        UT = (UB - UA) // RING
        o = UB * T

        def take(n, dt=None):
            nonlocal o
            a = bg(o, n)
            o += n
            return a.bitcast(dt) if dt else a

        val = take(768).rearrange("p (j f h k) -> p j f h k", j=3, f=2, h=PH)
        idu = take(768, U32).rearrange("p (j f h k) -> p j f h k", j=3, f=2, h=PH)
        idf = take(768).rearrange("p (j f h k) -> p j f h k", j=3, f=2, h=PH)
        rest = [take(NK) for _ in range(3)]
        cand = take(PH * NC_).rearrange("p (h n) -> p h n", h=PH)
        cidx = take(PH * NC_).rearrange("p (h n) -> p h n", h=PH)
        rest2 = [take(NC_) for _ in range(2)]
        sc = take(3 * P).rearrange("p (j h k) -> p j h k", j=3, h=PH)
        gate = take(3 * P).rearrange("p (j h k) -> p j h k", j=3, h=PH)
        posu = take(P, U32).rearrange("p (h k) -> p h k", h=PH)
        posf = take(P).rearrange("p (h k) -> p h k", h=PH)
        eq = [take(TK * NC_).rearrange("p (k n) -> p k n", k=TK) for _ in range(2)]
        eid = take(3 * P).rearrange("p (j n) -> p j n", j=3)
        eii = take(3 * P, I32).rearrange("p (j n) -> p j n", j=3)
        e12i = take(6 * P, I32).rearrange("p (j f n) -> p j f n", j=3, f=2)
        e12 = take(6 * P).rearrange("p (j f n) -> p j f n", j=3, f=2)
        sm = take(3 * PH).rearrange("p (j h) -> p j h", j=3)
        rs = take(3 * PH).rearrange("p (j h) -> p j h", j=3)
        assert o <= NK * T
        pq = [sem(f"peer_q{L}") for L in range(2)]
        psc = [sem(f"peer_scores{L}") for L in range(2)]
        ptk = [sem(f"peer_topk{L}") for L in range(2)]
        pge = [sem(f"peer_gelu{L}") for L in range(2)]
        psh = [sem(f"peer_shift{L}") for L in range(2)]
        pex = [sem(f"peer_exp{L}") for L in range(2)]
        pgt = [sem(f"peer_gate{L}") for L in range(2)]
        ptr = [sem(f"peer_tr{L}") for L in range(2)]
        ptc = [sem(f"peer_trc{L}") for L in range(2)]
        poh = [sem(f"peer_onehot{L}") for L in range(2)]
        pdf = [sem(f"peer_diff{L}") for L in range(2)]
        pab = [sem(f"peer_abs{L}") for L in range(2)]
        phA = [sem(f"peer_hot1_{L}") for L in range(2)]
        pG = [sem(f"peer_G{L}") for L in range(2)]
        pmul = [sem(f"peer_mul{L}") for L in range(2)]
        pacc = [sem(f"peer_acc{L}") for L in range(2)]
        pah = [sem(f"peer_act_hi{L}") for L in range(2)]
        pal = [sem(f"peer_act_lo{L}") for L in range(2)]

        def peer_query_pe(pe, L):
            pe.wait_ge(hs_lo, KC * (2, 5)[L])
            if L == 0:
                pe.wait_ge(s_keys, 16)

            def scores(i, k, first):
                pe.wait_ge(pq[L], i * 4 + k + 1)
                if not (first and k < 2):
                    pe.wait_ge(ptk[L], i * 4 + k - 1)
                for j, (t0, w) in enumerate(TILES):
                    mm = nc.tensor.matmul(ps[0:w, k % 2, j * NK:(j + 1) * NK], qbuf[k % 2][:, t0:t0 + w],
                                          keysT[:, L, k % 2, :], start=True, stop=True)
                mm.then_inc(psc[L], 1)

            def after(i, k, first):
                if k:
                    scores(i, k - 1, first)
                elif not first:
                    scores(i - 1, 3, False)
            project(pe, f"wq{L}", lambda i, k, first: None if first else pe.wait_ge(pq[L], i * 4 + k - 3), after)
            scores(3, 3, False)

        def peer_query_act(act, L):
            n0 = FIRST[f"wq{L}"]

            def post(i, k, first):
                block_used(act, f"wq{L}", i, k)
                if not (first and k < 2):
                    act.wait_ge(psc[L], i * 4 + k - 1)
                nc.scalar.activation(qbuf[k % 2], zbank(k), ACT.Copy, scale=UNSC).then_inc(pq[L], 1)
            act.wait_ge(hs_lo, KC * (2, 5)[L])
            per_block(act, f"wq{L}", split_hi, post)

        def states_out(eng, L):
            for o_ in ((out_s5,), (out_hgp, out_hgs))[L]:
                eng.wait_ge(o_, 16)

        def peer_topk_dve(v, cnt, L):
            vv = nc.vector
            states_out(v, L)
            for b in range(2 * PH):
                h, f = b // 2, b % 2
                v.wait_ge(psc[L], b + 1)
                for j, (_, w) in enumerate(TILES):
                    s = ps[0:w, b % 2, j * NK:(j + 1) * NK]
                    cnt.add(vv.max(val[0:w, j, f, h, 0:8], s))
                cnt.wait()
                for j, (_, w) in enumerate(TILES):
                    s = ps[0:w, b % 2, j * NK:(j + 1) * NK]
                    cnt.add(vv.max_index(idu[0:w, j, f, h, 0:8], val[0:w, j, f, h, 0:8], s))
                for j, (_, w) in enumerate(TILES):
                    s = ps[0:w, b % 2, j * NK:(j + 1) * NK]
                    ins = vv.match_replace(rest[j][0:w, :], val[0:w, j, f, h, 0:8], s, LOWEST)
                    if j == 2:
                        ins.then_inc(ptk[L], 1)
                    else:
                        cnt.add(ins)
                v.wait_ge(ptk[L], b + 1)
                for j, (_, w) in enumerate(TILES):
                    cnt.add(vv.max(val[0:w, j, f, h, 8:16], rest[j][0:w, :]))
                cnt.wait()
                for j, (_, w) in enumerate(TILES):
                    cnt.add(vv.max_index(idu[0:w, j, f, h, 8:16], val[0:w, j, f, h, 8:16], rest[j][0:w, :]))
                cnt.wait()

        def peer_pairs_dve(v, cnt, L):
            vv = nc.vector
            L_ = cnt.link
            for j, (_, w) in enumerate(TILES):
                for f in range(2):
                    L_(vv.tensor_copy(idf[0:w, j, f], idu[0:w, j, f]))
                L_(vv.tensor_scalar(idf[0:w, j, 0], idf[0:w, j, 0], float(NK), None, ALU.mult))
                for src, dst in ((val, cand), (idf, cidx)):
                    at = 0
                    for a0, na, nb in RECTS:
                        sh = [w, PH, na, nb]
                        cnt.add(vv.tensor_tensor(
                            dst[0:w, :, at:at + na * nb].rearrange("p h (a b) -> p h a b", a=na),
                            src[0:w, j, 0, :, a0:a0 + na, None].to_broadcast(sh),
                            src[0:w, j, 1, :, None, 0:nb].to_broadcast(sh), ALU.add))
                        at += na * nb
                cnt.wait()
                for h in range(PH):
                    c = cand[0:w, h, :]
                    r = rest2[h % 2][0:w, :]
                    L_(vv.max(sc[0:w, j, h, 0:8], c))
                    cnt.add(vv.max_index(posu[0:w, h, 0:8], sc[0:w, j, h, 0:8], c))
                    L_(vv.match_replace(r, sc[0:w, j, h, 0:8], c, LOWEST))
                    L_(vv.max(sc[0:w, j, h, 8:16], r))
                    L_(vv.max_index(posu[0:w, h, 8:16], sc[0:w, j, h, 8:16], r))
                L_(vv.tensor_copy(posf[0:w], posu[0:w]))
                sh = [w, TK, NC_]
                for h in range(PH):
                    e = eq[h % 2][0:w]
                    L_(vv.tensor_tensor(e, iota_c[0:w, None, :].to_broadcast(sh),
                                        posf[0:w, h, :, None].to_broadcast(sh), ALU.is_equal))
                    L_(vv.tensor_tensor(e, e, cidx[0:w, h, None, :].to_broadcast(sh), ALU.mult))
                    L_(vv.tensor_reduce(eid[0:w, j, h * TK:(h + 1) * TK], e, AX.X, ALU.add))
                vv.tensor_tensor(gate[0:w, j], sc[0:w, j], sc[0:w, j, :, 0:1].to_broadcast([w, PH, TK]),
                                 ALU.subtract).then_inc(psh[L], 1)
                L_(vv.tensor_copy(eii[0:w, j], eid[0:w, j]))
                cnt.add(vv.tensor_scalar(e12i[0:w, j, 0], eii[0:w, j], 7, None, ALU.arith_shift_right))
                L_(vv.tensor_scalar(e12i[0:w, j, 1], eii[0:w, j], NK - 1, None, ALU.bitwise_and))
                L_(vv.tensor_copy(e12[0:w, j], e12i[0:w, j]))

        def peer_gates_dve(v, cnt, L):
            vv = nc.vector
            L_ = cnt.link
            for j, (_, w) in enumerate(TILES):
                v.wait_ge(pex[L], j + 1)
                L_(vv.tensor_reduce(sm[0:w, j], gate[0:w, j], AX.X, ALU.add))
                L_(vv.reciprocal(rs[0:w, j], sm[0:w, j]))
                vv.tensor_tensor(gate[0:w, j], gate[0:w, j], rs[0:w, j, :, None].to_broadcast([w, PH, TK]),
                                 ALU.mult).then_inc(pgt[L], 1)
            for j, (t0, w) in enumerate(TILES):
                v.wait_ge(ptr[L], 3 * j + 3)
                g = ps[:, 2, 0:w]
                L_(vv.tensor_scalar(gate_hi[:, t0:t0 + w], g, SC, None, ALU.mult))
                cnt.add(vv.scalar_tensor_tensor(out=gate_lo[:, t0:t0 + w], in0=g, scalar=SC, in1=gate_hi[:, t0:t0 + w],
                                                op0=ALU.mult, op1=ALU.subtract))
                cnt.wait()
                for m, (dst, sign) in enumerate(((neg_i1T, -1.0), (i2T, 1.0))):
                    vv.tensor_scalar(dst[:, t0:t0 + w], ps[:, m, 0:w], sign, None, ALU.mult).then_inc(ptc[L], 1)

        def peer_exp_act(act, L):
            act.wait_ge(psh[L], 3)
            for j, (_, w) in enumerate(TILES):
                nc.scalar.activation(gate[0:w, j], gate[0:w, j], ACT.Exp).then_inc(pex[L], 1)

        def peer_tr_pe(pe, L):
            pe.wait_ge(pgt[L], 3)
            pe.wait_ge(ptk[L], 2 * PH)
            for j, (t0, w) in enumerate(TILES):
                for m in range(3):
                    src = (e12[0:w, j, m] if m < 2 else gate[0:w, j].rearrange("p h k -> p (h k)"))
                    if j:
                        pe.wait_ge(ptc[L], 2 * j)
                    nc.tensor.transpose(ps[:, m, 0:w], src, ident[0:w, 0:w]).then_inc(ptr[L], 1)

        def peer_u_pe(pe, L, part, a=0, b=None):
            if part == "ua":
                pe.wait_ge(pq[L], 16)
            off = 0 if part == "ua" else UA

            def free(i, k, first):
                if not (first and part == "ua"):
                    pe.wait_ge(pge[L], i * 4 + (off + k - 3))
            project(pe, f"{part}{L}", free, None, a, b)

        def peer_u_act(act, L, part, a=0, b=None):
            if part == "ua":
                states_out(act, L)
            elif a:
                act.wait_ge(ptr[L], 9)
            off = 0 if part == "ua" else UA

            def post(i, k, first):
                block_used(act, f"{part}{L}", i, k)
                nc.scalar.activation(act3[:, ds(i * RING + (off + k), 1), :].rearrange("p o t -> p (o t)"), zbank(k),
                                     ACT.Gelu, scale=UNSC).then_inc(pge[L], 1)
            per_block(act, f"{part}{L}", split_hi, post, a, b)

        def peer_u_dve(v, L, a=0, b=None):
            per_block(v, f"ub{L}", split_lo, lambda i, k, first: None, a, b)

        GROUPS = T // GT

        def spread_loop(eng, body):
            for x in range(2):
                body(0, x, True)
            with eng.Fori(1, GROUPS // 2) as i:
                for x in range(2):
                    body(i, x, False)

        def of_tokens(a, i, x):
            return a[:, None, ds(i * (2 * GT) + x * GT, GT)].to_broadcast([P, NK, GT])

        def peer_g_act(act, L):
            act.wait_ge(used, 2 * FIRST[f"v{L}"])

            def body(i, x, first):
                act.wait_ge(pdf[L], i * 2 + x + 1)
                if not first:
                    act.wait_ge(pG[L], i * 2 + x - 1)
                nc.scalar.activation(hot1[x].rearrange("p j t -> p (j t)"),
                                     ps[:, 4 + 2 * x:6 + 2 * x, :].rearrange("p b n -> p (b n)"),
                                     ACT.Abs).then_inc(pab[L], 1)
                act.wait_ge(pab[L], i * 2 + x + 1)
                nc.scalar.activation(hot1[x], hot1[x], ACT.Relu, bias=1.0, scale=-1.0).then_inc(phA[L], 1)
            spread_loop(act, body)

        def peer_g_dve(v, L):
            vv = nc.vector
            v.wait_ge(ptc[L], 6)
            v.wait_ge(pge[L], NK)
            v.wait_ge(used, 2 * FIRST[f"v{L}"])

            def mul(i, x):
                v.wait_ge(pG[L], i * 2 + x + 1)
                a = act3[:, :, ds(i * (2 * GT) + x * GT, GT)]
                vv.tensor_tensor(a, a, ps[:, 2 * x:2 * x + 2, :].rearrange("p b (s j) -> p j (b s)", j=NK),
                                 ALU.mult).then_inc(pmul[L], 1)

            def body(i, x, first):
                if not (first and x == 0):
                    v.wait_ge(poh[L], i * 6 + 3 * x)
                vv.tensor_tensor(hot2, iota_r[:, :, :], of_tokens(i2T, i, x), ALU.is_equal).then_inc(poh[L], 1)
                if not first:
                    v.wait_ge(pG[L], i * 2 + x - 1)
                v.wait_ge(poh[L], i * 6 + 3 * x + 1)
                for f, gate in enumerate((gate_hi, gate_lo)):
                    vv.tensor_tensor(hot2g[x][f], hot2, of_tokens(gate, i, x), ALU.mult).then_inc(poh[L], 1)
                if x:
                    mul(i, 0)
                elif not first:
                    mul(i - 1, 1)
            spread_loop(v, body)
            mul(GROUPS // 2 - 1, 1)

        def peer_g_pe(pe, L):
            pe.wait_ge(ptc[L], 6)
            pe.wait_ge(pge[L], NK)

            def difference(i, x, first):
                i, x = (i, x) if x < 2 else (i + 1, 0)
                if not first:
                    pe.wait_ge(pab[L], i * 2 + x - 1)
                nh = NK // 2
                for b in range(2):
                    out = ps[:, 4 + 2 * x + b, :]
                    nc.tensor.matmul(out, ident_h[:, :], iota_r[:, b * nh:(b + 1) * nh, :], start=True, stop=False)
                    mm = nc.tensor.matmul(out, ident_h[:, :],
                                          of_tokens(neg_i1T, i, x)[:, 0:nh, :], start=False, stop=True)
                mm.then_inc(pdf[L], 1)

            def body(i, x, first, last=False):
                if not last:
                    difference(i, x + 1, first and x == 0)
                if not first:
                    pe.wait_ge(pmul[L], i * 2 + x - 1)
                pe.wait_ge(phA[L], i * 2 + x + 1)
                pe.wait_ge(poh[L], i * 6 + 3 * x + 3)
                for s in range(GT):
                    out = ps[:, 2 * x + s // 4, (s % 4) * NK:(s % 4 + 1) * NK]
                    for f in range(2):
                        mm = nc.tensor.matmul(out, hot1[x][:, :, s], hot2g[x][f][:, :, s], start=(f == 0), stop=(f == 1))
                mm.then_inc(pG[L], 1)
            difference(0, 0, True)
            body(0, 0, True)
            body(0, 1, True)
            with pe.Fori(1, GROUPS // 2 - 1) as i:
                body(i, 0, False)
                body(i, 1, False)
            body(GROUPS // 2 - 1, 0, False)
            body(GROUPS // 2 - 1, 1, False, last=True)

        def peer_v_pe(pe, L):
            def post(i, k, first):
                pe.wait_ge(pal[L], i * RING + k + 1)
                hi, lo = asp[:, k % 2, 0, :], asp[:, k % 2, 1, :]
                for c in range(KC):
                    if c % 4 == 0:
                        lo_half_done(pe, f"v{L}", i, k, c // 4)
                    for bank, col, t0, w in ACC[c]:
                        mm = three_passes(ps[:, bank, col:col + w], k % 2, c, hi[:, t0:t0 + w], lo[:, t0:t0 + w],
                                          first and k == 0 and c < 6, False, skip_group_check=True)
                    if c % 4 == 3:
                        mm.then_inc(used, 1)
            per_block(pe, f"v{L}", None, post)

        def act_block(i, k):
            i, k = (i, k) if k < RING else (i + 1, k - RING)
            return act3[:, ds(i * RING + k, 1), :].rearrange("p o t -> p (o t)")

        def peer_v_act(act, L):
            act.wait_ge(pmul[L], GROUPS)

            def split(act, name, i, k):
                split_hi(act, name, i, k)
                nc.scalar.activation(asp[:, k % 2, 0, :], act_block(i, k), ACT.Copy).then_inc(pah[L], 1)
            per_block(act, f"v{L}", split, lambda i, k, first: None)

        def peer_v_dve(v, L):
            v.wait_ge(pmul[L], GROUPS)

            def split(v, name, i, k):
                split_lo(v, name, i, k)
                v.wait_ge(pah[L], i * RING + k + 1)
                nc.vector.tensor_tensor(asp[:, k % 2, 1, :], act_block(i, k), asp[:, k % 2, 0, :],
                                        ALU.subtract).then_inc(pal[L], 1)
            per_block(v, f"v{L}", split, lambda i, k, first: None)

        def peer_x_dve(v, L):
            v.wait_ge(used, 2 * (FIRST[f"v{L}"] + NK))
            for c in range(KC):
                for bank, col, t0, w in ACC[c]:
                    nc.vector.scalar_tensor_tensor(out=xT[:, c, t0:t0 + w], in0=ps[:, bank, col:col + w], scalar=UNSC,
                                                   in1=xT[:, c, t0:t0 + w], op0=ALU.mult,
                                                   op1=ALU.add).then_inc(pacc[L], 1)
            v.wait_ge(pacc[L], 10)
            v.sem_inc(x_ready, 1)

        U = KC * T

        def unit(k):
            return bg(U * k, U)

        def h3(a):
            return a.rearrange("p (h t) -> p h t", h=HH)

        Bc, K_, Q_, VT, GS, QM, QI, KM, KD, D1 = (unit(k) for k in range(10))
        CU = bg(U * 10, U)
        vtok = [bg(1024 * j, 1024) for j in range(3)]
        ktok = [bg(3072 + 1024 * j, 1024) for j in range(3)]
        sall = [bg(U * 10 + 1024 * c, 1024).rearrange("p (h v) -> p h v", h=HH) for c in range(NCH)]
        ss = bg(U * 10 + 4096, 8192).rearrange("p (h b v) -> p h b v", h=HH, b=NB)
        smask = bg(U * 10 + 4096 + 8192, TS)
        bmask = bg(U * 10 + 4096 + 8192 + TS, NB)
        pmask = bg(U * 10 + 4096 + 8192 + TS + NB, P)
        pp = [bg(U * 9 + 1024 * j, 1024 if j < 2 else 256).rearrange("p (h t) -> p h t", h=HH) for j in range(3)]
        vb = [bg(U * 8 + 1024 * k, 1024).rearrange("p (b v) -> p b v", b=NB) for k in range(2)]
        O_ = unit(3)
        SQ = unit(7)
        RS = unit(5)
        carry = sb("carry", [P, T])
        lbr = sb("lbr", [P, 2, KC])
        lb, oml = (small[:, 8 * k:8 * k + 8] for k in range(2))
        lt = [small[:, 16 + 8 * k:24 + 8 * k] for k in range(4)]
        dec = small[:, 64:64 + 12 * HH].rearrange("p (h c) -> p h c", h=HH)
        nwv = sb("nwv", [P, 1])

        hg_in = sem("hg_in")
        hg_s0 = sem("hg_s0")
        hg_lbm = sem("hg_lbm")
        hg_lbe = sem("hg_lbe")
        hg_mask = sem("hg_mask")
        hg_ev = sem("hg_evac")
        hg_f = sem("hg_f")
        hg_log = sem("hg_log")
        hg_cum = sem("hg_cum")
        hg_d = sem("hg_d")
        hg_e = sem("hg_e")
        hg_m = sem("hg_m")
        hg_tv = sem("hg_tv")
        hg_tk = sem("hg_tk")
        hg_tvc = sem("hg_tvc")
        hg_tkc = sem("hg_tkc")
        hg_z = sem("hg_z")
        hg_s = sem("hg_s")
        hg_p = sem("hg_p")
        hg_kv = sem("hg_kv")
        hg_S = sem("hg_S")
        hg_o = sem("hg_o")
        hg_oc = sem("hg_oc")
        hg_vb = sem("hg_vb")
        hg_kvs = sem("hg_kvs")
        hg_Ss = sem("hg_Ss")
        hg_sq = sem("hg_sq")
        hg_ssq = sem("hg_ssq")
        hg_rs = sem("hg_rs")
        hg_h = sem("hg_h")
        hg_x = sem("hg_x")

        def hg_masks_pool(g):
            g.wait_ge(x_ready, 3)
            step = [0]

            def L_(ins):
                ins.then_inc(hg_mask, 1)
                step[0] += 1
                g.wait_ge(hg_mask, step[0])
            for m in (pmask, smask, bmask):
                L_(nc.gpsimd.memset(m, 1.0))
            L_(nc.gpsimd.affine_select(out=pmask, in_=pmask, pattern=[[1, P]], base=0, channel_multiplier=-1,
                                       compare_op=ALU.is_ge, fill=0.0))
            L_(nc.gpsimd.memset(pmask[0:CH, CH:P], 0.0))
            s2 = smask[0:TS, :].rearrange("p (b i) -> p b i", b=NB)
            L_(nc.gpsimd.affine_select(out=s2, in_=s2, pattern=[[LS, NB], [1, LS]], base=0, channel_multiplier=-1,
                                       compare_op=ALU.is_ge, fill=0.0))
            for m, pat in ((s2, [[-LS, NB], [0, LS]]), (bmask[0:TS, :], [[-LS, NB]])):
                L_(nc.gpsimd.affine_select(out=m, in_=m, pattern=pat, base=0, channel_multiplier=1,
                                           compare_op=ALU.is_ge, fill=0.0))
                L_(nc.gpsimd.affine_select(out=m, in_=m, pattern=[[-a, n] for a, n in pat], base=LS - 1,
                                           channel_multiplier=-1, compare_op=ALU.is_ge, fill=0.0))
        N_MASK = 10

        def hg_lb_dve(v, cnt):
            vv = nc.vector
            v.wait_ge(hg_in, 32)
            cnt.link(vv.tensor_tensor(lt[0], lbr[:, 0, :], lbr[:, 1, :], ALU.max))
            vv.tensor_tensor(lt[1], lbr[:, 0, :], lt[0], ALU.subtract).then_inc(hg_lbm, 1)
            vv.tensor_tensor(lt[2], lbr[:, 1, :], lt[0], ALU.subtract).then_inc(hg_lbm, 1)
            v.wait_ge(hg_lbe, 2)
            cnt.link(vv.tensor_tensor(lt[3], lt[1], lt[2], ALU.add))
            cnt.link(vv.reciprocal(lt[0], lt[3]))
            cnt.add(vv.tensor_tensor(lt[1], lt[1], lt[0], ALU.mult))
            cnt.link(vv.tensor_tensor(lt[2], lt[2], lt[0], ALU.mult))
            cnt.link(vv.tensor_tensor(lt[3], lt[1], lt[2], ALU.add))
            cnt.link(vv.tensor_tensor(lb, lt[3], lt[1], ALU.subtract))
            cnt.link(vv.tensor_scalar(oml, lb, -1.0, 1.0, ALU.mult, ALU.add))
            cnt.add(vv.memset(carry[:, :], 1.0))
            cnt.wait()
            cnt.add(vv.memset(carry[:, 0:TP:CH], 0.0))
            cnt.link(vv.memset(carry[:, TP:T:LS], 0.0))

        def hg_lb_act(act):
            act.wait_ge(hg_lbm, 2)
            for k in (1, 2):
                nc.scalar.activation(lt[k], lt[k], ACT.Exp).then_inc(hg_lbe, 1)

        def hg_in_pe(pe):
            pe.wait_ge(hs_lo, 3 * KC)
            project(pe, "win", lambda i, k, first: None if first else pe.wait_ge(hg_ev, i * 4 + k - 3))

        def hg_evac_act(act, part, fns):
            n0 = FIRST["win"]

            def post(i, k, first):
                block_used(act, "win", i, k)
                for dst, fn, scale in fns:
                    ins = nc.scalar.activation(h3(dst)[:, ds(i * 4 + (k - 8 * part), 1), :].rearrange("p o t -> p (o t)"),
                                               zbank(k), fn, scale=scale * UNSC)
                ins.then_inc(hg_ev, 1)
            per_block(act, "win", split_hi, post, 2 * part, 2 * part + 2)

        def hg_act(act):
            act.wait_ge(x_ready, 3)
            hg_evac_act(act, 0, [(Bc, ACT.Sigmoid, 1.0), (K_, ACT.Sigmoid, -1.0)])
            act.wait_ge(hg_f, 1)
            nc.scalar.activation(Bc, Bc, ACT.Ln).then_inc(hg_log, 1)
            hg_evac_act(act, 1, [(Q_, ACT.Silu, 1.0)])
            act.wait_ge(hg_cum, 8)
            nc.scalar.activation(QI, CU, ACT.Exp).then_inc(hg_e, 1)
            act.wait_ge(hg_d, 2)
            nc.scalar.activation(QM, D1, ACT.Exp).then_inc(hg_e, 1)
            nc.scalar.activation(KM, D1, ACT.Exp, scale=-1.0).then_inc(hg_e, 1)
            act.wait_ge(hg_d, 4)
            nc.scalar.activation(KD, Bc, ACT.Exp).then_inc(hg_e, 1)
            hg_evac_act(act, 2, [(VT, ACT.Copy, 1.0)])
            hg_evac_act(act, 3, [(GS, ACT.Silu, 1.0)])
            for j, (_, w) in enumerate(TILES):
                act.wait_ge(hg_tv, j + 1)
                if j == 0:
                    act.wait_ge(hg_m, 4)
                nc.scalar.activation(vtok[j][0:w, :], ps[0:w, 0:2, :].rearrange("p b n -> p (b n)"),
                                     ACT.Copy).then_inc(hg_tvc, 1)
            act.wait_ge(hg_tv, 3)
            for h in range(HH):
                act.wait_ge(hg_o, h + 1)
                nc.scalar.activation(h3(O_)[:, h, :], ps[:, 6 + h % 2, 0:T], ACT.Copy).then_inc(hg_oc, 1)
            act.wait_ge(hg_oc, 8)
            nc.scalar.activation(SQ, O_, ACT.Square).then_inc(hg_sq, 1)
            for h in range(HH):
                act.wait_ge(hg_ssq, h + 1)
                nc.scalar.activation(h3(RS)[:, h, :], ps[:, 2 + h % 2, 0:T], ACT.Sqrt, bias=epsc[:, 0:1],
                                     scale=1.0 / P).then_inc(hg_rs, 1)
            act.wait_ge(hg_h, 1)
            for c in range(KC):
                high_part(c).then_inc(hs_hi, 1)
            per_block(act, "wout", split_hi, lambda i, k, first: None)

        def hg_dve(v, cnt):
            vv = nc.vector
            tt = vv.tensor_tensor
            v.wait_ge(hg_ev, 8)
            for h in range(HH):
                cnt.add(vv.tensor_scalar(h3(Bc)[:, h, :], h3(Bc)[:, h, :], oml[:, h:h + 1], lb[:, h:h + 1],
                                         ALU.mult, ALU.add))
            cnt.wait()
            vv.tensor_scalar(Bc, Bc, F_LEAST, None, ALU.max).then_inc(hg_f, 1)
            cnt.link(tt(h3(K_), h3(K_), oml[:, :, None].to_broadcast([P, HH, T]), ALU.mult))
            v.wait_ge(hg_log, 1)
            for h in range(HH):
                vv.tensor_tensor_scan(h3(CU)[:, h, :], carry[:, :], h3(Bc)[:, h, :], 0.0, ALU.mult,
                                      ALU.add).then_inc(hg_cum, 1)
            v.wait_ge(hg_cum, 8)

            def parts(a):
                p = h3(a)[:, :, 0:TP].rearrange("p h (c t) -> p h c t", c=NCH)
                s = h3(a)[:, :, TP:T].rearrange("p h (c t) -> p h c t", c=NB)
                return (p, NCH, CH), (s, NB, LS)
            for (b_, n, c), (d_, _, _) in zip(parts(CU), parts(D1)):
                tt(d_, b_, b_[:, :, :, c // 2:c // 2 + 1].to_broadcast([P, HH, n, c]), ALU.subtract).then_inc(hg_d, 1)
            for (b_, n, c), (d_, _, _) in zip(parts(CU), parts(Bc)):
                tt(d_, b_[:, :, :, c - 1:c].to_broadcast([P, HH, n, c]), b_, ALU.subtract).then_inc(hg_d, 1)
            v.wait_ge(hg_e, 1)
            cnt.add(vv.tensor_copy(dec[:, :, 0:NCH], h3(QI)[:, :, CH - 1:TP:CH]))
            cnt.link(vv.tensor_copy(dec[:, :, NCH:12], h3(QI)[:, :, TP + LS - 1:T:LS]))
            v.wait_ge(hg_e, 4)
            v.wait_ge(hg_ev, 16)
            for dst, src in ((QI, Q_), (QM, Q_), (KM, K_), (KD, K_)):
                tt(dst, dst, src, ALU.mult).then_inc(hg_m, 1)
            v.wait_ge(hg_e, 4)
            for j in range(3):
                vv.memset(pp[j], 0.0).then_inc(hg_z, 1)
            for j, (_, w) in enumerate(TILES):
                v.wait_ge(hg_tk, j + 1)
                if j == 0:
                    v.wait_ge(hg_m, 4)
                vv.tensor_copy(ktok[j][0:w, :], ps[0:w, 2:4, :].rearrange("p b n -> p (b n)")).then_inc(hg_tkc, 1)
            v.wait_ge(hg_mask, N_MASK)
            v.wait_ge(hg_z, 3)
            for j, (_, w) in enumerate(TILES):
                v.wait_ge(hg_s, j + 1)
                m = (pmask if w == P else smask)[0:w, None, 0:w].to_broadcast([w, 4, w]).bitcast(I32)
                for half in range(2):
                    bank = 4 + 2 * (j % 2) + half
                    vv.copy_predicated(pp[j][0:w, 4 * half:4 * half + 4, :], m,
                                       ps[0:w, bank, 0:4 * w].rearrange("p (h t) -> p h t", h=4)).then_inc(hg_p, 1)
            for c in range(NCH):
                kv = ps[:, 2 * (c % 2):2 * (c % 2) + 2, :].rearrange("p b (h v) -> p (b h) v", h=4)
                v.wait_ge(hg_kv, c + 1)
                if c == 0:
                    vv.tensor_copy(sall[0], kv).then_inc(hg_S, 1)
                else:
                    v.wait_ge(hg_S, c)
                    cnt.link(tt(sall[c], sall[c - 1], dec[:, :, c:c + 1].to_broadcast([P, HH, P]), ALU.mult))
                    tt(sall[c], sall[c], kv, ALU.add).then_inc(hg_S, 1)
            v.wait_ge(hg_tvc, 3)
            v.wait_ge(hg_s0, 16)
            v.wait_ge(hg_tk, 3)
            for h in range(HH):
                if h >= 2:
                    v.wait_ge(hg_kvs, h - 1)
                sh = [TS, NB, P]
                tt(vb[h % 2][0:TS], vtok[2][0:TS, None, h * P:(h + 1) * P].to_broadcast(sh),
                   bmask[0:TS, :, None].to_broadcast(sh), ALU.mult).then_inc(hg_vb, 1)
                v.wait_ge(hg_o, h + 1)
                cnt.link(tt(ss[:, h], ss[:, h], dec[:, h, NCH:12, None].to_broadcast([P, NB, P]), ALU.mult))
                v.wait_ge(hg_kvs, h + 1)
                b0 = 4 * (h % 2)
                tt(ss[:, h], ss[:, h], ps[:, b0:b0 + 2, :].rearrange("p b (c v) -> p (b c) v", c=4),
                   ALU.add).then_inc(hg_Ss, 1)
            v.wait_ge(hg_rs, 8)
            cnt.link(vv.reciprocal(RS, RS))
            cnt.link(tt(O_, O_, RS, ALU.mult))
            vv.scalar_tensor_tensor(out=hT[:, :, :].rearrange("p c t -> p (c t)"), in0=O_, scalar=nwv[:, 0:1],
                                    in1=GS, op0=ALU.mult, op1=ALU.mult).then_inc(hg_h, 1)
            for c in range(KC):
                v.wait_ge(hs_hi, 3 * KC + c + 1)
                low_part(c).then_inc(hs_lo, 1)

            def post(i, k, first):
                block_used(v, "wout", i, k)
                x = xT[:, ds(i * 4 + k, 1), :].rearrange("p o t -> p (o t)")
                vv.scalar_tensor_tensor(out=x, in0=zbank(k), scalar=UNSC, in1=x, op0=ALU.mult,
                                        op1=ALU.add).then_inc(hg_x, 1)
            per_block(v, "wout", split_lo, post)
            v.wait_ge(hg_x, 8)
            v.sem_inc(x_ready, 1)

        def hg_pe(pe):
            mm_, tr = nc.tensor.matmul, nc.tensor.transpose
            pe.wait_ge(hg_ev, 32)
            pe.wait_ge(hg_m, 4)
            for j, (t0, w) in enumerate(TILES):
                if j:
                    pe.wait_ge(hg_tvc, j)
                for h in range(HH):
                    mm = tr(ps[0:w, h // 4, (h % 4) * P:(h % 4 + 1) * P], h3(VT)[:, h, t0:t0 + w], ident[:, :])
                mm.then_inc(hg_tv, 1)
                if j:
                    pe.wait_ge(hg_tkc, j)
                for h in range(HH):
                    mm = tr(ps[0:w, 2 + h // 4, (h % 4) * P:(h % 4 + 1) * P], h3(KD)[:, h, t0:t0 + w], ident[:, :])
                mm.then_inc(hg_tk, 1)
            for j, (t0, w) in enumerate(TILES):
                if j == 2:
                    pe.wait_ge(hg_p, 2)
                for h in range(HH):
                    mm = mm_(ps[0:w, 4 + 2 * (j % 2) + h // 4, (h % 4) * w:(h % 4 + 1) * w],
                             h3(KM)[:, h, t0:t0 + w], h3(QM)[:, h, t0:t0 + w], start=True, stop=True)
                mm.then_inc(hg_s, 1)
            pe.wait_ge(hg_tvc, 3)
            pe.wait_ge(hg_tkc, 3)
            for c in range(NCH):
                if c >= 2:
                    pe.wait_ge(hg_S, c - 1)
                j, r0 = c // 2, CH * (c % 2)
                for h in range(HH):
                    mm = mm_(ps[:, 2 * (c % 2) + h // 4, (h % 4) * P:(h % 4 + 1) * P],
                             ktok[j][r0:r0 + CH, h * P:(h + 1) * P], vtok[j][r0:r0 + CH, h * P:(h + 1) * P],
                             start=True, stop=True)
                mm.then_inc(hg_kv, 1)
            pe.wait_ge(hg_p, 6)
            pe.wait_ge(hg_S, 3)
            pe.wait_ge(hg_s0, 16)
            for h in range(HH):
                if h >= 2:
                    pe.wait_ge(hg_oc, h - 1)
                bank = 6 + h % 2
                for j, (t0, w) in enumerate(TILES):
                    mm = mm_(ps[:, bank, t0:t0 + w], vtok[j][0:w, h * P:(h + 1) * P], pp[j][0:w, h, :],
                             start=True, stop=False, skip_group_check=True)
                    if w == P:
                        for c in range(2 * j, 2 * j + 2):
                            if c:
                                a = c * CH
                                mm = mm_(ps[:, bank, a:a + CH], sall[c - 1][:, h, :], h3(QI)[:, h, a:a + CH],
                                         start=False, stop=False, skip_group_check=True)
                    else:
                        for b in range(NB):
                            a = TP + b * LS
                            mm = mm_(ps[:, bank, a:a + LS], ss[:, h, b, :], h3(QI)[:, h, a:a + LS],
                                     start=False, stop=False, skip_group_check=True)
                mm.then_inc(hg_o, 1)
            pe.wait_ge(hg_S, 4)
            for h in range(HH):
                if h >= 2:
                    pe.wait_ge(hg_Ss, h - 1)
                pe.wait_ge(hg_vb, h + 1)
                b0 = 4 * (h % 2)
                for half in range(2):
                    mm = mm_(ps[:, b0 + half, :], ktok[2][0:TS, h * P:(h + 1) * P],
                             vb[h % 2][0:TS, 4 * half:4 * half + 4, :].rearrange("p b v -> p (b v)"),
                             start=True, stop=True)
                mm.then_inc(hg_kvs, 1)
            pe.wait_ge(hg_sq, 1)
            for h in range(HH):
                if h >= 2:
                    pe.wait_ge(hg_rs, h - 1)
                mm_(ps[:, 2 + h % 2, 0:T], ones[:, :], h3(SQ)[:, h, :], start=True, stop=True).then_inc(hg_ssq, 1)
            pe.wait_ge(hs_lo, 4 * KC)
            pe.wait_ge(hg_Ss, 8)
            pe.wait_ge(hg_oc, 8)
            project(pe, "wout", lambda i, k, first: None if first else pe.wait_ge(hg_x, i * 4 + k - 3))

        SQ5, SQP = TMPW, 0

        @block.sync
        def _(sp):
            sp.dma_start(xT[:, :, :], t_in["xT"]).then_inc(s_x, 16)
            sp.dma_start(normw[:, :, :], t_in["normw"]).then_inc(s_par, 16)
            for k, n in enumerate(("lam_re", "lam_im", "log_dt")):
                sp.dma_start(par[:, k, :], t_in[n]).then_inc(s5_in, 16)
            sp.dma_start(s5w, t_in["s5b"]).then_inc(s5_in, 16)
            sp.dma_start(craw, t_in["s5c"]).then_inc(s5_in, 16)
            sp.dma_start(dcol[:, :], t_in["s5d"]).then_inc(s5_in, 16)
            sp.dma_start(keysT[:, :, :, :], t_in["keysT"]).then_inc(s_keys, 16)
            sp.dma_start(lbr[:, :, :], t_in["lbr"]).then_inc(hg_in, 16)
            sp.dma_start(nwv[:, :], t_in["hgnw"]).then_inc(hg_in, 16)
            before = None
            for n, _ in SEGMENTS:
                stream_segment(sp, n, before)
                before = n
            sp.wait_ge(norm_h, 5 * KC)
            sp.dma_start(t_out["y"], hT[:, :, :]).then_inc(out_y, 16)
            sp.wait_ge(out_y, 16)

        @block.gpsimd
        def _(g):
            n = [0]

            def L_(ins):
                ins.then_inc(s_const, 1)
                n[0] += 1
                g.wait_ge(s_const, n[0])
            L_(nc.gpsimd.memset(ident[:, :], 0.0))
            L_(nc.gpsimd.affine_select(out=ident[:, :], in_=ident[:, :], compare_op=ALU.not_equal, fill=1.0,
                                       base=0, pattern=[[-1, P]], channel_multiplier=1))
            L_(nc.gpsimd.tensor_copy(ident_h[:, :], ident[:, :]))
            L_(nc.gpsimd.memset(ones[:, :], 1.0))
            L_(nc.gpsimd.memset(epsc[:, :], EPS))
            L_(nc.gpsimd.iota(iota_r[:, :, :], pattern=[[1, NK], [0, GT]], base=0, channel_multiplier=0,
                              allow_small_or_imprecise_dtypes=True))
            L_(nc.gpsimd.iota(iota_c[:, :], pattern=[[1, NC_]], base=0, channel_multiplier=0,
                              allow_small_or_imprecise_dtypes=True))
            s5_table_pool(g)
            g.dma_start(s0.rearrange("p r q b -> p (r q b)"), t_in["s5s0"]).then_inc(s5_s0, 16)
            s5_in_pool(g)
            g.wait_ge(s5_fin, 4)
            g.dma_start(t_out["s5f"], fin5.rearrange("p r q b -> p (r q b)")).then_inc(out_s5, 16)
            split_pool(g, "wq0")
            split_pool(g, "ua0")
            g.wait_ge(x_ready, 3)
            g.dma_start(ss.rearrange("p h b v -> p (h b v)"), t_in["hgs0"]).then_inc(hg_s0, 16)
            hg_masks_pool(g)
            split_pool(g, "win")
            g.wait_ge(hg_S, 4)
            g.dma_start(t_out["hgp"], sall[3].rearrange("p h v -> p (h v)")).then_inc(out_hgp, 16)
            g.wait_ge(hg_Ss, 8)
            g.dma_start(t_out["hgs"], ss.rearrange("p h b v -> p (h b v)")).then_inc(out_hgs, 16)
            split_pool(g, "wq1")
            split_pool(g, "ua1")
            g.wait_ge(out_s5, 16)
            g.wait_ge(out_hgp, 16)
            g.wait_ge(out_hgs, 16)

        @block.tensor
        def _(pe):
            pe.wait_ge(s_const, 7)
            norm_pe(pe, 0, SQ5)
            s5_in_pe(pe)
            s5_out_pe(pe)
            glu_pe(pe)
            for L in range(2):
                norm_pe(pe, 2 * L + 1, SQP)
                peer_query_pe(pe, L)
                peer_u_pe(pe, L, "ua")
                peer_u_pe(pe, L, "ub", 0, UT)
                peer_tr_pe(pe, L)
                peer_u_pe(pe, L, "ub", UT)
                peer_g_pe(pe, L)
                peer_v_pe(pe, L)
                norm_pe(pe, 2 * L + 2, SQP)
                if L == 0:
                    hg_in_pe(pe)
                    hg_pe(pe)

        @block.scalar
        def _(act):
            act.wait_ge(s_const, 7)
            act.wait_ge(s_x, 16)
            norm_act(act, 0, SQ5)
            s5_params_act(act)
            s5_in_act(act)
            s5_out_act(act)
            glu_act(act)
            for L in range(2):
                norm_act(act, 2 * L + 1, SQP)
                peer_query_act(act, L)
                peer_u_act(act, L, "ua")
                peer_exp_act(act, L)
                peer_u_act(act, L, "ub", 0, UT)
                peer_u_act(act, L, "ub", UT)
                peer_g_act(act, L)
                peer_v_act(act, L)
                norm_act(act, 2 * L + 2, SQP)
                if L == 0:
                    hg_lb_act(act)
                    hg_act(act)

        @block.vector
        def _(v):
            cnt = Count(v, dv)
            v.wait_ge(s_x, 16)
            v.wait_ge(s_par, 16)
            v.wait_ge(s_const, 7)
            v.sem_inc(x_ready, 1)
            norm_dve(v, cnt, 0)
            s5_params_dve(v, cnt)
            s5_table_dve(v, cnt)
            s5_in_dve(v)
            s5_samples_dve(v, cnt)
            s5_out_dve(v)
            glu_dve(v)
            for L in range(2):
                norm_dve(v, cnt, 2 * L + 1)
                peer_topk_dve(v, cnt, L)
                peer_pairs_dve(v, cnt, L)
                peer_u_dve(v, L, 0, UT)
                peer_gates_dve(v, cnt, L)
                peer_u_dve(v, L, UT)
                peer_g_dve(v, L)
                peer_v_dve(v, L)
                peer_x_dve(v, L)
                norm_dve(v, cnt, 2 * L + 2)
                if L == 0:
                    hg_lb_dve(v, cnt)
                    hg_dve(v, cnt)


def host_layout(i):
    f = {k: np.ascontiguousarray(np.asarray(v)) for k, v in i.items()}
    c = np.ascontiguousarray

    def cols(w):
        n = w.shape[1] // P
        return w.reshape(KC, P, n, P).transpose(2, 1, 0, 3).reshape(n, P, BLK)

    def vec(a):
        return np.moveaxis(a.reshape(a.shape[:-1] + (KC, P)), -1, 0)

    def states(a):
        b = a.reshape((PAIRS, 2, 64) + a.shape[2:])
        return np.moveaxis(b, 0, 2).reshape((P, PAIRS) + a.shape[2:])

    x = np.concatenate([f["x_prompt"].reshape(TP, D), f["x_sample"].reshape(TS, D)])
    glu = cols(f["s5_w_glu"][0])
    win = cols(f["hg_w_in"][0])
    r = {
        "xT": c(x.reshape(T, KC, P).transpose(2, 1, 0)),
        "normw": c(vec(np.stack([f["norm_mix"][0], f["norm_ffn"][0], f["norm_mix"][1], f["norm_ffn"][1],
                                 f["norm_final"]]))),
        "lam_re": c(states(f["s5_lambda_re"][0])),
        "lam_im": c(states(f["s5_lambda_im"][0])),
        "log_dt": c(states(np.repeat(f["s5_log_dt"][0][:, None], 64, axis=1))),
        "s5b": c(np.stack([states(f[n][0]) for n in ("s5_b_re", "s5_b_im")], 1).reshape(P, 2, PAIRS * GH)),
        "s5c": c(np.stack([states(f[n][0].transpose(0, 2, 1)) for n in ("s5_c_re", "s5_c_im")], 1)
                 .reshape(P, 2, PAIRS * GH)),
        "s5d": c(vec(f["s5_d"][0])),
        "s5s0": c(np.stack([states(f[n][0].transpose(1, 2, 0)) for n in ("state_s5_re", "state_s5_im")], 1)
                  .reshape(P, 2 * PAIRS * NB)),
        "keysT": c(np.stack([np.stack([f["peer_keys1"][l].T, f["peer_keys2"][l].T], 1) for l in range(2)], 1)),
        "lbr": c(vec(f["hg_lower_bounds"])),
        "hgnw": c(f["hg_norm_w"][0][:, None]),
        "hgs0": c(f["state_hgrn"][0].transpose(2, 1, 0, 3).reshape(P, HH * NB * P)),
        "glu": c(glu.reshape(2, KC, P, BLK).transpose(1, 0, 2, 3).reshape(16, P, BLK)),
        "win": c(np.concatenate([win[8:16], win[0:8], win[16:24], win[24:32]])),
        "wout": c(cols(f["hg_w_out"][0])),
    }
    for l in range(2):
        r[f"wq{l}"] = c(cols(f["peer_w_q"][l]))
        u = c(f["peer_u"][l].reshape(NK, NK, KC, P).transpose(1, 3, 2, 0).reshape(NK, P, BLK))
        r[f"ua{l}"], r[f"ub{l}"] = u[:UA], u[UA:]
        r[f"v{l}"] = c(f["peer_v"][l].reshape(NK, NK, D).transpose(1, 0, 2))
    return r


OUTS = {"y": (P, KC, T), "s5f": (P, 2 * PAIRS * 9), "hgp": (P, HH * P), "hgs": (P, HH * NB * P)}


def kernel(**inputs):
    import concourse.bacc as bacc
    from concourse.bass_utils import run_bass_kernel_spmd

    nc = bacc.Bacc("TRN2", target_bir_lowering=False, num_devices=1)
    arrays = host_layout(inputs)
    t_in = {k: nc.dram_tensor("in_" + k, a.shape, mybir.dt.from_np(a.dtype), kind="ExternalInput").ap()
            for k, a in arrays.items()}
    t_out = {k: nc.dram_tensor("out_" + k, s, F32, kind="ExternalOutput").ap() for k, s in OUTS.items()}
    build(nc, t_in, t_out)
    r = run_bass_kernel_spmd(nc, [{"in_" + k: a for k, a in arrays.items()}], core_ids=[0]).results[0]
    y = r["out_y"].transpose(2, 1, 0).reshape(T, D)
    s5 = r["out_s5f"].reshape(2, 64, 2, PAIRS, 9).transpose(2, 4, 3, 0, 1).reshape(2, 1, 9, 2 * PAIRS, 64)
    hgp = r["out_hgp"].reshape(P, HH, P).transpose(1, 0, 2).reshape(1, 1, HH, P, P)
    hgs = r["out_hgs"].reshape(P, HH, NB, P).transpose(2, 1, 0, 3).reshape(1, NB, HH, P, P)
    return (y[:TP].reshape(1, TP, D), y[TP:].reshape(NB, LS, D),
            s5[0, :, 0:1], s5[1, :, 0:1], hgp, s5[0, :, 1:], s5[1, :, 1:], hgs)
```

```python
from contextlib import ExitStack

import numpy as np
import concourse.bass as bass
from concourse import mybir

F32 = mybir.dt.float32
F16 = mybir.dt.float16
I32 = mybir.dt.int32
U32 = mybir.dt.uint32
ACT = mybir.ActivationFunctionType
ALU = mybir.AluOpType
AX = mybir.AxisListType
ds = bass.ds

P = 128
D = 1024
KC = D // P
TP, NB, LS = 256, 8, 4
TS = NB * LS
T = TP + TS
TILES = [(0, P), (P, P), (2 * P, TS)]

PAIRS = 32
GH = 16
QC = 4
HH = 8
CH = 64
NCH = TP // CH
PH, NK, TK = 8, 128, 16
RECTS = [(0, 1, 16), (1, 1, 8), (2, 2, 5), (4, 4, 3), (8, 8, 1)]
NC_ = sum(r * c for _, r, c in RECTS)

GT = 8
RING = 4
BLK = KC * P
EPS = 1e-6
F_LEAST = 2.0 ** -64
LOWEST = -3.0e38

SC = 16.0
UNSC = 1.0 / (SC * SC)

UA, UB = 72, 96
SEGMENTS = [("glu", 16), ("wq0", 16), ("ua0", UA), ("ub0", NK - UA), ("v0", NK), ("win", 32), ("wout", 8),
            ("wq1", 16), ("ua1", UA), ("ub1", NK - UA), ("v1", NK)]
FIRST, _n = {}, 0
for _name, _c in SEGMENTS:
    FIRST[_name] = _n
    _n += _c

BY_POOL = {"wq0", "ua0", "wq1", "ua1", "win"}
LO_FIRST, _c2 = {}, {True: 0, False: 0}
for _name, _c in SEGMENTS:
    LO_FIRST[_name] = _c2[_name in BY_POOL]
    _c2[_name in BY_POOL] += _c
N_BLOCKS = dict(SEGMENTS)

ACC = [[(c, 0, 0, T)] for c in range(6)] + \
      [[(0, T, 0, 512 - T), (1, T, 512 - T, 2 * T - 512)], [(2, T, 0, 512 - T), (3, T, 512 - T, 2 * T - 512)]]


class Count:

    def __init__(self, eng, sem):
        self.eng, self.sem, self.n, self.loop = eng, sem, 0, None

    def add(self, ins):
        ins.then_inc(self.sem, 1)
        self.n += 1
        return self.n

    def wait(self, n=None):
        v = self.n if n is None else n
        self.eng.wait_ge(self.sem, v if self.loop is None else v + self.loop)

    def link(self, ins):
        self.add(ins)
        self.wait()

    def enter(self, i, first, per):
        self.start, self.per, self.loop = self.n, per, (i - first) * per

    def leave(self, trips):
        assert self.n - self.start == self.per, (self.n - self.start, self.per)
        self.n, self.loop = self.start + trips * self.per, None


def build(nc, t_in, t_out):
    with ExitStack() as ctx:
        def sb(name, shape, dt=F32):
            return ctx.enter_context(nc.sbuf_tensor(name, shape, dt))

        def sem(name):
            return ctx.enter_context(nc.semaphore(name))

        big = sb("big", [P, NK * T])
        xT = sb("xT", [P, KC, T])
        hT = sb("hT", [P, KC, T])
        hs = sb("hs", [P, 2, KC, T], F16)
        ring = sb("ring", [P, RING, BLK])
        wsp = sb("wsp", [P, 2, 2, BLK], F16)
        ident = sb("ident", [P, P])
        ident_h = sb("ident_h", [P, P], F16)
        ones = sb("ones", [P, P])
        iota_r = sb("iota_r", [P, NK, GT], F16)
        iota_c = sb("iota_c", [P, NC_])
        epsc = sb("epsc", [P, 1])
        normw = sb("normw", [P, 5, KC])
        std = sb("std", [P, T])
        keysT = sb("keysT", [P, 2, 2, NK])
        hT_half = hT[:, :, :].rearrange("p c t -> p (c t)").bitcast(F16)
        neg_i1T, i2T, gate_hi, gate_lo = (hT_half[:, T * k:T * k + T] for k in range(4))
        gates = hT_half[:, 2 * T:4 * T].rearrange("p (f t) -> p f t", f=2)
        asp = hT[:, 3:5, :].rearrange("p a t -> p (a t)").bitcast(F16).rearrange("p (s f t) -> p s f t", s=2, f=2)
        q16 = [hT[:, 4 + k, :] for k in range(2)]
        qsp = [hT[:, 6 + k, :].bitcast(F16).rearrange("p (f t) -> p f t", f=2) for k in range(2)]
        hs_half = hs[:, :, :, :].rearrange("p f c t -> p (f c t)")

        def spread_buffer(k):
            n = NK * GT
            flat = (hs_half[:, n * k:n * k + n] if k < 4 else
                    hT_half[:, 4 * T + n * (k - 4):4 * T + n * (k - 4) + n])
            return flat.rearrange("p (j t) -> p j t", t=GT)
        hot1 = [spread_buffer(k) for k in range(2)]
        hot2g = [a.rearrange("p (f j t) -> p f j t", f=2, t=GT) for a in
                 (hs_half[:, 2 * NK * GT:4 * NK * GT], hT_half[:, 4 * T:4 * T + 2 * NK * GT])]
        spare = sb("spare", [P, NK * GT // 2])
        hot2 = [spread_buffer(6), spare[:, :].bitcast(F16).rearrange("p (j t) -> p j t", t=GT)]
        small = sb("small", [P, 256])
        ps = ctx.enter_context(nc.psum_tensor("ps", [P, 8, 512], F32))

        def bg(off, n):
            return big[:, off:off + n]

        loaded = [sem(f"loaded{k}") for k in range(RING)]
        scaled = sem("scaled")
        hi_ready = sem("hi_ready")
        lo_dve = sem("lo_dve")
        lo_pool = sem("lo_pool")
        used = sem("used")
        hs_hi = sem("hs_hi")
        hs_lo = sem("hs_lo")
        s_const = sem("s_const")
        s_x = sem("s_x")
        s_par = sem("s_par")
        s_keys = sem("s_keys")
        out_y = [sem(f"out_y{k}") for k in range(2)]
        out_s5 = sem("out_s5")
        out_hgp = sem("out_hgp")
        out_hgs = sem("out_hgs")
        dv = sem("dv")
        x_ready = sem("x_ready")
        norm_sq = sem("norm_sq")
        norm_ss = sem("norm_ss")
        norm_std = sem("norm_std")
        norm_h = sem("norm_h")

        block = ctx.enter_context(nc.Block())

        def zbank(k):
            return ps[:, 4 + k, 0:T]

        def lo_done(eng, name, i, k):
            lo_half_done(eng, name, i, k, 1)

        def lo_half_done(eng, name, i, k, h):
            eng.wait_ge(lo_pool if name in BY_POOL else lo_dve, i * 2 * RING + (2 * (LO_FIRST[name] + k) + h + 1))

        def block_used(eng, name, i, k):
            eng.wait_ge(used, i * 2 * RING + 2 * (FIRST[name] + k + 1))

        def stream_segment(sp, name, before):
            src, trips = t_in[name], N_BLOCKS[name] // RING

            def load(i, k):
                sp.dma_start(ring[:, k, :], src[i * RING + k]).then_inc(loaded[k], 16)
            for k in range(RING):
                if before:
                    lo_done(sp, before, N_BLOCKS[before] // RING - 1, k)
                load(0, k)
            with sp.Fori(1, trips) as i:
                for k in range(RING):
                    lo_done(sp, name, i - 1, k)
                    load(i, k)

        HALF = BLK // 2

        def split_hi(act, name, i, k):
            i, k = (i, k) if k < RING else (i + 1, k - RING)
            n0 = FIRST[name]
            act.wait_ge(loaded[k], i * 16 + 16 * (n0 // RING + 1))
            scale = SC
            if name in BY_POOL:
                nc.scalar.activation(ring[:, k, :], ring[:, k, :], ACT.Copy, scale=SC).then_inc(scaled, 1)
                act.wait_ge(scaled, i * RING + (LO_FIRST[name] + k + 1))
                scale = 1.0
            for h in range(2):
                if not (n0 == 0 and isinstance(i, int) and i == 0 and k < 2):
                    act.wait_ge(used, i * 2 * RING + (2 * (n0 + k) - 3 + h))
                cols = slice(h * HALF, (h + 1) * HALF)
                nc.scalar.activation(wsp[:, k % 2, 0, cols], ring[:, k, cols], ACT.Copy,
                                     scale=scale).then_inc(hi_ready, 1)

        def split_lo(eng, name, i, k):
            i, k = (i, k) if k < RING else (i + 1, k - RING)
            for h in range(2):
                eng.wait_ge(hi_ready, i * 2 * RING + (2 * (FIRST[name] + k) + h + 1))
                cols = slice(h * HALF, (h + 1) * HALF)
                hi, lo, w = wsp[:, k % 2, 0, cols], wsp[:, k % 2, 1, cols], ring[:, k, cols]
                if name in BY_POOL:
                    nc.gpsimd.tensor_tensor(lo, w, hi, ALU.subtract).then_inc(lo_pool, 1)
                else:
                    nc.vector.scalar_tensor_tensor(out=lo, in0=w, scalar=SC, in1=hi, op0=ALU.mult,
                                                   op1=ALU.subtract).then_inc(lo_dve, 1)

        def split_pool(g, name):
            with g.Fori(0, N_BLOCKS[name] // RING) as i:
                for k in range(RING):
                    split_lo(g, name, i, k)

        def per_block(eng, name, split, post, a=0, b=None, ahead=0, following=()):
            trips = N_BLOCKS[name] // RING
            b = trips if b is None else b

            def body(i, first, last):
                for k in range(RING):
                    if split and not (last and k >= 2):
                        split(eng, name, i, k + 2)
                    elif split and k - 2 < len(following):
                        split(eng, following[k - 2], 0, k - 2)
                    post(i, k, first)
            if split and a == 0:
                for k in range(ahead, 2):
                    split(eng, name, 0, k)
            if a == 0:
                body(0, True, trips == 1)
                a = 1
            end = b - 1 if b == trips else b
            if a + 1 == end:
                body(a, False, False)
            elif a < end:
                with eng.Fori(a, end) as i:
                    body(i, False, False)
            if b == trips and a < b:
                body(trips - 1, False, True)

        def three_passes(out, slot, c, hi, lo, start, stop, **kw):
            w_hi, w_lo = (wsp[:, slot, f, c * P:(c + 1) * P] for f in range(2))
            nc.tensor.matmul(out, w_hi, hi, start=start, stop=False, **kw)
            nc.tensor.matmul(out, w_hi, lo, start=False, stop=False, **kw)
            return nc.tensor.matmul(out, w_lo, hi, start=False, stop=stop, **kw)

        def project(pe, name, wait_bank, after=None, a=0, b=None, inputs=None):
            def post(i, k, first):
                wait_bank(i, k, first)
                for c in range(KC):
                    if inputs is not None and first and k == 0:
                        pe.wait_ge(hs_lo, KC * inputs + c + 1)
                    if c % 4 == 0:
                        lo_half_done(pe, name, i, k, c // 4)
                    mm = three_passes(zbank(k), k % 2, c, hs[:, 0, c, :], hs[:, 1, c, :], c == 0, c == KC - 1)
                    if c % 4 == 3:
                        mm.then_inc(used, 1)
                if after:
                    after(i, k, first)
            per_block(pe, name, None, post, a, b)

        def high_part(c):
            return nc.scalar.activation(hs[:, 0, c, :], hT[:, c, :], ACT.Copy, scale=SC)

        def low_part(c):
            return nc.vector.scalar_tensor_tensor(out=hs[:, 1, c, :], in0=hT[:, c, :], scalar=SC,
                                                  in1=hs[:, 0, c, :], op0=ALU.mult, op1=ALU.subtract)

        def x_chunk(eng, k, c):
            if k == 0:
                eng.wait_ge(s_x, 16)
            elif k == 1:
                eng.wait_ge(glu_x, c + 1)
            elif k == 3:
                eng.wait_ge(hg_x, c + 1)
            else:
                eng.wait_ge(pacc[k // 2 - 1], sum(len(ACC[m]) for m in range(c + 1)))

        def square(c):
            return bg(T * c, T)

        def norm_bank(k):
            return ps[:, 6 if k in (2, 4) else 0, 0:T]

        def norm_act(act, k, following=None):
            nc.scalar.activation(small[:, 176 + k:177 + k], epsc[:, 0:1], ACT.Sqrt)
            for c in range(KC):
                x_chunk(act, k, c)
                nc.scalar.activation(square(c), xT[:, c, :], ACT.Square).then_inc(norm_sq, 1)
            act.wait_ge(norm_ss, k + 1)
            nc.scalar.activation(std[:, :], norm_bank(k), ACT.Sqrt, bias=epsc[:, 0:1],
                                 scale=1.0 / D).then_inc(norm_std, 1)
            if following:
                split_hi(act, following, 0, 1)
            if 0 < k < 4:
                for c in range(KC):
                    act.wait_ge(norm_h, KC * k + c + 1)
                    high_part(c).then_inc(hs_hi, 1)

        def norm_pe(pe, k):
            for c in range(KC):
                pe.wait_ge(norm_sq, KC * k + c + 1)
                mm = nc.tensor.matmul(norm_bank(k), ones[:, :], square(c), start=(c == 0), stop=(c == KC - 1))
            mm.then_inc(norm_ss, 1)

        def norm_dve(v, cnt, k):
            v.wait_ge(norm_std, k + 1)
            cnt.link(nc.vector.reciprocal(std[:, :], std[:, :]))
            before = {1: 1, 2: 2, 3: 4}.get(k)

            def low(c):
                v.wait_ge(hs_hi, before * KC + c + 1)
                low_part(c).then_inc(hs_lo, 1)
            for c in range(KC):
                nc.vector.scalar_tensor_tensor(out=hT[:, c, :], in0=xT[:, c, :], scalar=normw[:, k, c:c + 1],
                                               in1=std[:, :], op0=ALU.mult, op1=ALU.mult).then_inc(norm_h, 1)
                if before and c >= 2:
                    low(c - 2)
            if before:
                low(KC - 2)
                low(KC - 1)

        ST = bg(0, 2 * PAIRS * T).rearrange("p (r q t) -> p r q t", r=2, q=PAIRS)
        TMPW = 2 * PAIRS * T
        DIAG = QC * (P + 2 * GH)
        TAB = [bg(TMPW + 8192 * k, 8192).rearrange("p (r q t) -> p r q t", r=2, q=PAIRS) for k in range(2)]
        bbar = bg(34816, 1024).rearrange("p (r n) -> p r n", r=2)
        craw = bg(35840, 1024).rearrange("p (r n) -> p r n", r=2)
        s5w = hs_half.bitcast(F32)[:, 0:2 * PAIRS * GH].rearrange("p (r n) -> p r n", r=2)
        bdiag = [a.rearrange("p (r m) -> p r m", r=2) for a in
                 (hs_half.bitcast(F32)[:, 2 * PAIRS * GH:2 * PAIRS * GH + 2 * DIAG],
                  wsp[:, :, :, :].rearrange("p a f n -> p (a f n)").bitcast(F32)[:, 0:2 * DIAG])]
        w0 = TMPW

        def s5_take(n):
            nonlocal w0
            w0 += n
            return bg(w0 - n, n)

        def s5_pair():
            return s5_take(2 * TP).rearrange("p (r t) -> p r t", r=2)

        btr = [a.rearrange("p (r m) -> p r m", r=2) for a in (hs_half.bitcast(F32)[:, 0:1024], s5_take(1024))]
        cdiag = [s5_take(3 * DIAG).rearrange("p (r m) -> p r m", r=3) for _ in range(2)]
        prod = [[s5_pair() for _ in range(2)] for _ in range(2)]
        zin = [s5_pair() for _ in range(2)]
        zsc = [s5_pair() for _ in range(2)]
        pout = [[s5_pair() for _ in range(2)] for _ in range(4)]
        s0 = s5_take(2 * PAIRS * NB).rearrange("p (r q b) -> p r q b", r=2, q=PAIRS)
        sa = [s5_take(2 * PAIRS * NB).rearrange("p (r q b) -> p r q b", r=2, q=PAIRS) for _ in range(2)]
        fin5 = s5_take(2 * PAIRS * 9).rearrange("p (r q b) -> p r q b", r=2, q=PAIRS)
        zend = s5_take(2 * PAIRS).rearrange("p (r q) -> p r q", r=2)
        zx = s5_take(4 * PAIRS).rearrange("p (m q) -> p m q", m=4)
        assert w0 <= 34816
        par = sb("par", [P, 16, PAIRS])
        dcol = sb("dcol", [P, KC])
        PR = {n: par[:, i, :] for i, n in enumerate(
            ["lr", "li", "dt", "mag", "ang", "c", "s", "ar", "ai", "zr", "zi", "t0", "t1", "t2", "t3", "t4"])}

        s5_in = sem("s5_in")
        s5_s0 = sem("s5_s0")
        s5_exp = sem("s5_exp")
        s5_arg = sem("s5_arg")
        s5_par = sem("s5_params")
        s5_tab_add = sem("s5_tab_add")
        s5_tab_addv = sem("s5_tab_addv")
        s5_tab_mul = sem("s5_tab_mul")
        s5_tab_act = sem("s5_tab_act")
        s5_sqr = sem("s5_squared")
        s5_zb = sem("s5_zero_b")
        s5_zc = sem("s5_zero_c")
        s5_db = sem("s5_diag_b")
        s5_dc = sem("s5_diag_c")
        s5_tr = sem("s5_tr")
        s5_trc = sem("s5_trc")
        s5_bu = sem("s5_bu")
        s5_smp = sem("s5_smp")
        s5_min = sem("s5_min")
        s5_ain = sem("s5_ain")
        s5_scan = sem("s5_scan")
        s5_end = sem("s5_end")
        s5_mout = sem("s5_mout")
        s5_pout = sem("s5_pout")
        s5_cs = sem("s5_cs")
        s5_yp = sem("s5_yp")
        s5_rec = sem("s5_rec")
        s5_y = sem("s5_y")
        s5_yd = sem("s5_yd")
        s5_g = sem("s5_g")
        s5_fin = sem("s5_fin")

        def s5_params_act(act):
            act.wait_ge(s5_in, 16 * 6)
            nc.scalar.activation(PR["dt"], PR["dt"], ACT.Exp).then_inc(s5_exp, 1)
            act.wait_ge(s5_arg, 1)
            nc.scalar.activation(PR["mag"], PR["t0"], ACT.Exp).then_inc(s5_exp, 1)

        def s5_params_dve(v, cnt):
            tt, ts = nc.vector.tensor_tensor, nc.vector.tensor_scalar
            L = cnt.link
            v.wait_ge(s5_in, 16 * 6)
            stt = nc.vector.scalar_tensor_tensor

            def fused(out, a, scalar, b, op0, op1):
                return stt(out=PR[out], in0=PR[a], scalar=scalar, in1=PR[b], op0=op0, op1=op1)

            def tp(out, a, b, op):
                return tt(PR[out], PR[a], PR[b], op)
            A, M, S = ALU.add, ALU.mult, ALU.subtract
            cnt.add(ts(craw[:, 1, :], craw[:, 1, :], -1.0, None, M))
            L(ts(PR["lr"], PR["lr"], -1e-4, None, ALU.min))
            cnt.add(tp("t4", "lr", "lr", M))
            L(tp("zr", "li", "li", M))
            v.wait_ge(s5_exp, 1)
            tp("t0", "lr", "dt", M).then_inc(s5_arg, 1)
            cnt.add(tp("t4", "t4", "zr", A))
            L(tp("ang", "li", "dt", M))
            rnd = 1.5 * 2.0 ** 23
            cnt.add(nc.vector.reciprocal(PR["t4"], PR["t4"]))
            L(ts(PR["t1"], PR["ang"], 1.0 / (2 * np.pi), rnd, M, A))
            L(ts(PR["t1"], PR["t1"], rnd, None, S))
            whole = 2 * np.pi
            for part in (6.28125, float(np.float32(whole - 6.28125)),
                         float(whole - 6.28125 - np.float64(np.float32(whole - 6.28125)))):
                L(fused("ang", "t1", -part, "ang", M, A))
            L(ts(PR["t1"], PR["ang"], 0.125, None, M))
            L(tp("t2", "t1", "t1", M))
            cnt.add(ts(PR["s"], PR["t2"], 1.0 / 362880, None, M))
            L(ts(PR["c"], PR["t2"], -1.0 / 3628800, None, M))
            for a, b in ((-1.0 / 5040, 1.0 / 40320), (1.0 / 120, -1.0 / 720), (-1.0 / 6, 1.0 / 24), (1.0, -0.5)):
                cnt.add(fused("s", "s", a, "t1" if a == 1.0 else "t2", A, M))
                L(fused("c", "c", b, "t2", A, M))
            for old, new in (("c", "t2"), ("t2", "c"), ("c", "t2")):
                cnt.add(fused("t3", "s", 2.0, old, M, M))
                L(fused(new, "s", -2.0, "s", M, M))
                L(fused("s", "s", 2.0, "t3", M, A))
            L(ts(PR["c"], PR["t2"], 1.0, None, A))
            v.wait_ge(s5_exp, 2)
            cnt.add(tp("ar", "mag", "c", M))
            L(tp("ai", "mag", "s", M))
            cnt.add(tp("t2", "ai", "li", M))
            cnt.add(tp("t3", "ai", "lr", M))
            L(ts(PR["t0"], PR["ar"], -1.0, None, A))
            cnt.add(tp("zr", "t0", "lr", M))
            L(tp("zi", "t0", "li", M))
            cnt.add(tp("zr", "zr", "t2", A))
            L(tp("zi", "t3", "zi", S))
            cnt.add(tp("zr", "zr", "t4", M))
            L(tp("zi", "zi", "t4", M))
            sh = [P, PAIRS, GH]
            zr, zi = (PR[n][:, :, None].to_broadcast(sh) for n in ("zr", "zi"))
            w3 = [s5w[:, r, :].rearrange("p (q h) -> p q h", q=PAIRS) for r in range(2)]
            b3 = [bbar[:, r, :].rearrange("p (q h) -> p q h", q=PAIRS) for r in range(2)]
            u3 = [bg(TMPW + 512 * k, 512).rearrange("p (q h) -> p q h", q=PAIRS) for k in range(4)]
            cnt.add(tt(u3[0], zr, w3[0], ALU.mult))
            cnt.add(tt(u3[1], zi, w3[1], ALU.mult))
            cnt.add(tt(u3[2], zr, w3[1], ALU.mult))
            L(tt(u3[3], zi, w3[0], ALU.mult))
            cnt.add(tt(b3[0], u3[0], u3[1], ALU.subtract))
            L(tt(b3[1], u3[2], u3[3], ALU.add))
            v.sem_inc(s5_par, 1)

        HQ = PAIRS // 2
        AG = 7
        AQ = 2 * AG
        NARROW, WIDE, LEVELS = 4, 6, 8

        def tab_mul_before(lev):
            return 4 * (lev - NARROW)

        def tab_add_before(lev):
            return 2 * (min(lev, WIDE) - NARROW) + 6 * max(lev - WIDE, 0)

        def table_sums(eng, q, w, done):
            done(eng.tensor_tensor(ST[:, 0, q, w:2 * w], TAB[0][:, 0, q, 0:w], TAB[1][:, 1, q, 0:w], ALU.subtract))
            done(eng.tensor_tensor(ST[:, 1, q, w:2 * w], TAB[0][:, 1, q, 0:w], TAB[1][:, 0, q, 0:w], ALU.add))

        def s5_table_dve(v, cnt):
            tt = nc.vector.tensor_tensor
            L = cnt.link
            cnt.add(nc.vector.memset(ST[:, 0, :, 0:1], 1.0))
            L(nc.vector.memset(ST[:, 1, :, 0:1], 0.0))
            cs = (PR["c"], PR["s"])

            def products(q, w):
                for k in range(2):
                    sh = [P, 2, q.stop - q.start, w]
                    yield tt(TAB[k][:, :, q, 0:w], ST[:, :, q, 0:w], cs[k][:, None, q, None].to_broadcast(sh), ALU.mult)
            for lev in range(LEVELS):
                w = 1 << lev
                if lev < NARROW:
                    for ins in products(slice(0, PAIRS), w):
                        cnt.add(ins)
                    cnt.wait()
                    table_sums(nc.vector, slice(0, PAIRS), w, cnt.add)
                else:
                    for half in range(2):
                        q = slice(HQ * half, HQ * half + HQ)
                        if half == 0 and lev >= WIDE:
                            q = slice(AQ, HQ)
                        if lev > NARROW:
                            if half:
                                v.wait_ge(s5_tab_addv, 2 * (lev - NARROW))
                            else:
                                v.wait_ge(s5_tab_add, tab_add_before(lev))
                        for ins in products(q, w):
                            ins.then_inc(s5_tab_mul, 1)
                    v.wait_ge(s5_tab_mul, tab_mul_before(lev + 1))
                    table_sums(nc.vector, q, w, lambda ins: ins.then_inc(s5_tab_addv, 1))
                if lev < LEVELS - 1:
                    cnt.add(tt(PR["t0"], cs[0], cs[0], ALU.mult))
                    cnt.add(tt(PR["t1"], cs[1], cs[1], ALU.mult))
                    L(nc.vector.scalar_tensor_tensor(out=PR["t2"], in0=cs[0], scalar=2.0, in1=cs[1], op0=ALU.mult,
                                                     op1=ALU.mult))
                    if lev >= WIDE:
                        v.wait_ge(s5_tab_act, 2 * AQ * (lev - WIDE + 1))
                    tt(cs[0], PR["t0"], PR["t1"], ALU.subtract).then_inc(s5_sqr, 1)
                    nc.vector.tensor_copy(cs[1], PR["t2"]).then_inc(s5_sqr, 1)
                    v.wait_ge(s5_sqr, 2 * lev + 2)

        def s5_table_act(act):
            for lev in range(WIDE, LEVELS):
                w = 1 << lev
                act.wait_ge(s5_sqr, 2 * lev)
                act.wait_ge(s5_tab_add, tab_add_before(lev))
                for q in range(AQ):
                    for k in range(2):
                        nc.scalar.activation(TAB[k][:, :, q, 0:w], ST[:, :, q, 0:w], ACT.Copy,
                                             scale=PR["cs"[k]][:, q:q + 1]).then_inc(s5_tab_act, 1)

        def s5_table_pool(g):
            for x in range(2):
                nc.gpsimd.memset(bdiag[x], 0.0).then_inc(s5_zb, 1)

            def done(ins):
                ins.then_inc(s5_tab_add, 1)
            for lev in range(NARROW, LEVELS):
                w = 1 << lev
                g.wait_ge(s5_tab_mul, tab_mul_before(lev) + 2)
                if lev < WIDE:
                    table_sums(nc.gpsimd, slice(0, HQ), w, done)
                else:
                    table_sums(nc.gpsimd, slice(AQ, HQ), w, done)
                    for n in range(2):
                        g.wait_ge(s5_tab_act, 2 * (AQ * (lev - WIDE) + AG * (n + 1)))
                        table_sums(nc.gpsimd, slice(AG * n, AG * n + AG), w, done)
            table_done(g)
            for x in range(2):
                nc.gpsimd.memset(cdiag[x], 0.0).then_inc(s5_zc, 1)
            g.wait_ge(s5_zc, 2)

        def table_done(eng):
            eng.wait_ge(s5_tab_add, tab_add_before(LEVELS))
            eng.wait_ge(s5_tab_addv, 2 * (LEVELS - NARROW))

        def fill_diag(dst, src, c, done, scale=1.0):
            for g2 in range(2):
                rows = slice(64 * g2, 64 * g2 + 64)
                d = dst[rows, :, :].rearrange("p r (q m) -> p r q m", q=QC)[:, :, :, GH * g2:GH * g2 + GH]
                s = src[rows, :, ds(c * (QC * GH), QC * GH)].rearrange("p r (q h) -> p r q h", q=QC)
                nc.scalar.activation(d, s, ACT.Copy, scale=scale).then_inc(done, 1)

        def s5_trips(eng, body):
            body(0, True, False)
            with eng.Fori(1, 3) as i:
                body(i, False, False)
            body(3, False, True)

        def e_of(pair):
            return ST[:, :, ds(pair, 1), 0:TP].rearrange("p r o t -> p r (o t)")

        def s5_pairs_pool(g):
            sh = [P, 2, TP]

            def add_in(i, k, first):
                g.wait_ge(s5_min, i * 16 + 2 * k + 2)
                if not (first and k < 2):
                    g.wait_ge(s5_scan, i * 16 + 2 * (k - 2) + 2)
                nc.gpsimd.tensor_tensor(zin[k % 2][:, 0, :], prod[k % 2][0][:, 0, :], prod[k % 2][1][:, 1, :],
                                        ALU.add).then_inc(s5_ain, 1)
                nc.gpsimd.tensor_tensor(zin[k % 2][:, 1, :], prod[k % 2][1][:, 0, :], prod[k % 2][0][:, 1, :],
                                        ALU.subtract).then_inc(s5_ain, 1)

            def mul_out(i, k, first):
                g.wait_ge(s5_scan, i * 16 + 2 * k + 2)
                if not (first and k < 4):
                    g.wait_ge(s5_cs, i * 8 + k - 3)
                nc.gpsimd.tensor_tensor(pout[k % 4][1], zsc[k % 2][:, 1:2, :].to_broadcast(sh),
                                        e_of(i * 8 + k), ALU.mult).then_inc(s5_pout, 1)

            def body(i, first, last):
                for k in range(8):
                    add_in(i, k, first)
                    if k:
                        mul_out(i, k - 1, first)
                    elif not first:
                        mul_out(i - 1, 7, False)
            s5_trips(g, body)
            mul_out(3, 7, False)

        def s5_pairs_pe(pe):
            def transposes(i, x, first, r):
                pe.wait_ge(s5_db, i * 4 + 2 * x + 2)
                if not (first and x == 0):
                    pe.wait_ge(s5_trc, i * 4 + 2 * x)
                for q in range(QC):
                    mm = nc.tensor.transpose(ps[:, r, q * P:(q + 1) * P], bdiag[x][:, r, q * P:(q + 1) * P],
                                             ident[:, :])
                if r:
                    mm.then_inc(s5_tr, 1)

            def c_products(i, k, first):
                x, q = k // QC, k % QC
                if q == 0:
                    pe.wait_ge(s5_dc, i * 8 + 4 * x + 4)
                    if not first:
                        pe.wait_ge(s5_yp, i * 2 + x - 1)
                pe.wait_ge(s5_mout, i * 8 + k + 1)
                pe.wait_ge(s5_pout, i * 8 + k + 1)
                for m, (r, (a, b)) in enumerate(((0, (0, 0)), (1, (0, 1)), (2, (1, 1)), (1, (1, 0)))):
                    mm = nc.tensor.matmul(ps[:, 6 + x, 0:TP], cdiag[x][:, r, q * P:(q + 1) * P],
                                          pout[k % 4][a][:, b, :], start=(q == 0 and m == 0),
                                          stop=(q == QC - 1 and m == 3))
                mm.then_inc(s5_cs, 1)

            for r in range(2):
                transposes(0, 0, True, r)
            pe.wait_ge(norm_h, KC)

            def body(i, first, last):
                for k in range(8):
                    x = k // QC
                    if k % QC == 0:
                        pe.wait_ge(s5_trc, i * 4 + 2 * x + 2)
                    if not (first and k < 2):
                        pe.wait_ge(s5_min, i * 16 + 2 * (k - 2) + 2)
                        pe.wait_ge(s5_smp, i * 8 + k - 1)
                    for r in range(2):
                        mm = nc.tensor.matmul(ps[:, 2 + 2 * (k % 2) + r, 0:T],
                                              btr[x][:, r, (k % QC) * P:(k % QC + 1) * P],
                                              hT[:, ds(i * 2 + x, 1), :].rearrange("p o t -> p (o t)"),
                                              start=True, stop=True)
                    mm.then_inc(s5_bu, 1)
                    if k >= 3:
                        c_products(i, k - 3, first)
                    elif not first:
                        c_products(i - 1, 5 + k, False)
                    if k in (1, 2):
                        transposes(i, 1, first, k - 1)
                    elif k in (5, 6) and not last:
                        transposes(i + 1, 0, False, k - 5)
            s5_trips(pe, body)
            c_products(3, 5, False)
            c_products(3, 6, False)
            c_products(3, 7, False)

        def s5_pairs_act(act):
            act.wait_ge(s5_par, 1)
            act.wait_ge(s5_zb, 2)

            def fill_b(i, x, first):
                if not first:
                    act.wait_ge(s5_tr, i * 2 + x - 1)
                fill_diag(bdiag[x], bbar, i * 2 + x, s5_db)

            def copy_b(i, x, first):
                act.wait_ge(s5_tr, i * 2 + x + 1)
                if not first:
                    act.wait_ge(s5_bu, i * 8 + x * 4 - 4)
                for r in range(2):
                    nc.scalar.activation(btr[x][:, r, :], ps[:, r, :], ACT.Copy).then_inc(s5_trc, 1)

            def end_of(i, k):
                act.wait_ge(s5_scan, i * 16 + 2 * k + 2)
                nc.scalar.activation(zend[:, :, ds(i * 8 + k, 1)], zsc[k % 2][:, :, TP - 1:TP],
                                     ACT.Copy).then_inc(s5_end, 1)

            fill_b(0, 0, True)
            copy_b(0, 0, True)
            s5_table_act(act)


            def body(i, first, last):
                for k in range(8):
                    x, q = k // QC, k % QC
                    act.wait_ge(s5_bu, i * 8 + k + 1)
                    nc.scalar.activation(
                        ST[:, :, ds(i * 8 + k, 1), TP:T].rearrange("p r o t -> p r (o t)"),
                        ps[:, 2 + 2 * (k % 2):4 + 2 * (k % 2), TP:T], ACT.Copy).then_inc(s5_smp, 1)
                    if k >= 2:
                        end_of(i, k - 2)
                    elif not first:
                        end_of(i - 1, 6 + k)
                    nxt = (i, 1, first) if x == 0 else (i + 1, 0, False)
                    if q == 0 and not (x and last):
                        fill_b(*nxt)
                    elif q == 1:
                        if not first:
                            act.wait_ge(s5_cs, i * 8 + 4 * x - 4)
                        elif x == 0:
                            act.wait_ge(s5_zc, 2)
                        fill_diag(cdiag[x][:, 0:2, :], craw, i * 2 + x, s5_dc)
                        fill_diag(cdiag[x][:, 2:3, :], craw[:, 0:1, :], i * 2 + x, s5_dc, scale=-1.0)
                    elif q == 3 and not (x and last):
                        copy_b(*nxt)
            s5_trips(act, body)
            end_of(3, 6)
            end_of(3, 7)

        def s5_pairs_dve(v, cnt):
            table_done(v)
            sh = [P, 2, TP]

            def mul_in(i, k, first):
                v.wait_ge(s5_smp, i * 8 + k + 1)
                if not (first and k < 2):
                    v.wait_ge(s5_ain, i * 16 + 2 * (k - 2) + 2)
                for m in range(2):
                    nc.vector.tensor_tensor(prod[k % 2][m], ps[:, 2 + 2 * (k % 2) + m, None, 0:TP].to_broadcast(sh),
                                            e_of(i * 8 + k), ALU.mult).then_inc(s5_min, 1)

            def scan_out(i, k, first):
                pair = i * 8 + k
                v.wait_ge(s5_ain, i * 16 + 2 * k + 2)
                if not (first and k < 2):
                    v.wait_ge(s5_mout, i * 8 + k - 1)
                    v.wait_ge(s5_pout, i * 8 + k - 1)
                    v.wait_ge(s5_end, i * 8 + k - 1)
                for r in range(2):
                    nc.vector.tensor_tensor_scan(zsc[k % 2][:, r, :], PR["mag"][:, ds(pair, 1)].to_broadcast([P, TP]),
                                                 zin[k % 2][:, r, :], 0.0, ALU.mult, ALU.add).then_inc(s5_scan, 1)
                v.wait_ge(s5_scan, i * 16 + 2 * k + 2)
                if not (first and k < 4):
                    v.wait_ge(s5_cs, i * 8 + k - 3)
                nc.vector.tensor_tensor(pout[k % 4][0], zsc[k % 2][:, 0:1, :].to_broadcast(sh),
                                        e_of(pair), ALU.mult).then_inc(s5_mout, 1)

            def y_prompt(i, x):
                v.wait_ge(s5_cs, i * 8 + 4 * x + 4)
                u = hT[:, ds(i * 2 + x, 1), 0:TP].rearrange("p o t -> p (o t)")
                nc.vector.scalar_tensor_tensor(out=u, in0=u, scalar=dcol[:, ds(i * 2 + x, 1)],
                                               in1=ps[:, 6 + x, 0:TP], op0=ALU.mult, op1=ALU.add).then_inc(s5_yp, 1)

            def body(i, first, last):
                for k in range(8):
                    mul_in(i, k, first)
                    if k:
                        scan_out(i, k - 1, first)
                    elif not first:
                        scan_out(i - 1, 7, False)
                    if k % QC == 0 and not first:
                        y_prompt(i - 1, k // QC)
                    if last and k % 2:
                        s5_sample_step(v, cnt, 0, k // 2)
            s5_trips(v, body)
            scan_out(3, 7, False)
            y_prompt(3, 0)

        def s5_sample_step(v, cnt, half, s):
            tt = nc.vector.tensor_tensor
            q = slice(HQ * half, HQ * half + HQ)
            smp = ST[:, :, q, TP:T].rearrange("p r q (b s) -> p r q b s", b=NB)
            if s == 0:
                v.wait_ge(s5_smp, HQ * half + HQ)
                v.wait_ge(s5_s0, 16)
            else:
                v.wait_ge(s5_rec, 8 * half + 2 * s)
            arb, aib = (PR[n][:, q, None].to_broadcast([P, HQ, NB]) for n in ("ar", "ai"))
            prev = [s0[:, r, q] if s == 0 else smp[:, r, :, :, s - 1] for r in range(2)]
            cnt.add(tt(sa[0][:, 0, q], arb, prev[0], ALU.mult))
            cnt.add(tt(sa[0][:, 1, q], arb, prev[1], ALU.mult))
            cnt.add(tt(sa[1][:, 0, q], aib, prev[1], ALU.mult))
            cnt.link(tt(sa[1][:, 1, q], aib, prev[0], ALU.mult))
            cnt.add(tt(sa[0][:, 0, q], sa[0][:, 0, q], sa[1][:, 0, q], ALU.subtract))
            cnt.link(tt(sa[0][:, 1, q], sa[0][:, 1, q], sa[1][:, 1, q], ALU.add))
            for r in range(2):
                tt(smp[:, r, :, :, s], smp[:, r, :, :, s], sa[0][:, r, q], ALU.add).then_inc(s5_rec, 1)

        def s5_samples_dve(v, cnt):
            tt = nc.vector.tensor_tensor
            smp = ST[:, :, :, TP:T].rearrange("p r q (b s) -> p r q b s", b=NB)
            for s in range(LS):
                s5_sample_step(v, cnt, 1, s)
            for k in range(2):
                split_lo(v, "glu", 0, k)
            v.wait_ge(s5_cs, PAIRS)
            nc.vector.scalar_tensor_tensor(
                out=hT[:, KC - 1, 0:TP], in0=hT[:, KC - 1, 0:TP], scalar=dcol[:, KC - 1:KC],
                in1=ps[:, 7, 0:TP], op0=ALU.mult, op1=ALU.add).then_inc(s5_yp, 1)
            s5_out_dve(v)
            v.wait_ge(s5_end, PAIRS)
            er, ei = (ST[:, r, :, TP - 1:TP].rearrange("p q o -> p (q o)") for r in range(2))
            for m, (a, b) in enumerate(((er, 0), (ei, 1), (ei, 0), (er, 1))):
                cnt.add(tt(zx[:, m], a, zend[:, b], ALU.mult))
            cnt.wait()
            v.wait_ge(s5_rec, 16)
            for r, op in enumerate((ALU.subtract, ALU.add)):
                tt(fin5[:, r, :, 0:1], zx[:, 2 * r, :, None], zx[:, 2 * r + 1, :, None], op).then_inc(s5_fin, 1)
                nc.vector.tensor_copy(fin5[:, r, :, 1:9], smp[:, r, :, :, LS - 1]).then_inc(s5_fin, 1)

        def s5_out_pe(pe):
            pe.wait_ge(s5_min, 2 * PAIRS)
            pe.wait_ge(s5_smp, PAIRS)
            for c in range(KC):
                if c % (KC // 2) == 0:
                    pe.wait_ge(s5_rec, 8 if c == 0 else 16)
                pe.wait_ge(s5_dc, 4 * KC + 2 * c + 2)
                if c >= 4:
                    pe.wait_ge(s5_yd, c - 3)
                for q in range(QC):
                    for r in range(2):
                        mm = nc.tensor.matmul(ps[:, 2 + c % 4, 0:TS], cdiag[c % 2][:, r, q * P:(q + 1) * P],
                                              ST[:, r, c * QC + q, TP:T],
                                              start=(q == 0 and r == 0), stop=(q == QC - 1 and r == 1))
                mm.then_inc(s5_y, 1)

        def s5_out_dve(v):
            for c in range(KC):
                v.wait_ge(s5_y, c + 1)
                nc.vector.scalar_tensor_tensor(out=hT[:, c, TP:T], in0=hT[:, c, TP:T], scalar=dcol[:, c:c + 1],
                                               in1=ps[:, 2 + c % 4, 0:TS], op0=ALU.mult,
                                               op1=ALU.add).then_inc(s5_yd, 1)

        def s5_out_act(act):
            for k in range(2):
                split_hi(act, "glu", 0, k)
            for c in range(KC + 4):
                if c < KC:
                    if c < 2:
                        act.wait_ge(s5_cs, 28 + 4 * c)
                    else:
                        act.wait_ge(s5_y, c - 1)
                    fill_diag(cdiag[c % 2][:, 0:2, :], craw, c, s5_dc)
                if c >= 4:
                    act.wait_ge(s5_yp, c - 3)
                    act.wait_ge(s5_yd, c - 3)
                    nc.scalar.activation(hT[:, c - 4, :], hT[:, c - 4, :], ACT.Gelu).then_inc(s5_g, 1)
            for c in range(KC):
                act.wait_ge(s5_g, c + 1)
                high_part(c).then_inc(hs_hi, 1)

        sig = [bg(TMPW + T * k, T) for k in range(2)]
        gated = [bg(TMPW + 2 * T + T * k, T) for k in range(2)]
        glu_sig = sem("glu_sig")
        glu_mul = sem("glu_mul")
        glu_x = sem("glu_x")

        def glu_pe(pe):
            pe.wait_ge(s5_min, 2 * PAIRS)

            def free(i, k, first):
                if k % 2 == 0 and not first:
                    pe.wait_ge(glu_mul, i * 2 + k // 2 - 1)

            project(pe, "glu", free, inputs=0)

        def glu_act(act):
            act.wait_ge(s5_y, KC)

            def post(i, k, first):
                if k % 2:
                    m = k // 2
                    block_used(act, "glu", i, k)
                    if not first:
                        act.wait_ge(glu_mul, i * 2 + m - 1)
                    nc.scalar.activation(sig[m], zbank(k), ACT.Sigmoid, scale=UNSC).then_inc(glu_sig, 1)
            per_block(act, "glu", split_hi, post, ahead=2, following=["wq0"])

        def glu_dve(v):
            for c in range(KC):
                v.wait_ge(hs_hi, c + 1)
                low_part(c).then_inc(hs_lo, 1)

            def post(i, k, first):
                if k % 2:
                    m = k // 2
                    v.wait_ge(glu_sig, i * 2 + m + 1)
                    if not first:
                        v.wait_ge(glu_x, i * 2 + m - 1)
                    nc.vector.scalar_tensor_tensor(out=gated[m], in0=zbank(k - 1), scalar=UNSC, in1=sig[m],
                                                   op0=ALU.mult, op1=ALU.mult).then_inc(glu_mul, 1)
                    v.wait_ge(glu_mul, i * 2 + m + 1)
                    x = xT[:, ds(i * 2 + m, 1), :].rearrange("p o t -> p (o t)")
                    nc.vector.tensor_tensor(x, x, gated[m], ALU.add).then_inc(glu_x, 1)
            per_block(v, "glu", split_lo, post, ahead=2)
            v.wait_ge(glu_x, KC)
            v.sem_inc(x_ready, 1)

        act3 = big[:, :].rearrange("p (j t) -> p j t", j=NK)
        UT = (UB - UA) // RING
        o = UB * T

        def take(n, dt=None):
            nonlocal o
            a = bg(o, n)
            o += n
            return a.bitcast(dt) if dt else a

        NS = 3 * NK
        score = bg(UA * T, 2 * PH * NS).rearrange("p (b n) -> p b n", b=2 * PH)
        assert UA * T + 2 * PH * NS <= UB * T
        ksp = take(2 * NK).bitcast(F16).rearrange("p (f n k) -> p f n k", f=2, n=2)
        val = take(768).rearrange("p (j f h k) -> p j f h k", j=3, f=2, h=PH)
        idu = take(768, U32).rearrange("p (j f h k) -> p j f h k", j=3, f=2, h=PH)
        idf = take(768).rearrange("p (j f h k) -> p j f h k", j=3, f=2, h=PH)
        rest = [take(NK) for _ in range(3)]
        cand = take(PH * NC_).rearrange("p (h n) -> p h n", h=PH)
        cidx = take(PH * NC_).rearrange("p (h n) -> p h n", h=PH)
        rest2 = [take(NC_) for _ in range(2)]
        sc = take(3 * P).rearrange("p (j h k) -> p j h k", j=3, h=PH)
        gate = take(3 * P).rearrange("p (j h k) -> p j h k", j=3, h=PH)
        posu = take(P, U32).rearrange("p (h k) -> p h k", h=PH)
        posf = take(P).rearrange("p (h k) -> p h k", h=PH)
        eq = [take(TK * NC_).rearrange("p (k n) -> p k n", k=TK) for _ in range(2)]
        eid = take(3 * P).rearrange("p (j n) -> p j n", j=3)
        eii = take(3 * P, I32).rearrange("p (j n) -> p j n", j=3)
        e12i = take(6 * P, I32).rearrange("p (j f n) -> p j f n", j=3, f=2)
        e12 = take(6 * P).rearrange("p (j f n) -> p j f n", j=3, f=2)
        sm = take(3 * PH).rearrange("p (j h) -> p j h", j=3)
        rs = take(3 * PH).rearrange("p (j h) -> p j h", j=3)
        assert o <= NK * T
        pq = [sem(f"peer_q{L}") for L in range(2)]
        pkh = [sem(f"peer_key_hi{L}") for L in range(2)]
        pkl = [sem(f"peer_key_lo{L}") for L in range(2)]
        pql = [sem(f"peer_q_lo{L}") for L in range(2)]
        pss = [sem(f"peer_scores_out{L}") for L in range(2)]
        psc = [sem(f"peer_scores{L}") for L in range(2)]
        pge = [sem(f"peer_gelu{L}") for L in range(2)]
        psh = [sem(f"peer_shift{L}") for L in range(2)]
        pex = [sem(f"peer_exp{L}") for L in range(2)]
        pgt = [sem(f"peer_gate{L}") for L in range(2)]
        ptr = [sem(f"peer_tr{L}") for L in range(2)]
        ptc = [sem(f"peer_trc{L}") for L in range(2)]
        poh = [sem(f"peer_onehot{L}") for L in range(2)]
        pe2 = [sem(f"peer_equal{L}") for L in range(2)]
        pdf = [sem(f"peer_diff{L}") for L in range(2)]
        pab = [sem(f"peer_abs{L}") for L in range(2)]
        phA = [sem(f"peer_hot1_{L}") for L in range(2)]
        pG = [sem(f"peer_G{L}") for L in range(2)]
        pmul = [sem(f"peer_mul{L}") for L in range(2)]
        pacc = [sem(f"peer_acc{L}") for L in range(2)]
        pah = [sem(f"peer_act_hi{L}") for L in range(2)]
        pal = [sem(f"peer_act_lo{L}") for L in range(2)]

        def peer_query_pe(pe, L):

            def scores(i, k, first):
                pe.wait_ge(pq[L], i * 8 + 2 * k + 2)
                pe.wait_ge(pql[L], i * 4 + k + 1)
                if first and k == 0:
                    pe.wait_ge(pkl[L], 1)
                if not (first and k < 2):
                    pe.wait_ge(pss[L], i * 4 + k - 1)
                for j, (t0, w) in enumerate(TILES):
                    for n, (f, m) in enumerate(((0, 0), (1, 0), (0, 1))):
                        mm = nc.tensor.matmul(ps[0:w, k % 2, j * NK:(j + 1) * NK], qsp[k % 2][:, f, t0:t0 + w],
                                              ksp[:, m, k % 2, :], start=(n == 0), stop=(n == 2))
                mm.then_inc(psc[L], 1)

            def after(i, k, first):
                if k:
                    scores(i, k - 1, first)
                elif not first:
                    scores(i - 1, 3, False)
            project(pe, f"wq{L}", lambda i, k, first: None if first else pe.wait_ge(pq[L], i * 8 + 2 * k - 6), after,
                    inputs=(1, 4)[L])
            scores(3, 3, False)

        def peer_query_act(act, L):
            if L == 0:
                act.wait_ge(s_keys, 16)
            states_out(act, L)
            nc.scalar.activation(ksp[:, 0], keysT[:, L], ACT.Copy, scale=SC).then_inc(pkh[L], 1)

            def scores_out(i, k):
                act.wait_ge(psc[L], i * 4 + k + 1)
                nc.scalar.activation(score[:, ds(i * 4 + k, 1), :].rearrange("p o n -> p (o n)"),
                                     ps[:, k % 2, 0:NS], ACT.Copy, scale=UNSC).then_inc(pss[L], 1)

            def post(i, k, first):
                if first and k == 0:
                    act.wait_ge(hs_lo, KC * (2, 5)[L])
                block_used(act, f"wq{L}", i, k)
                if not (first and k < 2):
                    act.wait_ge(pql[L], i * 4 + k - 1)
                    act.wait_ge(psc[L], i * 4 + k - 1)
                for dst in (q16[k % 2], qsp[k % 2][:, 0, :]):
                    nc.scalar.activation(dst, zbank(k), ACT.Copy, scale=UNSC * SC).then_inc(pq[L], 1)
                if k:
                    scores_out(i, k - 1)
                elif not first:
                    scores_out(i - 1, 3)
            per_block(act, f"wq{L}", split_hi, post, ahead=2, following=[f"ua{L}"] * 2)
            scores_out(3, 3)

        def peer_query_pool(g, L):
            def post(i, k, first):
                g.wait_ge(pq[L], i * 8 + 2 * k + 2)
                if not (first and k < 2):
                    g.wait_ge(psc[L], i * 4 + k - 1)
                nc.gpsimd.tensor_tensor(qsp[k % 2][:, 1, :], q16[k % 2], qsp[k % 2][:, 0, :],
                                        ALU.subtract).then_inc(pql[L], 1)
            per_block(g, f"wq{L}", split_lo, post)

        def states_out(eng, L):
            for o_ in ((out_s5,), (out_hgp, out_hgs))[L]:
                eng.wait_ge(o_, 16)

        def peer_topk_dve(v, cnt, L):
            vv = nc.vector
            states_out(v, L)
            v.wait_ge(pkh[L], 1)
            vv.scalar_tensor_tensor(out=ksp[:, 1], in0=keysT[:, L], scalar=SC, in1=ksp[:, 0], op0=ALU.mult,
                                    op1=ALU.subtract).then_inc(pkl[L], 1)
            for b in range(2 * PH):
                h, f = b // 2, b % 2
                v.wait_ge(pss[L], b + 1)
                for j, (_, w) in enumerate(TILES):
                    s = score[0:w, b, j * NK:(j + 1) * NK]
                    cnt.add(vv.max(val[0:w, j, f, h, 0:8], s))
                cnt.wait()
                for j, (_, w) in enumerate(TILES):
                    s = score[0:w, b, j * NK:(j + 1) * NK]
                    cnt.add(vv.max_index(idu[0:w, j, f, h, 0:8], val[0:w, j, f, h, 0:8], s))
                for j, (_, w) in enumerate(TILES):
                    s = score[0:w, b, j * NK:(j + 1) * NK]
                    cnt.add(vv.match_replace(rest[j][0:w, :], val[0:w, j, f, h, 0:8], s, LOWEST))
                cnt.wait()
                for j, (_, w) in enumerate(TILES):
                    cnt.add(vv.max(val[0:w, j, f, h, 8:16], rest[j][0:w, :]))
                cnt.wait()
                for j, (_, w) in enumerate(TILES):
                    cnt.add(vv.max_index(idu[0:w, j, f, h, 8:16], val[0:w, j, f, h, 8:16], rest[j][0:w, :]))
                cnt.wait()

        def peer_pairs_dve(v, cnt, L):
            vv = nc.vector
            L_ = cnt.link
            for j, (_, w) in enumerate(TILES):
                for f in range(2):
                    L_(vv.tensor_copy(idf[0:w, j, f], idu[0:w, j, f]))
                L_(vv.tensor_scalar(idf[0:w, j, 0], idf[0:w, j, 0], float(NK), None, ALU.mult))
                for src, dst in ((val, cand), (idf, cidx)):
                    at = 0
                    for a0, na, nb in RECTS:
                        sh = [w, PH, na, nb]
                        cnt.add(vv.tensor_tensor(
                            dst[0:w, :, at:at + na * nb].rearrange("p h (a b) -> p h a b", a=na),
                            src[0:w, j, 0, :, a0:a0 + na, None].to_broadcast(sh),
                            src[0:w, j, 1, :, None, 0:nb].to_broadcast(sh), ALU.add))
                        at += na * nb
                cnt.wait()
                for h in range(PH):
                    c = cand[0:w, h, :]
                    r = rest2[h % 2][0:w, :]
                    L_(vv.max(sc[0:w, j, h, 0:8], c))
                    cnt.add(vv.max_index(posu[0:w, h, 0:8], sc[0:w, j, h, 0:8], c))
                    L_(vv.match_replace(r, sc[0:w, j, h, 0:8], c, LOWEST))
                    L_(vv.max(sc[0:w, j, h, 8:16], r))
                    L_(vv.max_index(posu[0:w, h, 8:16], sc[0:w, j, h, 8:16], r))
                L_(vv.tensor_copy(posf[0:w], posu[0:w]))
                sh = [w, TK, NC_]
                for h in range(PH):
                    e = eq[h % 2][0:w]
                    L_(vv.tensor_tensor(e, iota_c[0:w, None, :].to_broadcast(sh),
                                        posf[0:w, h, :, None].to_broadcast(sh), ALU.is_equal))
                    L_(vv.tensor_tensor(e, e, cidx[0:w, h, None, :].to_broadcast(sh), ALU.mult))
                    L_(vv.tensor_reduce(eid[0:w, j, h * TK:(h + 1) * TK], e, AX.X, ALU.add))
                vv.tensor_tensor(gate[0:w, j], sc[0:w, j], sc[0:w, j, :, 0:1].to_broadcast([w, PH, TK]),
                                 ALU.subtract).then_inc(psh[L], 1)
                L_(vv.tensor_copy(eii[0:w, j], eid[0:w, j]))
                cnt.add(vv.tensor_scalar(e12i[0:w, j, 0], eii[0:w, j], 7, None, ALU.arith_shift_right))
                L_(vv.tensor_scalar(e12i[0:w, j, 1], eii[0:w, j], NK - 1, None, ALU.bitwise_and))
                L_(vv.tensor_copy(e12[0:w, j], e12i[0:w, j]))

        def peer_softmax_dve(v, cnt, L):
            vv = nc.vector
            L_ = cnt.link
            for j, (_, w) in enumerate(TILES):
                v.wait_ge(pex[L], j + 1)
                L_(vv.tensor_reduce(sm[0:w, j], gate[0:w, j], AX.X, ALU.add))
                L_(vv.reciprocal(rs[0:w, j], sm[0:w, j]))
                vv.tensor_tensor(gate[0:w, j], gate[0:w, j], rs[0:w, j, :, None].to_broadcast([w, PH, TK]),
                                 ALU.mult).then_inc(pgt[L], 1)

        def peer_gates_dve(v, cnt, L):
            vv = nc.vector
            L_ = cnt.link
            v.wait_ge(ptr[L], 9)
            g = ps[:, 2, 0:T]
            L_(vv.tensor_scalar(gate_hi, g, SC, None, ALU.mult))
            vv.scalar_tensor_tensor(out=gate_lo, in0=g, scalar=SC, in1=gate_hi, op0=ALU.mult,
                                    op1=ALU.subtract).then_inc(ptc[L], 1)
            for m, (dst, sign) in enumerate(((neg_i1T, -1.0), (i2T, 1.0))):
                vv.tensor_scalar(dst, ps[:, m, 0:T], sign, None, ALU.mult).then_inc(ptc[L], 1)

        def peer_exp_act(act, L):
            act.wait_ge(psh[L], 3)
            for j, (_, w) in enumerate(TILES):
                nc.scalar.activation(gate[0:w, j], gate[0:w, j], ACT.Exp).then_inc(pex[L], 1)

        def peer_tr_pe(pe, L):
            pe.wait_ge(pgt[L], 3)
            pe.wait_ge(pss[L], 2 * PH)
            for j, (t0, w) in enumerate(TILES):
                for m in range(3):
                    src = (e12[0:w, j, m] if m < 2 else gate[0:w, j].rearrange("p h k -> p (h k)"))
                    nc.tensor.transpose(ps[:, m, t0:t0 + w], src, ident[0:w, 0:w]).then_inc(ptr[L], 1)

        def peer_u_pe(pe, L, part, a=0, b=None):
            if part == "ua":
                pe.wait_ge(pq[L], 32)
            off = 0 if part == "ua" else UA

            def free(i, k, first):
                if not (first and part == "ua"):
                    pe.wait_ge(pge[L], i * 4 + (off + k - 3))
            project(pe, f"{part}{L}", free, None, a, b)

        def peer_u_act(act, L, part, a=0, b=None):
            if part == "ua":
                states_out(act, L)
            elif a:
                act.wait_ge(ptr[L], 9)
            off = 0 if part == "ua" else UA

            def post(i, k, first):
                block_used(act, f"{part}{L}", i, k)
                nc.scalar.activation(act3[:, ds(i * RING + (off + k), 1), :].rearrange("p o t -> p (o t)"), zbank(k),
                                     ACT.Gelu, scale=UNSC).then_inc(pge[L], 1)
            per_block(act, f"{part}{L}", split_hi, post, a, b, ahead=2,
                      following=[f"ub{L}" if part == "ua" else f"v{L}"] * 2)

        def peer_u_dve(v, L, a=0, b=None):
            per_block(v, f"ub{L}", split_lo, lambda i, k, first: None, a, b)

        GROUPS = T // GT

        def spread_loop(eng, body, last=False):
            for x in range(2):
                body(0, x, True)
            with eng.Fori(1, GROUPS // 2 - last) as i:
                for x in range(2):
                    body(i, x, False)
            if last:
                body(GROUPS // 2 - 1, 0, False)
                body(GROUPS // 2 - 1, 1, False, last=True)

        def of_tokens(a, i, x):
            return a[:, None, ds(i * (2 * GT) + x * GT, GT)].to_broadcast([P, NK, GT])

        def peer_g_act(act, L):
            act.wait_ge(used, 2 * FIRST[f"v{L}"])

            def body(i, x, first):
                act.wait_ge(pdf[L], i * 2 + x + 1)
                if not first:
                    act.wait_ge(pG[L], i * 2 + x - 1)
                nc.scalar.activation(hot1[x].rearrange("p j t -> p (j t)"),
                                     ps[:, 4 + 2 * x:6 + 2 * x, :].rearrange("p b n -> p (b n)"),
                                     ACT.Abs).then_inc(pab[L], 1)
                act.wait_ge(pab[L], i * 2 + x + 1)
                nc.scalar.activation(hot1[x], hot1[x], ACT.Relu, bias=1.0, scale=-1.0).then_inc(phA[L], 1)
            spread_loop(act, body)

        def peer_g_dve(v, L):
            vv = nc.vector
            v.wait_ge(ptc[L], 3)
            v.wait_ge(pge[L], NK)
            v.wait_ge(used, 2 * FIRST[f"v{L}"])

            def mul(i, x):
                v.wait_ge(pG[L], i * 2 + x + 1)
                a = act3[:, :, ds(i * (2 * GT) + x * GT, GT)]
                vv.tensor_tensor(a, a, ps[:, 2 * x:2 * x + 2, :].rearrange("p b (s j) -> p j (b s)", j=NK),
                                 ALU.mult).then_inc(pmul[L], 1)

            def equal(i, x, first):
                i, x = (i, x) if x < 2 else (i + 1, 0)
                if not first:
                    v.wait_ge(poh[L], i * 2 + x - 1)
                vv.tensor_tensor(hot2[x], iota_r[:, :, :], of_tokens(i2T, i, x), ALU.is_equal).then_inc(pe2[L], 1)

            def body(i, x, first, last=False):
                if not last:
                    equal(i, x + 1, first and x == 0)
                if not first:
                    v.wait_ge(pG[L], i * 2 + x - 1)
                v.wait_ge(pe2[L], i * 2 + x + 1)
                sh = [P, 2, NK, GT]
                vv.tensor_tensor(hot2g[x], hot2[x][:, None].to_broadcast(sh),
                                 gates[:, :, None, ds(i * (2 * GT) + x * GT, GT)].to_broadcast(sh),
                                 ALU.mult).then_inc(poh[L], 1)
                if x:
                    mul(i, 0)
                elif not first:
                    mul(i - 1, 1)
            equal(0, 0, True)
            spread_loop(v, body, last=True)
            mul(GROUPS // 2 - 1, 1)

        def peer_g_pe(pe, L):
            pe.wait_ge(ptc[L], 3)
            pe.wait_ge(pge[L], NK)

            def difference(i, x, first):
                i, x = (i, x) if x < 2 else (i + 1, 0)
                if not first:
                    pe.wait_ge(pab[L], i * 2 + x - 1)
                nh = NK // 2
                for b in range(2):
                    out = ps[:, 4 + 2 * x + b, :]
                    nc.tensor.matmul(out, ident_h[:, :], iota_r[:, b * nh:(b + 1) * nh, :], start=True, stop=False)
                    mm = nc.tensor.matmul(out, ident_h[:, :],
                                          of_tokens(neg_i1T, i, x)[:, 0:nh, :], start=False, stop=True)
                mm.then_inc(pdf[L], 1)

            def body(i, x, first, last=False):
                if not last:
                    difference(i, x + 1, first and x == 0)
                if not first:
                    pe.wait_ge(pmul[L], i * 2 + x - 1)
                pe.wait_ge(phA[L], i * 2 + x + 1)
                pe.wait_ge(poh[L], i * 2 + x + 1)
                for s in range(GT):
                    out = ps[:, 2 * x + s // 4, (s % 4) * NK:(s % 4 + 1) * NK]
                    for f in range(2):
                        mm = nc.tensor.matmul(out, hot1[x][:, :, s], hot2g[x][:, f, :, s],
                                              start=(f == 0), stop=(f == 1))
                mm.then_inc(pG[L], 1)
            difference(0, 0, True)
            spread_loop(pe, body, last=True)

        def peer_v_pe(pe, L):
            def post(i, k, first):
                pe.wait_ge(pal[L], i * RING + k + 1)
                hi, lo = asp[:, k % 2, 0, :], asp[:, k % 2, 1, :]
                for c in range(KC):
                    if c % 4 == 0:
                        lo_half_done(pe, f"v{L}", i, k, c // 4)
                    for bank, col, t0, w in ACC[c]:
                        mm = three_passes(ps[:, bank, col:col + w], k % 2, c, hi[:, t0:t0 + w], lo[:, t0:t0 + w],
                                          first and k == 0 and c < 6, False, skip_group_check=True)
                    if c % 4 == 3:
                        mm.then_inc(used, 1)
            per_block(pe, f"v{L}", None, post)

        def act_block(i, k):
            i, k = (i, k) if k < RING else (i + 1, k - RING)
            return act3[:, ds(i * RING + k, 1), :].rearrange("p o t -> p (o t)")

        def peer_v_act(act, L):
            act.wait_ge(pmul[L], GROUPS)

            def split(act, name, i, k):
                if name != f"v{L}":
                    split_hi(act, name, i, k)
                    return
                if not (isinstance(i, int) and i == 0 and k < 2):
                    split_hi(act, name, i, k)
                nc.scalar.activation(asp[:, k % 2, 0, :], act_block(i, k), ACT.Copy).then_inc(pah[L], 1)
            per_block(act, f"v{L}", split, lambda i, k, first: None, following=["win"] if L == 0 else [])

        def peer_v_dve(v, L):
            v.wait_ge(pmul[L], GROUPS)

            def split(v, name, i, k):
                split_lo(v, name, i, k)
                v.wait_ge(pah[L], i * RING + k + 1)
                nc.vector.tensor_tensor(asp[:, k % 2, 1, :], act_block(i, k), asp[:, k % 2, 0, :],
                                        ALU.subtract).then_inc(pal[L], 1)
            per_block(v, f"v{L}", split, lambda i, k, first: None)

        def peer_x_dve(v, L):
            v.wait_ge(used, 2 * (FIRST[f"v{L}"] + NK))
            for c in range(KC):
                for bank, col, t0, w in ACC[c]:
                    nc.vector.scalar_tensor_tensor(out=xT[:, c, t0:t0 + w], in0=ps[:, bank, col:col + w], scalar=UNSC,
                                                   in1=xT[:, c, t0:t0 + w], op0=ALU.mult,
                                                   op1=ALU.add).then_inc(pacc[L], 1)
            v.wait_ge(pacc[L], 10)
            v.sem_inc(x_ready, 1)

        U = KC * T

        def unit(k):
            return bg(U * k, U)

        def h3(a):
            return a.rearrange("p (h t) -> p h t", h=HH)

        Bc, K_, Q_, VT, GS, QM, QI, KM, KD, D1 = (unit(k) for k in range(10))
        CU = bg(U * 10, U)
        vtok = [bg(1024 * j, 1024) for j in range(3)]
        ktok = [bg(3072 + 1024 * j, 1024) for j in range(3)]
        sall = [bg(U * 10 + 1024 * c, 1024).rearrange("p (h v) -> p h v", h=HH) for c in range(NCH)]
        ss = bg(U * 10 + 4096, 8192).rearrange("p (h b v) -> p h b v", h=HH, b=NB)
        smask = bg(U * 10 + 4096 + 8192, TS)
        bmask = bg(U * 10 + 4096 + 8192 + TS, NB)
        pmask = bg(U * 10 + 4096 + 8192 + TS + NB, P)
        pp = [bg(U * 9 + 1024 * j, 1024 if j < 2 else 256).rearrange("p (h t) -> p h t", h=HH) for j in range(3)]
        vb = [bg(U * 8 + 1024 * k, 1024).rearrange("p (b v) -> p b v", b=NB) for k in range(2)]
        O_ = unit(3)
        ssp = [[bg(U * 5 + 1024 * k + 512 * f, 512).bitcast(F16).rearrange("p (b v) -> p b v", b=NB)
                for f in range(2)] for k in range(2)]
        qds = bg(U * 5 + 2048, HH * TS).bitcast(F16).rearrange("p (f h t) -> p f h t", f=2, h=HH)
        sq = [bg(U * 7 + T * k, T) for k in range(2)]
        spread_h = bg(U * 7 + 2 * T, HH * P).rearrange("p (h m) -> p h m", h=HH)
        carry = spare[:, 0:T]
        lbr = sb("lbr", [P, 2, KC])
        lb, oml = (small[:, 8 * k:8 * k + 8] for k in range(2))
        lt = [small[:, 16 + 8 * k:24 + 8 * k] for k in range(4)]
        dec = small[:, 64:64 + 12 * HH].rearrange("p (h c) -> p h c", h=HH)
        sum_h = small[:, 160:160 + 2 * HH - 1]
        rstd_h = bg(U * 7 + 2 * T + HH * P, T)[0:HH, :]
        nwv = sb("nwv", [P, 1])

        hg_in = sem("hg_in")
        hg_s0 = sem("hg_s0")
        hg_lbm = sem("hg_lbm")
        hg_lbe = sem("hg_lbe")
        hg_mask = sem("hg_mask")
        hg_ev = sem("hg_evac")
        hg_f = sem("hg_f")
        hg_log = sem("hg_log")
        hg_cum = sem("hg_cum")
        hg_d = sem("hg_d")
        hg_e = sem("hg_e")
        hg_m = sem("hg_m")
        hg_tv = sem("hg_tv")
        hg_tk = sem("hg_tk")
        hg_tvc = sem("hg_tvc")
        hg_tkc = sem("hg_tkc")
        hg_z = sem("hg_z")
        hg_s = sem("hg_s")
        hg_p = sem("hg_p")
        hg_kv = sem("hg_kv")
        hg_S = sem("hg_S")
        hg_o = sem("hg_o")
        hg_oc = sem("hg_oc")
        hg_vb = sem("hg_vb")
        hg_kvs = sem("hg_kvs")
        hg_Ss = sem("hg_Ss")
        hg_qh = sem("hg_q_hi")
        hg_ql = sem("hg_q_lo")
        hg_sh = sem("hg_s0_hi")
        hg_sl = sem("hg_s0_lo")
        hg_dc = sem("hg_s0_decayed")
        hg_sq = sem("hg_sq")
        hg_ssq = sem("hg_ssq")
        hg_rs = sem("hg_rs")
        hg_ri = sem("hg_rstd")
        hg_gate = sem("hg_gated")
        hg_bc = sem("hg_rstd_spread")
        hg_h = sem("hg_h")
        hg_x = sem("hg_x")

        def hg_masks_pool(g):
            g.wait_ge(x_ready, 2)
            step = [0]

            def L_(ins):
                ins.then_inc(hg_mask, 1)
                step[0] += 1
                g.wait_ge(hg_mask, step[0])
            for m in (pmask, smask, bmask):
                L_(nc.gpsimd.memset(m, 1.0))
            L_(nc.gpsimd.affine_select(out=pmask, in_=pmask, pattern=[[1, P]], base=0, channel_multiplier=-1,
                                       compare_op=ALU.is_ge, fill=0.0))
            L_(nc.gpsimd.memset(pmask[0:CH, CH:P], 0.0))
            s2 = smask[0:TS, :].rearrange("p (b i) -> p b i", b=NB)
            L_(nc.gpsimd.affine_select(out=s2, in_=s2, pattern=[[LS, NB], [1, LS]], base=0, channel_multiplier=-1,
                                       compare_op=ALU.is_ge, fill=0.0))
            for m, pat in ((s2, [[-LS, NB], [0, LS]]), (bmask[0:TS, :], [[-LS, NB]])):
                L_(nc.gpsimd.affine_select(out=m, in_=m, pattern=pat, base=0, channel_multiplier=1,
                                           compare_op=ALU.is_ge, fill=0.0))
                L_(nc.gpsimd.affine_select(out=m, in_=m, pattern=[[-a, n] for a, n in pat], base=LS - 1,
                                           channel_multiplier=-1, compare_op=ALU.is_ge, fill=0.0))
        N_MASK = 10

        def hg_lb_dve(v, cnt):
            vv = nc.vector
            v.wait_ge(hg_in, 32)
            cnt.link(vv.tensor_tensor(lt[0], lbr[:, 0, :], lbr[:, 1, :], ALU.max))
            vv.tensor_tensor(lt[1], lbr[:, 0, :], lt[0], ALU.subtract).then_inc(hg_lbm, 1)
            vv.tensor_tensor(lt[2], lbr[:, 1, :], lt[0], ALU.subtract).then_inc(hg_lbm, 1)
            v.wait_ge(hg_lbe, 2)
            cnt.link(vv.tensor_tensor(lt[3], lt[1], lt[2], ALU.add))
            cnt.link(vv.reciprocal(lt[0], lt[3]))
            cnt.add(vv.tensor_tensor(lt[1], lt[1], lt[0], ALU.mult))
            cnt.link(vv.tensor_tensor(lt[2], lt[2], lt[0], ALU.mult))
            cnt.link(vv.tensor_tensor(lt[3], lt[1], lt[2], ALU.add))
            cnt.link(vv.tensor_tensor(lb, lt[3], lt[1], ALU.subtract))
            cnt.link(vv.tensor_scalar(oml, lb, -1.0, 1.0, ALU.mult, ALU.add))
            cnt.add(vv.memset(carry[:, :], 1.0))
            cnt.wait()
            cnt.add(vv.memset(carry[:, 0:TP:CH], 0.0))
            cnt.link(vv.memset(carry[:, TP:T:LS], 0.0))

        def hg_lb_act(act):
            act.wait_ge(hg_lbm, 2)
            for k in (1, 2):
                nc.scalar.activation(lt[k], lt[k], ACT.Exp).then_inc(hg_lbe, 1)

        def hg_in_pe(pe):
            project(pe, "win", lambda i, k, first: None if first else pe.wait_ge(hg_ev, i * 4 + k - 3),
                    inputs=2)

        def hg_evac_act(act, trip, fns):

            def post(i, k, first):
                block_used(act, "win", i, k)
                for dst, fn, scale in fns:
                    ins = nc.scalar.activation(h3(dst)[:, (4 * trip + k) % HH, :],
                                               zbank(k), fn, scale=scale * UNSC)
                ins.then_inc(hg_ev, 1)
            per_block(act, "win", split_hi, post, trip, trip + 1, ahead=2)

        def hg_act(act):
            act.wait_ge(x_ready, 2)
            for trip in range(2):
                hg_evac_act(act, trip, [(Bc, ACT.Sigmoid, 1.0), (K_, ACT.Sigmoid, -1.0)])
            hg_evac_act(act, 2, [(Q_, ACT.Silu, 1.0)])
            hg_evac_act(act, 3, [(Q_, ACT.Silu, 1.0)])
            act.wait_ge(hg_f, 1)
            nc.scalar.activation(Bc, Bc, ACT.Ln).then_inc(hg_log, 1)
            hg_evac_act(act, 4, [(VT, ACT.Copy, 1.0)])
            act.wait_ge(hg_cum, 8)
            nc.scalar.activation(QI, CU, ACT.Exp).then_inc(hg_e, 1)
            act.wait_ge(hg_d, 2)
            nc.scalar.activation(QM, D1, ACT.Exp).then_inc(hg_e, 1)
            hg_evac_act(act, 5, [(VT, ACT.Copy, 1.0)])
            nc.scalar.activation(KM, D1, ACT.Exp, scale=-1.0).then_inc(hg_e, 1)
            act.wait_ge(hg_d, 4)
            nc.scalar.activation(KD, Bc, ACT.Exp).then_inc(hg_e, 1)
            hg_evac_act(act, 6, [(GS, ACT.Silu, 1.0)])
            hg_evac_act(act, 7, [(GS, ACT.Silu, 1.0)])
            for j, (_, w) in enumerate(TILES):
                act.wait_ge(hg_tv, j + 1)
                if j == 0:
                    act.wait_ge(hg_m, 4)
                nc.scalar.activation(vtok[j][0:w, :], ps[0:w, 0:2, :].rearrange("p b n -> p (b n)"),
                                     ACT.Copy).then_inc(hg_tvc, 1)
            act.wait_ge(hg_tv, 3)
            act.wait_ge(hg_s, 3)
            act.wait_ge(hg_m, 4)
            nc.scalar.activation(qds[:, 0], h3(QI)[:, :, TP:T], ACT.Copy, scale=SC).then_inc(hg_qh, 1)
            act.wait_ge(hg_s0, 16)

            def state_hi(h):
                if h >= 2:
                    act.wait_ge(hg_o, h - 1)
                nc.scalar.activation(ssp[h % 2][0], ss[:, h], ACT.Copy, scale=SC).then_inc(hg_sh, 1)
            state_hi(0)
            for h in range(HH):
                if h + 1 < HH:
                    state_hi(h + 1)
                act.wait_ge(hg_sl, h + 1)
                for b in range(NB):
                    nc.scalar.activation(ss[:, h, b], ss[:, h, b], ACT.Copy,
                                         scale=dec[:, h, NCH + b:NCH + b + 1]).then_inc(hg_dc, 1)
                act.wait_ge(hg_o, h + 1)
                nc.scalar.activation(h3(O_)[:, h, 0:TP], ps[:, 6 + h % 2, 0:TP], ACT.Copy).then_inc(hg_oc, 1)
                nc.scalar.activation(h3(O_)[:, h, TP:T], ps[:, 6 + h % 2, TP:T], ACT.Copy,
                                     scale=UNSC).then_inc(hg_oc, 1)
                act.wait_ge(hg_oc, 2 * h + 2)
                if h >= 2:
                    act.wait_ge(hg_ssq, h - 1)
                nc.scalar.activation(sq[h % 2], h3(O_)[:, h, :], ACT.Square).then_inc(hg_sq, 1)
                if h == HH - 2:
                    for k in range(2):
                        split_hi(act, "wout", 0, k)
            act.wait_ge(hg_ssq, HH)
            nc.scalar.activation(rstd_h, ps[0:HH, 2, 0:T], ACT.Sqrt, bias=epsc[0:HH, 0:1],
                                 scale=1.0 / P).then_inc(hg_rs, 1)
            for c in range(KC):
                act.wait_ge(hg_h, c + 1)
                high_part(c).then_inc(hs_hi, 1)
            per_block(act, "wout", split_hi, lambda i, k, first: None, ahead=2, following=["wq1"])

        def hg_dve(v, cnt):
            vv = nc.vector
            tt = vv.tensor_tensor
            v.wait_ge(hg_ev, 8)
            for h in range(HH):
                cnt.add(vv.tensor_scalar(h3(Bc)[:, h, :], h3(Bc)[:, h, :], oml[:, h:h + 1], lb[:, h:h + 1],
                                         ALU.mult, ALU.add))
            cnt.wait()
            vv.tensor_scalar(Bc, Bc, F_LEAST, None, ALU.max).then_inc(hg_f, 1)
            cnt.link(tt(h3(K_), h3(K_), oml[:, :, None].to_broadcast([P, HH, T]), ALU.mult))
            v.wait_ge(hg_log, 1)
            for h in range(HH):
                vv.tensor_tensor_scan(h3(CU)[:, h, :], carry[:, :], h3(Bc)[:, h, :], 0.0, ALU.mult,
                                      ALU.add).then_inc(hg_cum, 1)
            v.wait_ge(hg_cum, 8)

            def parts(a):
                p = h3(a)[:, :, 0:TP].rearrange("p h (c t) -> p h c t", c=NCH)
                s = h3(a)[:, :, TP:T].rearrange("p h (c t) -> p h c t", c=NB)
                return (p, NCH, CH), (s, NB, LS)
            for (b_, n, c), (d_, _, _) in zip(parts(CU), parts(D1)):
                tt(d_, b_, b_[:, :, :, c // 2:c // 2 + 1].to_broadcast([P, HH, n, c]), ALU.subtract).then_inc(hg_d, 1)
            for (b_, n, c), (d_, _, _) in zip(parts(CU), parts(Bc)):
                tt(d_, b_[:, :, :, c - 1:c].to_broadcast([P, HH, n, c]), b_, ALU.subtract).then_inc(hg_d, 1)
            v.wait_ge(hg_e, 1)
            cnt.add(vv.tensor_copy(dec[:, :, 0:NCH], h3(QI)[:, :, CH - 1:TP:CH]))
            cnt.link(vv.tensor_copy(dec[:, :, NCH:12], h3(QI)[:, :, TP + LS - 1:T:LS]))
            v.wait_ge(hg_e, 4)
            v.wait_ge(hg_ev, 16)
            for dst, src in ((QI, Q_), (QM, Q_), (KM, K_), (KD, K_)):
                tt(dst, dst, src, ALU.mult).then_inc(hg_m, 1)
            v.wait_ge(hg_e, 4)
            for j in range(3):
                vv.memset(pp[j], 0.0).then_inc(hg_z, 1)
            for j, (_, w) in enumerate(TILES):
                v.wait_ge(hg_tk, j + 1)
                if j == 0:
                    v.wait_ge(hg_m, 4)
                vv.tensor_copy(ktok[j][0:w, :], ps[0:w, 2:4, :].rearrange("p b n -> p (b n)")).then_inc(hg_tkc, 1)
            v.wait_ge(hg_mask, N_MASK)
            v.wait_ge(hg_z, 3)
            for j, (_, w) in enumerate(TILES):
                v.wait_ge(hg_s, j + 1)
                m = (pmask if w == P else smask)[0:w, None, 0:w].to_broadcast([w, 4, w]).bitcast(I32)
                for half in range(2):
                    bank = 4 + 2 * (j % 2) + half
                    vv.copy_predicated(pp[j][0:w, 4 * half:4 * half + 4, :], m,
                                       ps[0:w, bank, 0:4 * w].rearrange("p (h t) -> p h t", h=4)).then_inc(hg_p, 1)
            v.wait_ge(hg_p, 6)
            cnt.link(vv.tensor_scalar(pp[2][0:TS], pp[2][0:TS], SC * SC, None, ALU.mult))
            v.sem_inc(hg_p, 1)
            v.wait_ge(hg_s, 3)
            v.wait_ge(hg_qh, 1)
            vv.scalar_tensor_tensor(out=qds[:, 1], in0=h3(QI)[:, :, TP:T], scalar=SC, in1=qds[:, 0],
                                    op0=ALU.mult, op1=ALU.subtract).then_inc(hg_ql, 1)
            cnt.add(vv.memset(sum_h, 0.0))
            cnt.link(vv.tensor_copy(spread_h[0:HH], ident[0:HH, 0:HH, None].to_broadcast([HH, HH, P])))
            cnt.link(vv.memset(sum_h[:, HH - 1:HH], 1.0))
            for c in range(NCH):
                kv = ps[:, 2 * (c % 2):2 * (c % 2) + 2, :].rearrange("p b (h v) -> p (b h) v", h=4)
                v.wait_ge(hg_kv, c + 1)
                if c == 0:
                    vv.tensor_copy(sall[0], kv).then_inc(hg_S, 1)
                else:
                    v.wait_ge(hg_S, c)
                    cnt.link(tt(sall[c], sall[c - 1], dec[:, :, c:c + 1].to_broadcast([P, HH, P]), ALU.mult))
                    tt(sall[c], sall[c], kv, ALU.add).then_inc(hg_S, 1)
            v.wait_ge(hg_tvc, 3)
            v.wait_ge(hg_s0, 16)
            v.wait_ge(hg_tk, 3)

            def state_lo(h):
                v.wait_ge(hg_sh, h + 1)
                vv.scalar_tensor_tensor(out=ssp[h % 2][1], in0=ss[:, h], scalar=SC, in1=ssp[h % 2][0],
                                        op0=ALU.mult, op1=ALU.subtract).then_inc(hg_sl, 1)

            def finish(h):
                v.wait_ge(hg_kvs, h + 1)
                v.wait_ge(hg_dc, NB * (h + 1))
                b0 = 4 * (h % 2)
                tt(ss[:, h], ss[:, h], ps[:, b0:b0 + 2, :].rearrange("p b (c v) -> p (b c) v", c=4),
                   ALU.add).then_inc(hg_Ss, 1)
                v.wait_ge(hg_sq, h + 1)
                o = h3(O_)[:, h, :]
                vv.scalar_tensor_tensor(out=o, in0=o, scalar=nwv[:, 0:1], in1=h3(GS)[:, h, :], op0=ALU.mult,
                                        op1=ALU.mult).then_inc(hg_gate, 1)
            state_lo(0)
            for h in range(HH):
                if h + 1 < HH:
                    state_lo(h + 1)
                if h >= 2:
                    v.wait_ge(hg_kvs, h - 1)
                sh = [TS, NB, P]
                tt(vb[h % 2][0:TS], vtok[2][0:TS, None, h * P:(h + 1) * P].to_broadcast(sh),
                   bmask[0:TS, :, None].to_broadcast(sh), ALU.mult).then_inc(hg_vb, 1)
                if h:
                    finish(h - 1)
            for k in range(2):
                split_lo(v, "wout", 0, k)
            finish(HH - 1)
            v.wait_ge(hg_rs, 1)
            vv.reciprocal(rstd_h, rstd_h).then_inc(hg_ri, 1)
            v.wait_ge(hg_gate, HH)
            for h in range(HH):
                v.wait_ge(hg_bc, h + 1)
                tt(hT[:, h, :], h3(O_)[:, h, :], ps[:, 4 + h % 4, 0:T], ALU.mult).then_inc(hg_h, 1)
                if h:
                    v.wait_ge(hs_hi, 3 * KC + h)
                    low_part(h - 1).then_inc(hs_lo, 1)
            v.wait_ge(hs_hi, 4 * KC)
            low_part(KC - 1).then_inc(hs_lo, 1)

            def post(i, k, first):
                block_used(v, "wout", i, k)
                x = xT[:, ds(i * 4 + k, 1), :].rearrange("p o t -> p (o t)")
                vv.scalar_tensor_tensor(out=x, in0=zbank(k), scalar=UNSC, in1=x, op0=ALU.mult,
                                        op1=ALU.add).then_inc(hg_x, 1)
            per_block(v, "wout", split_lo, post, ahead=2)
            v.wait_ge(hg_x, 8)
            v.sem_inc(x_ready, 1)

        def hg_pe(pe):
            mm_, tr = nc.tensor.matmul, nc.tensor.transpose
            pe.wait_ge(hg_ev, 32)
            pe.wait_ge(hg_m, 4)
            for j, (t0, w) in enumerate(TILES):
                if j:
                    pe.wait_ge(hg_tvc, j)
                for h in range(HH):
                    mm = tr(ps[0:w, h // 4, (h % 4) * P:(h % 4 + 1) * P], h3(VT)[:, h, t0:t0 + w], ident[:, :])
                mm.then_inc(hg_tv, 1)
                if j:
                    pe.wait_ge(hg_tkc, j)
                for h in range(HH):
                    mm = tr(ps[0:w, 2 + h // 4, (h % 4) * P:(h % 4 + 1) * P], h3(KD)[:, h, t0:t0 + w], ident[:, :])
                mm.then_inc(hg_tk, 1)
            for j, (t0, w) in enumerate(TILES):
                if j == 2:
                    pe.wait_ge(hg_p, 2)
                for h in range(HH):
                    mm = mm_(ps[0:w, 4 + 2 * (j % 2) + h // 4, (h % 4) * w:(h % 4 + 1) * w],
                             h3(KM)[:, h, t0:t0 + w], h3(QM)[:, h, t0:t0 + w], start=True, stop=True)
                mm.then_inc(hg_s, 1)
            pe.wait_ge(hg_tvc, 3)
            pe.wait_ge(hg_tkc, 3)
            for c in range(NCH):
                if c >= 2:
                    pe.wait_ge(hg_S, c - 1)
                j, r0 = c // 2, CH * (c % 2)
                for h in range(HH):
                    mm = mm_(ps[:, 2 * (c % 2) + h // 4, (h % 4) * P:(h % 4 + 1) * P],
                             ktok[j][r0:r0 + CH, h * P:(h + 1) * P], vtok[j][r0:r0 + CH, h * P:(h + 1) * P],
                             start=True, stop=True)
                mm.then_inc(hg_kv, 1)
            pe.wait_ge(hg_p, 7)
            pe.wait_ge(hg_S, NCH)
            pe.wait_ge(hg_ql, 1)

            def square_sums(h):
                pe.wait_ge(hg_sq, h + 1)
                mm_(ps[0:HH, 2, 0:T], sum_h[:, HH - 1 - h:2 * HH - 1 - h], sq[h % 2],
                    start=(h == 0), stop=(h == HH - 1)).then_inc(hg_ssq, 1)
            for h in range(HH):
                if h >= 2:
                    pe.wait_ge(hg_oc, 2 * h - 2)
                bank = 6 + h % 2
                for j, (t0, w) in enumerate(TILES):
                    mm_(ps[:, bank, t0:t0 + w], vtok[j][0:w, h * P:(h + 1) * P], pp[j][0:w, h, :],
                        start=True, stop=False, skip_group_check=True)
                    if w == P:
                        for c in range(2 * j, 2 * j + 2):
                            if c:
                                a = c * CH
                                mm_(ps[:, bank, a:a + CH], sall[c - 1][:, h, :], h3(QI)[:, h, a:a + CH],
                                    start=False, stop=False, skip_group_check=True)
                pe.wait_ge(hg_sl, h + 1)
                for b in range(NB):
                    a = TP + b * LS
                    s_hi, s_lo = (ssp[h % 2][f][:, b, :] for f in range(2))
                    q_hi, q_lo = (qds[:, f, h, b * LS:(b + 1) * LS] for f in range(2))
                    for s_, q_ in ((s_hi, q_hi), (s_hi, q_lo), (s_lo, q_hi)):
                        mm = mm_(ps[:, bank, a:a + LS], s_, q_, start=False, stop=False, skip_group_check=True)
                mm.then_inc(hg_o, 1)
                if h >= 2:
                    pe.wait_ge(hg_Ss, h - 1)
                pe.wait_ge(hg_vb, h + 1)
                b0 = 4 * (h % 2)
                for half in range(2):
                    mm = mm_(ps[:, b0 + half, :], ktok[2][0:TS, h * P:(h + 1) * P],
                             vb[h % 2][0:TS, 4 * half:4 * half + 4, :].rearrange("p b v -> p (b v)"),
                             start=True, stop=True)
                mm.then_inc(hg_kvs, 1)
                if h:
                    square_sums(h - 1)
            square_sums(HH - 1)
            pe.wait_ge(hg_ri, 1)
            pe.wait_ge(hg_Ss, HH)
            pe.wait_ge(hg_oc, 2 * HH)
            for h in range(HH):
                if h >= 4:
                    pe.wait_ge(hg_h, h - 3)
                mm_(ps[:, 4 + h % 4, 0:T], spread_h[0:HH, h, :], rstd_h, start=True, stop=True).then_inc(hg_bc, 1)
            pe.wait_ge(hg_h, HH)
            project(pe, "wout", lambda i, k, first: None if first else pe.wait_ge(hg_x, i * 4 + k - 3), inputs=3)

        @block.sync
        def _(sp):
            for k, n in enumerate(("lam_re", "lam_im", "log_dt")):
                sp.dma_start(par[:, k, :], t_in[n]).then_inc(s5_in, 16)
            sp.dma_start(s5w, t_in["s5b"]).then_inc(s5_in, 16)
            sp.dma_start(craw, t_in["s5c"]).then_inc(s5_in, 16)
            sp.dma_start(dcol[:, :], t_in["s5d"]).then_inc(s5_in, 16)
            sp.dma_start(normw[:, :, :], t_in["normw"]).then_inc(s_par, 16)
            sp.dma_start(xT[:, :, :], t_in["xT"]).then_inc(s_x, 16)
            sp.dma_start(keysT[:, :, :, :], t_in["keysT"]).then_inc(s_keys, 16)
            sp.dma_start(lbr[:, :, :], t_in["lbr"]).then_inc(hg_in, 16)
            sp.dma_start(nwv[:, :], t_in["hgnw"]).then_inc(hg_in, 16)
            before = None
            for n, _ in SEGMENTS:
                stream_segment(sp, n, before)
                before = n
            for half in range(2):
                c = slice(half * KC // 2, (half + 1) * KC // 2)
                sp.wait_ge(norm_h, 4 * KC + c.stop)
                sp.dma_start(t_out["y"][:, c, :], hT[:, c, :]).then_inc(out_y[half], 16)
            for half in range(2):
                sp.wait_ge(out_y[half], 16)

        @block.gpsimd
        def _(g):
            n = [0]

            def L_(ins):
                ins.then_inc(s_const, 1)
                n[0] += 1
                g.wait_ge(s_const, n[0])
            L_(nc.gpsimd.memset(ident[:, :], 0.0))
            L_(nc.gpsimd.affine_select(out=ident[:, :], in_=ident[:, :], compare_op=ALU.not_equal, fill=1.0,
                                       base=0, pattern=[[-1, P]], channel_multiplier=1))
            L_(nc.gpsimd.tensor_copy(ident_h[:, :], ident[:, :]))
            L_(nc.gpsimd.memset(ones[:, :], 1.0))
            L_(nc.gpsimd.memset(epsc[:, :], EPS))
            L_(nc.gpsimd.iota(iota_r[:, :, :], pattern=[[1, NK], [0, GT]], base=0, channel_multiplier=0,
                              allow_small_or_imprecise_dtypes=True))
            L_(nc.gpsimd.iota(iota_c[:, :], pattern=[[1, NC_]], base=0, channel_multiplier=0,
                              allow_small_or_imprecise_dtypes=True))
            s5_table_pool(g)
            g.dma_start(s0.rearrange("p r q b -> p (r q b)"), t_in["s5s0"]).then_inc(s5_s0, 16)
            s5_pairs_pool(g)
            g.wait_ge(s5_fin, 4)
            g.dma_start(t_out["s5f"], fin5.rearrange("p r q b -> p (r q b)")).then_inc(out_s5, 16)
            peer_query_pool(g, 0)
            split_pool(g, "ua0")
            g.wait_ge(x_ready, 2)
            g.dma_start(ss.rearrange("p h b v -> p (h b v)"), t_in["hgs0"]).then_inc(hg_s0, 16)
            split_pool(g, "win")
            hg_masks_pool(g)
            g.wait_ge(hg_S, 4)
            g.dma_start(t_out["hgp"], sall[3].rearrange("p h v -> p (h v)")).then_inc(out_hgp, 16)
            g.wait_ge(hg_Ss, 8)
            g.dma_start(t_out["hgs"], ss.rearrange("p h b v -> p (h b v)")).then_inc(out_hgs, 16)
            peer_query_pool(g, 1)
            split_pool(g, "ua1")
            g.wait_ge(out_s5, 16)
            g.wait_ge(out_hgp, 16)
            g.wait_ge(out_hgs, 16)

        @block.tensor
        def _(pe):
            pe.wait_ge(s_const, 7)
            norm_pe(pe, 0)
            s5_pairs_pe(pe)
            s5_out_pe(pe)
            glu_pe(pe)
            for L in range(2):
                norm_pe(pe, 2 * L + 1)
                peer_query_pe(pe, L)
                peer_u_pe(pe, L, "ua")
                peer_u_pe(pe, L, "ub", 0, UT)
                peer_tr_pe(pe, L)
                peer_u_pe(pe, L, "ub", UT)
                peer_g_pe(pe, L)
                peer_v_pe(pe, L)
                norm_pe(pe, 2 * L + 2)
                if L == 0:
                    hg_in_pe(pe)
                    hg_pe(pe)

        @block.scalar
        def _(act):
            act.wait_ge(s_const, 7)
            s5_params_act(act)
            norm_act(act, 0)
            s5_pairs_act(act)
            s5_out_act(act)
            glu_act(act)
            for L in range(2):
                norm_act(act, 2 * L + 1, f"wq{L}")
                peer_query_act(act, L)
                peer_u_act(act, L, "ua")
                peer_exp_act(act, L)
                peer_u_act(act, L, "ub", 0, UT)
                peer_u_act(act, L, "ub", UT)
                peer_g_act(act, L)
                peer_v_act(act, L)
                norm_act(act, 2 * L + 2, "win" if L == 0 else None)
                if L == 0:
                    hg_lb_act(act)
                    hg_act(act)

        @block.vector
        def _(v):
            cnt = Count(v, dv)
            s5_params_dve(v, cnt)
            v.wait_ge(s_par, 16)
            v.wait_ge(s_const, 7)
            norm_dve(v, cnt, 0)
            s5_table_dve(v, cnt)
            s5_pairs_dve(v, cnt)
            s5_samples_dve(v, cnt)
            glu_dve(v)
            for L in range(2):
                norm_dve(v, cnt, 2 * L + 1)
                peer_topk_dve(v, cnt, L)
                peer_pairs_dve(v, cnt, L)
                peer_u_dve(v, L, 0, 1)
                peer_softmax_dve(v, cnt, L)
                peer_u_dve(v, L, 1, UT)
                peer_gates_dve(v, cnt, L)
                peer_u_dve(v, L, UT)
                peer_g_dve(v, L)
                peer_v_dve(v, L)
                peer_x_dve(v, L)
                norm_dve(v, cnt, 2 * L + 2)
                if L == 0:
                    hg_lb_dve(v, cnt)
                    hg_dve(v, cnt)


def host_layout(i):
    f = {k: np.ascontiguousarray(np.asarray(v)) for k, v in i.items()}
    c = np.ascontiguousarray

    def cols(w):
        n = w.shape[1] // P
        return w.reshape(KC, P, n, P).transpose(2, 1, 0, 3).reshape(n, P, BLK)

    def vec(a):
        return np.moveaxis(a.reshape(a.shape[:-1] + (KC, P)), -1, 0)

    def states(a):
        b = a.reshape((PAIRS, 2, 64) + a.shape[2:])
        return np.moveaxis(b, 0, 2).reshape((P, PAIRS) + a.shape[2:])

    x = np.concatenate([f["x_prompt"].reshape(TP, D), f["x_sample"].reshape(TS, D)])
    glu = cols(f["s5_w_glu"][0])
    win = cols(f["hg_w_in"][0])
    r = {
        "xT": c(x.reshape(T, KC, P).transpose(2, 1, 0)),
        "normw": c(vec(np.stack([f["norm_mix"][0], f["norm_ffn"][0], f["norm_mix"][1], f["norm_ffn"][1],
                                 f["norm_final"]]))),
        "lam_re": c(states(f["s5_lambda_re"][0])),
        "lam_im": c(states(f["s5_lambda_im"][0])),
        "log_dt": c(states(np.repeat(f["s5_log_dt"][0][:, None], 64, axis=1))),
        "s5b": c(np.stack([states(f[n][0]) for n in ("s5_b_re", "s5_b_im")], 1).reshape(P, 2, PAIRS * GH)),
        "s5c": c(np.stack([states(f[n][0].transpose(0, 2, 1)) for n in ("s5_c_re", "s5_c_im")], 1)
                 .reshape(P, 2, PAIRS * GH)),
        "s5d": c(vec(f["s5_d"][0])),
        "s5s0": c(np.stack([states(f[n][0].transpose(1, 2, 0)) for n in ("state_s5_re", "state_s5_im")], 1)
                  .reshape(P, 2 * PAIRS * NB)),
        "keysT": c(np.stack([np.stack([f["peer_keys1"][l].T, f["peer_keys2"][l].T], 1) for l in range(2)], 1)),
        "lbr": c(vec(f["hg_lower_bounds"])),
        "hgnw": c(f["hg_norm_w"][0][:, None]),
        "hgs0": c(f["state_hgrn"][0].transpose(2, 1, 0, 3).reshape(P, HH * NB * P)),
        "glu": c(glu.reshape(2, KC, P, BLK).transpose(1, 0, 2, 3).reshape(16, P, BLK)),
        "win": c(np.concatenate([win[8:16], win[0:8], win[16:24], win[24:32]])),
        "wout": c(cols(f["hg_w_out"][0])),
    }
    for l in range(2):
        r[f"wq{l}"] = c(cols(f["peer_w_q"][l]))
        u = c(f["peer_u"][l].reshape(NK, NK, KC, P).transpose(1, 3, 2, 0).reshape(NK, P, BLK))
        r[f"ua{l}"], r[f"ub{l}"] = u[:UA], u[UA:]
        r[f"v{l}"] = c(f["peer_v"][l].reshape(NK, NK, D).transpose(1, 0, 2))
    return r


OUTS = {"y": (P, KC, T), "s5f": (P, 2 * PAIRS * 9), "hgp": (P, HH * P), "hgs": (P, HH * NB * P)}


def kernel(**inputs):
    import concourse.bacc as bacc
    from concourse.bass_utils import run_bass_kernel_spmd

    nc = bacc.Bacc("TRN2", target_bir_lowering=False, num_devices=1)
    arrays = host_layout(inputs)
    t_in = {k: nc.dram_tensor("in_" + k, a.shape, mybir.dt.from_np(a.dtype), kind="ExternalInput").ap()
            for k, a in arrays.items()}
    t_out = {k: nc.dram_tensor("out_" + k, s, F32, kind="ExternalOutput").ap() for k, s in OUTS.items()}
    build(nc, t_in, t_out)
    r = run_bass_kernel_spmd(nc, [{"in_" + k: a for k, a in arrays.items()}], core_ids=[0]).results[0]
    y = r["out_y"].transpose(2, 1, 0).reshape(T, D)
    s5 = r["out_s5f"].reshape(2, 64, 2, PAIRS, 9).transpose(2, 4, 3, 0, 1).reshape(2, 1, 9, 2 * PAIRS, 64)
    hgp = r["out_hgp"].reshape(P, HH, P).transpose(1, 0, 2).reshape(1, 1, HH, P, P)
    hgs = r["out_hgs"].reshape(P, HH, NB, P).transpose(2, 1, 0, 3).reshape(1, NB, HH, P, P)
    return (y[:TP].reshape(1, TP, D), y[TP:].reshape(NB, LS, D),
            s5[0, :, 0:1], s5[1, :, 0:1], hgp, s5[0, :, 1:], s5[1, :, 1:], hgs)
```
